# Optimizing a Trainium2 kernel written in Bass

```python
import math
import jax, jax.numpy as jnp
from jax import lax
import numpy as np

D_MODEL = 1024
BATCH = 1
SEQ = 256
DEPTH = 2

CHUNK = 64
GDN_HEADS = 4
GDN_DK = 128
GDN_DV = 128
CONV_K = 4
GDN_QK = GDN_HEADS * GDN_DK
GDN_V = GDN_HEADS * GDN_DV
CONV_CH = 2 * GDN_QK + GDN_V
SWA_Q_HEADS = 8
SWA_KV_HEADS = 2
SWA_HEAD_DIM = 64
SWA_Q = SWA_Q_HEADS * SWA_HEAD_DIM
SWA_KV = SWA_KV_HEADS * SWA_HEAD_DIM
WINDOW = 128
WINDOW_CHUNKS = WINDOW // CHUNK
ROT_DIM = SWA_HEAD_DIM // 4
ROPE_THETA = 500000.0
D_FF = 3584
N_EXPERTS = 8
TOP_K = 2
EPS = 1e-6
IN_SPLITS = (GDN_QK, GDN_QK, GDN_V, GDN_V, GDN_HEADS, GDN_HEADS,
             SWA_Q, SWA_KV, SWA_KV, D_MODEL, D_MODEL)
IN_WIDTH = sum(IN_SPLITS)

kernel_name = "hybrid_gdn_swa_moe_block"

def rmsnorm(x, w):
    x32 = x.astype(jnp.float32)
    y = x32 * lax.rsqrt(jnp.mean(x32 * x32, axis=-1, keepdims=True) + EPS)
    return (y * w.astype(jnp.float32)).astype(x.dtype)

def modulate(h, shift, scale):
    return h * (1.0 + scale[:, None, :]) + shift[:, None, :]

def l2norm(x):
    return x * lax.rsqrt(jnp.sum(x * x, axis=-1, keepdims=True) + EPS)

def causal_depthwise_conv(x, w):
    ch = x.shape[-1]
    return lax.conv_general_dilated(
        x, w[:, None, :].astype(x.dtype), window_strides=(1,), padding=[(CONV_K - 1, 0)],
        dimension_numbers=("NWC", "WIO", "NWC"), feature_group_count=ch)

def gated_delta_rule(q, k, v, g, beta):
    b_, seq, nh, dk = q.shape
    dv = v.shape[-1]
    n = seq // CHUNK
    to_c = lambda t: t.reshape(b_, n, CHUNK, nh, -1).transpose(0, 3, 1, 2, 4)
    q, k, v = to_c(q), to_c(k), to_c(v)
    g = g.reshape(b_, n, CHUNK, nh).transpose(0, 3, 1, 2)
    beta = beta.reshape(b_, n, CHUNK, nh).transpose(0, 3, 1, 2)
    g_cum = jnp.cumsum(g, axis=-1)
    idx = jnp.arange(CHUNK)
    incl = idx[:, None] >= idx[None, :]
    strict = idx[:, None] > idx[None, :]
    decay = jnp.exp(jnp.where(incl, g_cum[..., :, None] - g_cum[..., None, :], -jnp.inf))
    k_beta = k * beta[..., None]
    v_beta = v * beta[..., None]
    lmat = jnp.where(strict, jnp.einsum('bhncd,bhnsd->bhncs', k_beta, k) * decay, 0.0)
    eye = jnp.eye(CHUNK, dtype=q.dtype)
    t_mat = lax.linalg.triangular_solve(eye + lmat, jnp.broadcast_to(eye, lmat.shape),
                                        left_side=True, lower=True, unit_diagonal=True)
    u = jnp.einsum('bhncs,bhnse->bhnce', t_mat, v_beta)
    w = jnp.einsum('bhncs,bhnsd->bhncd', t_mat, k_beta * jnp.exp(g_cum)[..., None])
    attn_intra = jnp.where(incl, jnp.einsum('bhncd,bhnsd->bhncs', q, k) * decay, 0.0)
    g_last = g_cum[..., -1]
    k_to_end = k * jnp.exp(g_last[..., None] - g_cum)[..., None]
    q_decay = q * jnp.exp(g_cum)[..., None]
    mv = lambda t: jnp.moveaxis(t, 2, 0)
    xs = (mv(q_decay), mv(k_to_end), mv(u), mv(w), mv(attn_intra), mv(g_last))

    def step(state, inp):
        qd, kd, u_c, w_c, a_c, gl = inp
        v_new = u_c - jnp.einsum('bhcd,bhde->bhce', w_c, state)
        o = jnp.einsum('bhcd,bhde->bhce', qd, state) + jnp.einsum('bhcs,bhse->bhce', a_c, v_new)
        state = state * jnp.exp(gl)[..., None, None] + jnp.einsum('bhcd,bhce->bhde', kd, v_new)
        return state, o

    s0 = jnp.zeros((b_, nh, dk, dv), q.dtype)
    _, o = lax.scan(step, s0, xs)
    return o.transpose(1, 0, 3, 2, 4).reshape(b_, seq, nh, dv)

def partial_rope(x, positions):
    half = ROT_DIM // 2
    inv_freq = ROPE_THETA ** (-jnp.arange(0, ROT_DIM, 2, dtype=jnp.float32) / ROT_DIM)
    ang = positions.astype(jnp.float32)[..., None] * inv_freq
    cos = jnp.cos(ang)[:, :, None, :]
    sin = jnp.sin(ang)[:, :, None, :]
    xr = x[..., :ROT_DIM].astype(jnp.float32)
    x1, x2 = xr[..., :half], xr[..., half:]
    rot = jnp.concatenate([x1 * cos - x2 * sin, x2 * cos + x1 * sin], axis=-1)
    return jnp.concatenate([rot.astype(x.dtype), x[..., ROT_DIM:]], axis=-1)

def kv_band(t):
    b_, seq, hk, dh = t.shape
    n = seq // CHUNK
    tp = jnp.pad(t, ((0, 0), ((WINDOW_CHUNKS - 1) * CHUNK, 0), (0, 0), (0, 0)))
    parts = [tp[:, wi * CHUNK: wi * CHUNK + seq].reshape(b_, n, CHUNK, hk, dh)
             for wi in range(WINDOW_CHUNKS)]
    return jnp.concatenate(parts, axis=2)

def sliding_window_sink_attention(q, k, v, sinks):
    b_, seq, hq, dh = q.shape
    n = seq // CHUNK
    grp = SWA_Q_HEADS // SWA_KV_HEADS
    span = WINDOW_CHUNKS * CHUNK
    qc = q.reshape(b_, n, CHUNK, SWA_KV_HEADS, grp, dh)
    kb, vb = kv_band(k), kv_band(v)
    s = jnp.einsum('bnqhgd,bnkhd->bhgnqk', qc, kb).astype(jnp.float32) * (dh ** -0.5)
    kchunk = jnp.arange(n)[:, None] - (WINDOW_CHUNKS - 1) + jnp.arange(span)[None, :] // CHUNK
    s = jnp.where((kchunk >= 0)[:, None, :], s, -jnp.inf)
    sink = sinks.astype(jnp.float32).reshape(SWA_KV_HEADS, grp)[None, :, :, None, None]
    m = jnp.maximum(jnp.max(s, axis=-1), sink)
    p = jnp.exp(s - m[..., None])
    denom = jnp.sum(p, axis=-1) + jnp.exp(sink - m)
    p = (p / denom[..., None]).astype(v.dtype)
    o = jnp.einsum('bhgnqk,bnkhd->bnqhgd', p, vb)
    return o.reshape(b_, seq, hq, dh)

def token_mixer(h, positions, w_in, conv_w, a_log, dt_bias, gdn_norm_w, sinks,
                w_a_out, w_b_out, w_mix_out):
    b_, seq, _ = h.shape
    f32 = jnp.float32
    split_at = np.cumsum(IN_SPLITS)[:-1].tolist()
    (q_a, k_a, v_a, z_a, b_a, a_a, q_b, k_b, v_b, g_a, g_b) = jnp.split(h @ w_in, split_at, axis=-1)
    qkv = jax.nn.silu(causal_depthwise_conv(jnp.concatenate([q_a, k_a, v_a], axis=-1), conv_w))
    q_a, k_a, v_a = jnp.split(qkv, [GDN_QK, 2 * GDN_QK], axis=-1)
    q_a = l2norm(q_a.reshape(b_, seq, GDN_HEADS, GDN_DK).astype(f32)) * (GDN_DK ** -0.5)
    k_a = l2norm(k_a.reshape(b_, seq, GDN_HEADS, GDN_DK).astype(f32))
    v_a = v_a.reshape(b_, seq, GDN_HEADS, GDN_DV).astype(f32)
    beta = jax.nn.sigmoid(b_a.astype(f32))
    g = -jnp.exp(a_log.astype(f32)) * jax.nn.softplus(a_a.astype(f32) + dt_bias.astype(f32))
    o_a = gated_delta_rule(q_a, k_a, v_a, g, beta)
    o_a = rmsnorm(o_a, gdn_norm_w) * jax.nn.silu(z_a.reshape(b_, seq, GDN_HEADS, GDN_DV).astype(f32))
    o_a = o_a.reshape(b_, seq, GDN_V).astype(h.dtype)
    q_b = partial_rope(q_b.reshape(b_, seq, SWA_Q_HEADS, SWA_HEAD_DIM), positions)
    k_b = partial_rope(k_b.reshape(b_, seq, SWA_KV_HEADS, SWA_HEAD_DIM), positions)
    v_b = v_b.reshape(b_, seq, SWA_KV_HEADS, SWA_HEAD_DIM)
    o_b = sliding_window_sink_attention(q_b, k_b, v_b, sinks).reshape(b_, seq, SWA_Q)
    y = jax.nn.sigmoid(g_a) * (o_a @ w_a_out) + jax.nn.sigmoid(g_b) * (o_b @ w_b_out)
    return y @ w_mix_out

def swiglu(h, w_gate, w_up, w_down):
    return (jax.nn.silu(h @ w_gate) * (h @ w_up)) @ w_down

def moe_swiglu(h, router_w, router_b, w_gate, w_up, w_down):
    logits = (h @ router_w).astype(jnp.float32) + router_b.astype(jnp.float32)
    top_v, top_i = lax.top_k(logits, TOP_K)
    wts = jax.nn.softmax(top_v, axis=-1)
    combine = jnp.sum(jax.nn.one_hot(top_i, N_EXPERTS, dtype=jnp.float32) * wts[..., None], axis=-2)
    combine = combine.astype(h.dtype)
    out = jnp.zeros_like(h)
    for e in range(N_EXPERTS):
        out = out + combine[..., e:e + 1] * swiglu(h, w_gate[e], w_up[e], w_down[e])
    return out

def setup_inputs(seed: int = 0) -> dict:
    key = jax.random.key(seed)
    ks = iter(jax.random.split(key, 40))
    f32 = jnp.float32
    normal = lambda shape: jax.random.normal(next(ks), shape, f32)
    nrm = lambda shape, fan_in: normal(shape) * (fan_in ** -0.5)
    n_dense = (DEPTH + 1) // 2
    n_moe = DEPTH // 2
    x = normal((BATCH, SEQ, D_MODEL))
    c = normal((BATCH, D_MODEL))
    positions = (jax.random.randint(next(ks), (BATCH, 1), 0, 4096, dtype=jnp.int32)
                 + jnp.arange(SEQ, dtype=jnp.int32)[None, :])
    ada_w = nrm((DEPTH, D_MODEL, 6 * D_MODEL), D_MODEL)
    ada_b = 0.02 * normal((DEPTH, 6 * D_MODEL))
    norm_mix_w = 1.0 + 0.05 * normal((DEPTH, D_MODEL))
    norm_ffn_w = 1.0 + 0.05 * normal((DEPTH, D_MODEL))
    w_in = nrm((DEPTH, D_MODEL, IN_WIDTH), D_MODEL)
    conv_w = nrm((DEPTH, CONV_K, CONV_CH), CONV_K)
    a_log = jnp.log(jax.random.uniform(next(ks), (DEPTH, GDN_HEADS), f32, 1.0, 16.0))
    dt = jnp.exp(jax.random.uniform(next(ks), (DEPTH, GDN_HEADS), f32, math.log(1e-3), math.log(1e-1)))
    dt_bias = dt + jnp.log(-jnp.expm1(-dt))
    gdn_norm_w = 1.0 + 0.05 * normal((DEPTH, GDN_DV))
    sinks = 0.5 * normal((DEPTH, SWA_Q_HEADS))
    w_a_out = nrm((DEPTH, GDN_V, D_MODEL), GDN_V)
    w_b_out = nrm((DEPTH, SWA_Q, D_MODEL), SWA_Q)
    w_mix_out = nrm((DEPTH, D_MODEL, D_MODEL), D_MODEL)
    ffn_w_gate = nrm((n_dense, D_MODEL, D_FF), D_MODEL)
    ffn_w_up = nrm((n_dense, D_MODEL, D_FF), D_MODEL)
    ffn_w_down = nrm((n_dense, D_FF, D_MODEL), D_FF)
    router_w = nrm((n_moe, D_MODEL, N_EXPERTS), D_MODEL)
    router_b = 0.01 * normal((n_moe, N_EXPERTS))
    moe_w_gate = nrm((n_moe, N_EXPERTS, D_MODEL, D_FF), D_MODEL)
    moe_w_up = nrm((n_moe, N_EXPERTS, D_MODEL, D_FF), D_MODEL)
    moe_w_down = nrm((n_moe, N_EXPERTS, D_FF, D_MODEL), D_FF)
    final_norm_w = 1.0 + 0.05 * normal((D_MODEL,))
    return {"x": x, "c": c, "positions": positions, "ada_w": ada_w, "ada_b": ada_b,
            "norm_mix_w": norm_mix_w, "norm_ffn_w": norm_ffn_w, "w_in": w_in, "conv_w": conv_w,
            "a_log": a_log, "dt_bias": dt_bias, "gdn_norm_w": gdn_norm_w, "sinks": sinks,
            "w_a_out": w_a_out, "w_b_out": w_b_out, "w_mix_out": w_mix_out,
            "ffn_w_gate": ffn_w_gate, "ffn_w_up": ffn_w_up, "ffn_w_down": ffn_w_down,
            "router_w": router_w, "router_b": router_b, "moe_w_gate": moe_w_gate,
            "moe_w_up": moe_w_up, "moe_w_down": moe_w_down, "final_norm_w": final_norm_w}

def reference(x, c, positions, ada_w, ada_b, norm_mix_w, norm_ffn_w, w_in, conv_w, a_log,
              dt_bias, gdn_norm_w, sinks, w_a_out, w_b_out, w_mix_out, ffn_w_gate, ffn_w_up,
              ffn_w_down, router_w, router_b, moe_w_gate, moe_w_up, moe_w_down, final_norm_w):
    c_act = jax.nn.silu(c)
    for layer in range(DEPTH):
        ada = c_act @ ada_w[layer] + ada_b[layer]
        sh1, sc1, gt1, sh2, sc2, gt2 = jnp.split(ada, 6, axis=-1)
        h = modulate(rmsnorm(x, norm_mix_w[layer]), sh1, sc1)
        x = x + gt1[:, None, :] * token_mixer(
            h, positions, w_in[layer], conv_w[layer], a_log[layer], dt_bias[layer],
            gdn_norm_w[layer], sinks[layer], w_a_out[layer], w_b_out[layer], w_mix_out[layer])
        h = modulate(rmsnorm(x, norm_ffn_w[layer]), sh2, sc2)
        j = layer // 2
        if layer % 2 == 0:
            f = swiglu(h, ffn_w_gate[j], ffn_w_up[j], ffn_w_down[j])
        else:
            f = moe_swiglu(h, router_w[j], router_b[j], moe_w_gate[j], moe_w_up[j], moe_w_down[j])
        x = x + gt2[:, None, :] * f
    return rmsnorm(x, final_norm_w)


_drawn_inputs = setup_inputs


def setup_inputs(seed=0):
    import zlib

    import numpy as np

    out = dict(_drawn_inputs(seed))
    spreads = {}
    factors = {'sinks': 8.0, 'router_b': 4.231}
    for name, (base, spread) in spreads.items():
        noise = np.random.default_rng([zlib.crc32(name.encode()), seed]).standard_normal(out[name].shape)
        drawn = base * np.exp(spread * noise) if base else spread * noise
        out[name] = __import__('jax').numpy.asarray(drawn.astype(out[name].dtype))
    for name, factor in factors.items():
        out[name] = (out[name] * factor).astype(out[name].dtype)
    return out
```

```python
import math
from contextlib import ExitStack

import numpy as np

import concourse.bass as bass
from concourse import mybir

F32 = mybir.dt.float32
F32R = mybir.dt.float32r
BF16 = mybir.dt.bfloat16
I32 = mybir.dt.int32
ALU = mybir.AluOpType
ACT = mybir.ActivationFunctionType
AX = mybir.AxisListType

P = 128
EPS = 1e-6
NEG = -1e30
CHUNK = 64
ROPE_THETA = 500000.0


def build_program(nc, x, c, positions, ada_w, ada_b, norm_mix_w, norm_ffn_w, w_in, conv_w, a_log,
                  dt_bias, gdn_norm_w, sinks, w_a_out, w_b_out, w_mix_out, ffn_w_gate, ffn_w_up,
                  ffn_w_down, router_w, router_b, moe_w_gate, moe_w_up, moe_w_down, final_norm_w, out):
    D = x.shape[2]
    T = x.shape[1]
    L = ada_w.shape[0]
    KO = D // P
    TB = T // P
    NCH = T // CHUNK
    H = a_log.shape[1]
    DK = P
    NQH = sinks.shape[1]
    DH = CHUNK
    G = 2
    J = NQH // G
    F = ffn_w_gate.shape[2]
    E = moe_w_gate.shape[1]
    FC = F // 512
    ROT = DH // 4
    HALF = ROT // 2
    C_SWA = 4 * H * DK + 2 * H
    C_GATE = C_SWA + NQH * DH + 2 * G * DH
    C_BA = 4 * H * DK
    CTAPS = conv_w.shape[1]
    assert (D, T, L, H, NQH, E) == (1024, 256, 2, 4, 8, 8) and F % 512 == 0
    PAD = CTAPS - 1
    RAWW = T + PAD

    RING = 6
    UW = 2048
    units = []
    for q in range(12):
        for kh in range(2):
            units.append((("ada", 0, q, kh), False))

    def mixer_units(l):
        for j in range(8):
            units.append((("qkvz", l, j), True))
        for kh in range(2):
            units.append((("swq", l, kh), True))
        units.append((("swkv", l), True))
        for j in range(8):
            units.append((("gate", l, j), True))
        for cc in range(2):
            units.append((("wa", l, cc), True))
        for cc in range(2):
            units.append((("wb", l, cc), True))
        for cc in range(2):
            for kh in range(2):
                units.append((("mix", l, cc, kh), True))

    mixer_units(0)
    ada1 = [("ada", 1, q, kh) for q in range(12) for kh in range(2)]
    for i in range(2 * FC):
        units.append((("fg", i), True))
        units.append((("fu", i), True))
        if i > 0:
            units.append((("fd", i - 1), True))
        for _ in range(2):
            if ada1:
                units.append((ada1.pop(0), False))
    units.append((("fd", 2 * FC - 1), True))
    mixer_units(1)
    u_of = {k: n for n, (k, _) in enumerate(units)}
    split_keys = [k for k, pe_ in units if pe_]
    s_of = {k: n for n, k in enumerate(split_keys)}
    U0, S0 = len(units), len(split_keys)
    MU = 6 * FC
    NS_PRE, NS_MOE = 2, 3
    assert not ada1 and U0 % RING == 0 and MU % RING == 0 and S0 % NS_MOE == 0 and MU % NS_MOE == 0
    moe_units = []
    for fc in range(FC):
        moe_units += [("g", fc, 0), ("g", fc, 1), ("u", fc, 0), ("u", fc, 1)]
        if fc > 0:
            moe_units += [("d", fc - 1, 0), ("d", fc - 1, 1)]
    moe_units += [("d", FC - 1, 0), ("d", FC - 1, 1)]
    mp = {k: n for n, k in enumerate(moe_units)}
    assert len(moe_units) == MU
    turned_after = {(mp[("d", f - 1, 0)] if f else mp[("g", 1, 0)]): f for f in range(FC)}

    def k_rows(ap):
        return ap.rearrange("(k p) n -> p k n", p=P)

    def unit_dram(key):
        kind, l = key[0], key[1]
        if kind == "ada":
            q, kh = key[2:]
            return k_rows(ada_w[l, kh * 512:(kh + 1) * 512, q * 512:(q + 1) * 512]), 4
        if kind == "qkvz":
            return k_rows(w_in[l, :, key[2] * 256:(key[2] + 1) * 256]), 8
        if kind == "swq":
            return k_rows(w_in[l, key[2] * 512:(key[2] + 1) * 512, C_SWA:C_SWA + 512]), 4
        if kind == "swkv":
            return k_rows(w_in[l, :, C_SWA + 512:C_SWA + 768]), 8
        if kind == "gate":
            return k_rows(w_in[l, :, C_GATE + key[2] * 256:C_GATE + (key[2] + 1) * 256]), 8
        if kind == "wa":
            return k_rows(w_a_out[l, :, key[2] * 512:(key[2] + 1) * 512]), 4
        if kind == "mix":
            cc, kh = key[2:]
            return k_rows(w_mix_out[l, kh * 512:(kh + 1) * 512, cc * 512:(cc + 1) * 512]), 4
        if kind in ("fg", "fu"):
            w = ffn_w_gate if kind == "fg" else ffn_w_up
            return k_rows(w[0, :, l * 256:(l + 1) * 256]), 8
        assert kind == "fd"
        return k_rows(ffn_w_down[0, l * 256:(l + 1) * 256, :]), 2

    ctx = ExitStack()
    with ctx:
        def sb(name, shape, dt=F32, where=ctx):
            return where.enter_context(nc.sbuf_tensor(name, shape, dt))

        def sem(name):
            return ctx.enter_context(nc.semaphore(name))

        ps = [ctx.enter_context(nc.psum_tensor(f"bank{b}", [P, 512], F32)) for b in range(8)]

        ring = sb("ring", [P, RING, UW])
        w_hi = [sb(f"w_hi{i}", [P, UW], F32R) for i in range(NS_PRE)]
        w_lo = [sb(f"w_lo{i}", [P, UW], F32R) for i in range(NS_PRE)]
        xs = sb("xs", [P, TB, D])
        hT_hi = sb("hT_hi", [P, KO, T], F32R)
        hT_lo = sb("hT_lo", [P, KO, T], F32R)
        ident = sb("ident", [P, P])
        ones = sb("ones", [P, P])
        incl_blk = sb("incl_blk", [P, P])
        after_blk = sb("after_blk", [P, P])
        before_blk = sb("before_blk", [P, P])
        lev_mask = sb("lev_mask", [P, 7, P], BF16)
        am0 = sb("am0", [P, P], BF16)
        am1 = sb("am1", [P, 2 * P], BF16)
        cols = sb("cols", [P, 2 * P])
        c_silu = sb("c_silu", [P, KO])
        adac = sb("adac", [P, L, 48])
        wsc = sb("wsc", [P, KO])
        eps_c = sb("eps_c", [P, 1])
        one_c = sb("one_c", [P, 1])
        ba_hi = sb("ba_hi", [P, L, KO, 8], F32R)
        ba_lo = sb("ba_lo", [P, L, KO, 8], F32R)
        rw_hi = sb("rw_hi", [P, KO, E], F32R)
        rw_lo = sb("rw_lo", [P, KO, E], F32R)
        head_rows = sb("head_rows", [P, 3 * L * H])
        sink_rows = sb("sink_rows", [P, L, NQH])
        rb_row = sb("rb_row", [P, E])
        rope = sb("rope", [P, TB, 2, HALF])
        stat = sb("stat", [P, 16])
        ba = sb("ba", [P, TB, 8])
        gb = sb("gb", [P, 6, TB, H])
        egl = sb("egl", [P, H, NCH])
        smax = sb("smax", [P, 4, NQH])
        lev_f = sb("lev_f", [P, P])
        meta = sb("meta", [P, 4], I32)

        gm = ExitStack()
        oa_hi = sb("oa_hi", [P, H, T], F32R, gm)
        oa_lo = sb("oa_lo", [P, H, T], F32R, gm)
        ob_hi = sb("ob_hi", [P, J, T], F32R, gm)
        ob_lo = sb("ob_lo", [P, J, T], F32R, gm)
        work = sb("work", [P, 17152], F32, gm)
        gm.close()

        def wk(at, *shape):
            n = int(np.prod(shape))
            v = work[:, at:at + n]
            if len(shape) == 2:
                return v.rearrange("p (a b) -> p a b", a=shape[0])
            if len(shape) == 3:
                return v.rearrange("p (a b c) -> p a b c", a=shape[0], b=shape[1])
            return v

        m_xn = wk(0, TB, D)
        m_tmp = wk(4096, KO, T)
        m_acc = wk(8192, 12, 512)
        prm_a = wk(14400, P)
        prm_b = wk(14528, P)
        ba_raw = wk(14656, L * KO * 8)
        rw_raw = wk(14784, KO * E)
        pos_i = wk(14848, 2 * TB)[:, 0:TB].bitcast(I32)
        ang = wk(14860, 6, TB * 2 * HALF)
        invf = wk(15060, 2 * HALF)
        qkv = wk(0, 16, T)
        qT, kT, vT, zT = (qkv[:, 4 * i:4 * i + 4, :] for i in range(4))
        raw = [wk(4096 + i * 2 * RAWW, 2, RAWW) for i in range(2)]
        cv = [wk(5200 + i * 512, 2, T) for i in range(2)]
        sq = [wk(6256 + i * 512, 512) for i in range(2)]
        gate_sb = wk(4096, 16, T)
        a_s = wk(4096, NQH, 2 * P)
        a_pt = wk(6144, 16, P)
        a_qk = wk(8192, TB, 10, DH)
        a_v = wk(9472, TB, P)
        a_qT = wk(9728, J, T)
        a_kT = wk(10752, T)
        a_rt = wk(14080, 4, TB * 10 * HALF)
        rinv = wk(15104, 8, T)
        KB = wk(11008, H, T)
        EG = wk(12032, H, T)
        ED = wk(13056, H, T)
        g_rows = [wk(14080, TB, 512), wk(15104, TB, 512), wk(16128, TB, 512)]
        LT = wk(14080, TB * H, P)
        AT = wk(15104, TB * H, P)
        U = wk(16128, TB * H, P)
        X = wk(8192, TB * H, P)
        XT = wk(9216, TB * H, P)
        v_tok = wk(12032, TB, H, P)
        k_tok = wk(13056, TB, H, P)
        state = wk(14080, H, P)
        resid = wk(14592, H, P)
        v_new = wk(16128, H, P)
        OT = wk(8192, H, T)
        o_sq = wk(11008, H, T)
        o_r = wk(9216, H, T)
        y_sum = wk(0, KO, T)
        y_tmp = wk(11008, 4, T)
        m_gt = wk(2048, D)
        m_dg = wk(3072, KO, P)
        m_xt = wk(13056, 2, 512)

        gf = ExitStack()
        f_xn = sb("f_xn", [P, TB, D], F32, gf)
        f_tmp = sb("f_tmp", [P, KO, T], F32, gf)
        f_hi = [sb(f"f_hi{i}", [P, 2, T], F32R, gf) for i in range(2)]
        f_lo = [sb(f"f_lo{i}", [P, 2, T], F32R, gf) for i in range(2)]
        f_g = [sb(f"f_g{i}", [P, 2, T], F32, gf) for i in range(2)]
        f_h = sb("f_h", [P, 2, T], F32, gf)
        f_acc = sb("f_acc", [P, 12, 512], F32, gf)
        f_gt = sb("f_gt", [P, D], F32, gf)
        f_dg = sb("f_dg", [P, KO, P], F32, gf)
        gf.close()

        ge = ExitStack()
        w_hi.append(sb("w_hi2", [P, UW], F32R, ge))
        w_lo.append(sb("w_lo2", [P, UW], F32R, ge))
        e_xn = sb("e_xn", [P, TB, D], F32, ge)
        e_tmp = sb("e_tmp", [P, KO, T], F32, ge)
        e_acc = sb("e_acc", [P, TB, D], F32, ge)
        e_xf = sb("e_xf", [P, KO, P], F32, ge)
        xg_hi = sb("xg_hi", [P, KO, P], F32R, ge)
        xg_lo = sb("xg_lo", [P, KO, P], F32R, ge)
        e_g = [sb(f"e_g{i}", [P, 512], F32, ge) for i in range(2)]
        e_h = [sb(f"e_h{i}", [P, 512], F32, ge) for i in range(2)]
        h_hi = [sb(f"h_hi{i}", [P, 4, P], F32R, ge) for i in range(2)]
        h_lo = [sb(f"h_lo{i}", [P, 4, P], F32R, ge) for i in range(2)]
        e_y = sb("e_y", [P, D], F32, ge)
        e_p = sb("e_p", [P, TB, P], F32, ge)
        e_pw = sb("e_pw", [P, TB, P], F32, ge)
        e_pwT = sb("e_pwT", [P, T], F32, ge)
        e_gt = sb("e_gt", [P, D], F32, ge)
        e_dg = sb("e_dg", [P, KO, P], F32, ge)
        fw_row = sb("fw_row", [P, D], F32, ge)
        upper = sb("upper", [P, P], F32, ge)
        slots = sb("slots", [P, P], F32, ge)
        lg = sb("lg", [P, 12, TB, E], F32, ge)
        rsm = sb("rsm", [P, 24, E], F32, ge)
        slot_of = sb("slot_of", [P, TB, E + 4], F32, ge)
        wt_of = sb("wt_of", [P, TB, E + 4], F32, ge)
        cur = sb("cur", [P, 4, TB], F32, ge)
        metaf = sb("metaf", [P, 4], F32, ge)
        ge.close()

        landed = [sem(f"landed{i}") for i in range(RING)]
        taken = sem("taken")
        hi_ready = sem("hi_ready")
        split_used = sem("split_used")
        x_in = sem("x_in")
        setup_in = sem("setup_in")
        setup_b = sem("setup_b")
        zeroed = sem("zeroed")
        consts = sem("consts")
        pool_c = sem("pool_chain")
        dve_c = sem("dve_chain")
        act_c = sem("act_chain")
        prm_t = sem("params_turned")
        cols_s = sem("cols_ready")
        csil = sem("c_silu_ready")
        small_hi = sem("small_hi")
        small_lo = sem("small_lo")
        rope_pre = sem("rope_angles")
        rope_s = sem("rope_ready")
        ada_ps = sem("ada_cols_in_psum")
        ada_s = sem("ada_cols_ready")
        ssq = sem("square_sums")
        rstd_s = sem("rstd_ready")
        xn_s = sem("xn_ready")
        xnT = sem("xn_turned")
        hmod = sem("h_modulated")
        h_hi_s = sem("h_hi_ready")
        h_s = sem("h_ready")
        ba_ps = sem("ba_in_psum")
        ba_s = sem("ba_copied")
        raw_s = sem("raw_ready")
        conv_s = sem("conv_done")
        qkv_s = sem("qkvz_ready")
        sq_s = sem("qk_squares")
        l2_ps = sem("l2_in_psum")
        rinv_s = sem("rinv_ready")
        qkn_s = sem("qk_normed")
        beta_e = sem("beta_exp")
        beta_a = sem("beta_args")
        gsteps = sem("g_steps")
        grow_s = sem("g_rows_ready")
        maps = sem("maps_in_psum")
        kb_s = sem("kbeta_ready")
        exps_s = sem("exp_maps_ready")
        dt_s = sem("decay_ready")
        dtm_s = sem("decay_masked")
        lat = sem("la_in_psum")
        lat_s = sem("la_ready")
        kgb_s = sem("scaled_qk_ready")
        tok_ps = sem("tok_turned")
        tok_s = sem("tok_ready")
        l0_ps = sem("l_turned")
        inv0 = sem("inverse_started")
        u_ps = sem("u_in_psum")
        u_s = sem("u_ready")
        xu_ps = sem("xu_in_psum")
        xx_s = sem("x_updated")
        ks_ps = sem("ks_in_psum")
        res_s = sem("resid_ready")
        vn_ps = sem("vnew_in_psum")
        vn_s = sem("vnew_ready")
        su_ps = sem("state_update_in_psum")
        st_s = sem("state_ready")
        o_ps = sem("o_in_psum")
        o_s = sem("o_copied")
        osq_s = sem("o_squares")
        on_ps = sem("o_norm_in_psum")
        on_s = sem("o_rinv_ready")
        oaf = sem("oa_ready_f32")
        oa_h = sem("oa_hi_ready")
        oa_s = sem("oa_ready")
        sw_s = sem("swa_copied")
        rot_s = sem("rotated")
        att_ps = sem("attention_in_psum")
        att_a = sem("attention_act_read")
        att_d = sem("attention_dve_read")
        mx_s = sem("row_max_ready")
        pe_s = sem("exp_scores_ready")
        pn_s = sem("probs_ready")
        gate_s = sem("gates_ready")
        obh_s = sem("ob_hi_ready")
        ln_s = sem("qk_logs")
        ln2_s = sem("o_logs")
        xf_s = sem("channel_mixer_added")
        out_s = sem("out_ready")
        upper_s = sem("expert_memory_cleared")
        cur_s = sem("current_slots")
        yb_s = sem("branch_read")
        y_hi_s = sem("y_hi_ready")
        y_s = sem("y_ready")
        gtd_s = sem("gate_diag_ready")
        gt_ps = sem("gate_row_in_psum")
        gt_s = sem("gate_row_ready")
        mix_s = sem("mix_added")
        fs_s = sem("ffn_silu")
        fh_s = sem("ffn_hidden")
        fhh_s = sem("ffn_hidden_hi")
        fhl_s = sem("ffn_hidden_lo")
        logit_ps = sem("logits_in_psum")
        lg_s = sem("logits_ready")
        lge_s = sem("logit_exp")
        sel_s = sem("selection_ready")
        pos_ps = sem("positions_in_psum")
        route_s = sem("routing_ready")
        p_s = sem("perm_ready")
        ga_ps = sem("gather_in_psum")
        ga_s = sem("gather_read")
        xgh_s = sem("xg_hi_ready")
        xg_s = sem("xg_ready")
        pw_s = sem("weighted_perm_ready")
        pwt_ps = sem("weighted_perm_turned")
        pwt_s = sem("weighted_perm_T_ready")
        ms_s = sem("expert_silu")
        mh_s = sem("expert_hidden")
        mt_ps = sem("expert_hidden_turned")
        mhh_s = sem("expert_hidden_hi")
        mhl_s = sem("expert_hidden_lo")
        y_c = sem("expert_out_copied")
        cb_ps = sem("combine_in_psum")
        cb_s = sem("combined")
        fin_s = sem("final_rows_ready")
        stored = sem("stored")

        SETUP_IN = 16 * (2 * L + 4)
        SETUP_B = 16 * (7 + TB)
        landed_at, level = [], [0] * RING
        for u, (key, _) in enumerate(units):
            level[u % RING] += 16 * (G if key[0] == "wb" else 1)
            landed_at.append(level[u % RING])
        COL_NM, COL_NF, COL_CONV = 0, L * KO, 2 * L * KO
        COL_AB, COL_C, COL_GN = P, P + L * 48, P + L * 48 + KO

        att_reader = ["a"] * 3 + ["d"] * 2 + ["a"] * 2 + ["d"] * 2 + ["d"] * 4 + ["a"] * 4 + ["d"] * 2
        T_SCORE, T_TURN, T_PV = (3, 9), (5, 13), (7, 17)
        NTASK = len(att_reader)
        NATT_A = att_reader.count("a")
        NATT_D = att_reader.count("d")

        def att_freed(eng, l, t):
            r = att_reader[t]
            n = att_reader[:t + 1].count(r) + l * (NATT_A if r == "a" else NATT_D)
            eng.wait_ge(att_a if r == "a" else att_d, n)

        block = ctx.enter_context(nc.Block())

        @block.sync
        def _(sp):
            sp.dma_start(xs[:], x[0].rearrange("(b p) d -> p b d", p=P)).then_inc(x_in, 16)
            for l in range(L):
                sp.dma_start(prm_a[COL_NM + l * KO:COL_NM + (l + 1) * KO, :],
                             norm_mix_w[l].rearrange("(r n) -> r n", n=P)).then_inc(setup_in, 16)
                sp.dma_start(prm_a[COL_NF + l * KO:COL_NF + (l + 1) * KO, :],
                             norm_ffn_w[l].rearrange("(r n) -> r n", n=P)).then_inc(setup_in, 16)
            sp.dma_start(prm_a[COL_CONV:P, :],
                         conv_w.rearrange("l j (t n) -> (l j t) n", n=P)).then_inc(setup_in, 16)
            sp.wait_ge(zeroed, 1)
            sp.dma_start(prm_b[0:L * 48, :],
                         ada_b.rearrange("l (t n) -> (l t) n", n=P)).then_inc(setup_in, 16)
            sp.dma_start(prm_b[L * 48:L * 48 + KO, :],
                         c[0].rearrange("(r n) -> r n", n=P)).then_inc(setup_in, 16)
            sp.dma_start(prm_b[L * 48 + KO:L * 48 + KO + L, :], gdn_norm_w).then_inc(setup_in, 16)

            def load(u):
                key = units[u][0]
                if u >= RING:
                    sp.wait_ge(taken, u - RING + 1)
                if key[0] == "wb":
                    dst = ring[:, u % RING, :].rearrange("p (k n) -> p k n", k=4)
                    for g in range(G):
                        src = w_b_out[key[1], g * J * DH:(g + 1) * J * DH,
                                      key[2] * 512:(key[2] + 1) * 512]
                        ins = sp.dma_start(dst[g * DH:(g + 1) * DH],
                                           src.rearrange("(j d) n -> d j n", d=DH))
                        ins.then_inc(landed[u % RING], 16)
                else:
                    src, k = unit_dram(key)
                    dst = ring[:, u % RING, :].rearrange("p (k n) -> p k n", k=k)
                    sp.dma_start(dst, src).then_inc(landed[u % RING], 16)

            for u in range(RING):
                load(u)
            for tb in range(TB):
                sp.dma_start(pos_i[:, tb:tb + 1],
                             positions[0, tb * P:(tb + 1) * P].unsqueeze(1)).then_inc(setup_b, 16)
            sp.dma_start(head_rows[:, 0:L * H],
                         a_log.rearrange("l h -> (l h)").partition_broadcast(P)).then_inc(setup_b, 16)
            sp.dma_start(head_rows[:, L * H:2 * L * H],
                         dt_bias.rearrange("l h -> (l h)").partition_broadcast(P)).then_inc(setup_b, 16)
            sp.dma_start(sink_rows[:].rearrange("p l h -> p (l h)"),
                         sinks.rearrange("l h -> (l h)").partition_broadcast(P)).then_inc(setup_b, 16)
            sp.dma_start(ba_raw.rearrange("p (l k n) -> p l k n", l=L, k=KO)[:, 0],
                         k_rows(w_in[0, :, C_BA:C_BA + 8])).then_inc(setup_b, 16)
            sp.dma_start(ba_raw.rearrange("p (l k n) -> p l k n", l=L, k=KO)[:, 1],
                         k_rows(w_in[1, :, C_BA:C_BA + 8])).then_inc(setup_b, 16)
            sp.dma_start(rw_raw.rearrange("p (k n) -> p k n", k=KO),
                         k_rows(router_w[0])).then_inc(setup_b, 16)
            sp.dma_start(rb_row[:], router_b[0].partition_broadcast(P)).then_inc(setup_b, 16)
            for u in range(RING, U0):
                load(u)

            def expert_loads(item, e):
                for n, (kind, fc, half) in enumerate(moe_units):
                    sp.wait_ge(taken, U0 + n - RING + 1 + item * MU)
                    slot = n % RING
                    if kind == "d":
                        src = moe_w_down[0, e, fc * 512 + half * 256:fc * 512 + (half + 1) * 256, :]
                        k = 2
                    else:
                        w = moe_w_gate if kind == "g" else moe_w_up
                        src = w[0, e, half * 512:(half + 1) * 512, fc * 512:(fc + 1) * 512]
                        k = 4
                    sp.dma_start(ring[:, slot, :].rearrange("p (k n) -> p k n", k=k),
                                 k_rows(src)).then_inc(landed[slot], 16)

            with sp.Fori(0, E) as e:
                expert_loads(e, e)
            sp.wait_ge(route_s, 1)
            n_items = sp.value_load(meta[0:1, 0:1], min_val=E, max_val=E + 3)
            with sp.If(n_items > E):
                with sp.Fori(E, n_items) as item:
                    e = sp.value_load(meta[0:1, bass.ds(item - (E - 1), 1)], min_val=0, max_val=E - 1)
                    expert_loads(item, e)
            sp.dma_start(fw_row[:], final_norm_w.partition_broadcast(P)).then_inc(fin_s, 16)
            sp.wait_ge(out_s, 1)
            sp.dma_start(out[0].rearrange("(b p) d -> p b d", p=P), e_acc[:]).then_inc(stored, 16)
            sp.wait_ge(stored, 16)

        @block.gpsimd
        def _(pool):
            n_chain = [0]

            def link(ins):
                n_chain[0] += 1
                ins.then_inc(pool_c, 1)
                pool.wait_ge(pool_c, n_chain[0])

            def keep(view, pattern, base, mult, op=ALU.is_ge, fill=0.0):
                link(pool.affine_select(out=view, in_=view, compare_op=op, fill=fill, base=base,
                                        pattern=pattern, channel_multiplier=mult))

            pool.memset(prm_b, 0.0).then_inc(zeroed, 1)
            pool.memset(eps_c[:], EPS)
            pool.memset(one_c[:], 1.0)
            link(pool.memset(ones[:], 1.0))
            link(pool.memset(ident[:], 0.0))
            pool.affine_select(out=ident[:], in_=ident[:], compare_op=ALU.not_equal, fill=1.0, base=0,
                               pattern=[[-1, P]], channel_multiplier=1).then_inc(consts, 1)
            for i in range(HALF):
                for k in range(2):
                    link(pool.memset(invf[:, k * HALF + i:k * HALF + i + 1],
                                     float(np.float32(ROPE_THETA) ** np.float32(-2.0 * i / ROT))))
            pool.tensor_copy(one_c[:], ones[:, 0:1]).then_inc(consts, 1)
            for m, base, cm, step in ((incl_blk, 0, -1, 1), (after_blk, -1, 1, -1), (before_blk, -1, -1, 1)):
                link(pool.memset(m[:], 1.0))
                keep(m[:], [[step, P]], base, cm)
                v = m[:].rearrange("p (b n) -> p b n", n=CHUNK)
                keep(v, [[-CHUNK, P // CHUNK], [0, CHUNK]], 0, 1)
                keep(v, [[CHUNK, P // CHUNK], [0, CHUNK]], CHUNK - 1, -1)
            for lev in range(7):
                w = 1 << (lev % 6)
                link(pool.memset(lev_f[:], 0.0))
                v = lev_f[:].rearrange("p (b n) -> p b n", n=2 * w)
                lo_half = v[:, :, 0:w] if lev < 6 else v[:, :, w:2 * w]
                link(pool.memset(lo_half, 1.0))
                nb = P // (2 * w)
                first = w if lev < 6 else 0
                keep(lo_half, [[-2 * w, nb], [0, w]], -first, 1)
                keep(lo_half, [[2 * w, nb], [0, w]], first + w - 1, -1)
                link(pool.tensor_copy(lev_mask[:, lev, :], lev_f[:]))
            link(pool.memset(am0[:], 0.0))
            link(pool.memset(am0[0:CHUNK, CHUNK:2 * CHUNK], NEG))
            link(pool.memset(am1[:], 0.0))
            link(pool.memset(am1[0:CHUNK, 0:CHUNK], NEG))
            link(pool.memset(am1[0:CHUNK, 3 * CHUNK:4 * CHUNK], NEG))
            pool.memset(am1[CHUNK:P, 0:2 * CHUNK], NEG).then_inc(consts, 1)

            pool.wait_ge(consts, 3)
            pool.wait_ge(rope_s, 1)
            for l in range(L):
                pool.wait_ge(sw_s, 6 * (l + 1))
                cs = [rope[:, :, i, :].unsqueeze(2).to_broadcast([P, TB, 10, HALF]) for i in range(2)]
                x1, x2 = a_qk[:, :, :, 0:HALF], a_qk[:, :, :, HALF:ROT]
                pr = [a_rt[:, i, :].rearrange("p (t h e) -> p t h e", t=TB, h=10) for i in range(4)]
                pool.tensor_tensor(pr[0], x1, cs[1], ALU.mult)
                pool.tensor_tensor(pr[1], x2, cs[0], ALU.mult)
                pool.tensor_tensor(pr[2], x2, cs[1], ALU.mult)
                link(pool.tensor_tensor(pr[3], x1, cs[0], ALU.mult))
                pool.tensor_tensor(x1, pr[0], pr[1], ALU.subtract)
                pool.tensor_tensor(x2, pr[2], pr[3], ALU.add).then_inc(rot_s, 1)

            pool.wait_ge(mix_s, 4 * L)
            for t in (e_acc, e_y, slot_of, wt_of):
                pool.memset(t[:], 0.0)
            pool.memset(e_pwT[:], 0.0).then_inc(pwt_s, 1)
            link(pool.memset(upper[:], 1.0))
            pool.affine_select(out=upper[:], in_=upper[:], compare_op=ALU.is_ge, fill=0.0, base=-1,
                               pattern=[[1, P]], channel_multiplier=-1).then_inc(upper_s, 1)

        @block.scalar
        def _(act):
            n_chain = [0]

            def link(ins):
                n_chain[0] += 1
                ins.then_inc(act_c, 1)
                act.wait_ge(act_c, n_chain[0])

            done = [0]

            def hi(n, u_wait, ring_slot, buf, free):
                act.wait_ge(landed[ring_slot], u_wait)
                if free is not None:
                    act.wait_ge(split_used, free)
                act.copy(w_hi[buf][:], ring[:, ring_slot, :]).then_inc(hi_ready, 1)

            def ahead(key, by=1):
                upto = min(s_of[key] + by, S0 - 1)
                while done[0] <= upto:
                    s = done[0]
                    u = u_of[split_keys[s]]
                    hi(s, landed_at[u], u % RING, s % NS_PRE, s - NS_PRE + 1 if s >= NS_PRE else None)
                    done[0] += 1

            def product(key, by=1):
                ahead(key, by)
                act.wait_ge(split_used, s_of[key] + 1)

            def norm(m, tmp):
                for tb in range(TB):
                    act.activation(tmp[:, tb * 4:(tb + 1) * 4, :].rearrange("p a b -> p (a b)"), xs[:, tb, :],
                                   ACT.Square, accum_out=stat[:, tb:tb + 1]).then_inc(ssq, 1)
                act.wait_ge(ssq, 2 * m + 2)
                act.activation(stat[:, 2:4], stat[:, 0:2], ACT.Sqrt, bias=eps_c[:, 0:1],
                               scale=1.0 / D).then_inc(rstd_s, 1)

            def h_high(m, tmp):
                for kp in range(4):
                    act.wait_ge(hmod, 4 * m + kp + 1)
                    act.copy(hT_hi[:, 2 * kp:2 * kp + 2, :], tmp[:, 2 * kp:2 * kp + 2, :]).then_inc(h_hi_s, 1)

            act.wait_ge(cols_s, 1)
            act.activation(c_silu[:], cols[:, COL_C:COL_C + KO], ACT.Silu).then_inc(csil, 1)
            act.wait_ge(rope_pre, 1)
            act.activation(rope[:].rearrange("p t k e -> p (t k e)"), ang[:, 5, :], ACT.Sin).then_inc(rope_s, 1)
            act.copy(ba_hi[:].rearrange("p l k n -> p (l k n)"), ba_raw).then_inc(small_hi, 1)
            act.copy(rw_hi[:].rearrange("p k n -> p (k n)"), rw_raw).then_inc(small_hi, 1)

            for l in range(L):
                if l == 0:
                    act.wait_ge(x_in, 16)
                else:
                    act.wait_ge(xf_s, 1)
                    act.wait_ge(ada_ps, l + 1)
                norm(2 * l, m_tmp)
                h_high(2 * l, m_tmp)

                def silu_of(j):
                    act.wait_ge(conv_s, 6 * l + j + 1)
                    act.activation(qkv[:, 2 * j:2 * j + 2, :], cv[j % 2], ACT.Silu).then_inc(qkv_s, 1)
                    if j < 4:
                        act.wait_ge(qkv_s, 8 * l + j + 1)
                        if j >= 2:
                            act.wait_ge(l2_ps, 4 * l + j - 1)
                        act.activation(sq[j % 2], qkv[:, 2 * j:2 * j + 2, :].rearrange("p a b -> p (a b)"),
                                       ACT.Square).then_inc(sq_s, 1)

                for j in range(6):
                    product(("qkvz", l, j))
                    if j >= 2:
                        act.wait_ge(conv_s, 6 * l + j - 1)
                    act.copy(raw[j % 2][:, :, PAD:], ps[j % 2][:].rearrange("p (a b) -> p a b", a=2)).then_inc(raw_s, 1)
                    if j:
                        silu_of(j - 1)
                silu_of(5)
                for j in (6, 7):
                    product(("qkvz", l, j))
                    act.activation(qkv[:, 2 * j:2 * j + 2, :].rearrange("p a b -> p (a b)"), ps[j % 2][:],
                                   ACT.Silu).then_inc(qkv_s, 1)
                product(("swq", l, 1))
                for tb in range(TB):
                    act.copy(a_qk[:, tb, 0:NQH, :].rearrange("p (j g) d -> p g j d", g=G),
                             ps[2 + tb][:].rearrange("p (g j d) -> p g j d", g=G, j=J)).then_inc(sw_s, 1)
                product(("swkv", l))
                for tb in range(TB):
                    act.copy(a_qk[:, tb, NQH:NQH + G, :],
                             ps[tb][:, 0:P].rearrange("p (g d) -> p g d", g=G)).then_inc(sw_s, 1)
                    act.copy(a_v[:, tb, :], ps[tb][:, P:2 * P]).then_inc(sw_s, 1)
                for j in range(4):
                    act.wait_ge(l2_ps, 4 * l + j + 1)
                    act.activation(rinv[:, 2 * j:2 * j + 2, :].rearrange("p a b -> p (a b)"), ps[4 + j][:],
                                   ACT.Ln, bias=eps_c[:, 0:1]).then_inc(ln_s, 1)
                act.wait_ge(ln_s, 4 * (l + 1))
                act.activation(rinv, rinv, ACT.Exp, scale=-0.5).then_inc(rinv_s, 1)
                act.wait_ge(beta_a, l + 1)
                act.activation(gb[:, 0], ba[:, :, 0:H], ACT.Exp, scale=-1.0)
                link(act.activation(gb[:, 4], gb[:, 3], ACT.Exp, scale=-1.0))
                if l == 0:
                    act.activation(head_rows[:, 2 * L * H:3 * L * H], head_rows[:, 0:L * H], ACT.Exp)
                act.activation(gb[:, 4], gb[:, 4], ACT.Ln, bias=one_c[:, 0:1]).then_inc(beta_e, 1)

                def att(t):
                    act.wait_ge(att_ps, NTASK * l + t + 1)

                for t in (0, 1):
                    att(t)
                    act.copy(a_qT[:, 2 * t:2 * t + 2, :].rearrange("p a b -> p (a b)"),
                             ps[t % 4][:]).then_inc(att_a, 1)
                att(2)
                act.copy(a_kT, ps[2][:, 0:T]).then_inc(att_a, 1)
                for tb in range(TB):
                    keys = P * (tb + 1)
                    act.wait_ge(mx_s, TB * l + tb + 1)
                    act.activation(smax[:, 3, :], smax[:, 3, :], ACT.Exp)
                    for h in range(NQH):
                        ins = act.activation(a_s[:, h, 0:keys], a_s[:, h, 0:keys], ACT.Exp,
                                             bias=smax[:, 0, h:h + 1], accum_out=smax[:, 2, h:h + 1])
                    ins.then_inc(pe_s, 1)
                    for n in range(2 * (tb + 1)):
                        t = T_TURN[tb] + n
                        att(t)
                        act.copy(a_pt[:, 4 * n:4 * n + 4, :].rearrange("p a b -> p (a b)"),
                                 ps[t % 4][:]).then_inc(att_a, 1)
                    for g in range(G):
                        t = T_PV[tb] + g
                        att(t)
                        rows = slice(g * DH, (g + 1) * DH)
                        act.copy(ob_hi[rows, :, tb * P:(tb + 1) * P],
                                 ps[t % 4][rows, :].rearrange("p (j q) -> p j q", j=J)).then_inc(obh_s, 1)
                for tb in range(TB):
                    act.wait_ge(maps, 4 * l + 2)
                    act.activation(EG[:, :, tb * P:(tb + 1) * P], ps[6 + tb][:].rearrange("p (h c) -> p h c", h=H),
                                   ACT.Exp).then_inc(exps_s, 1)
                for tb in range(TB):
                    act.wait_ge(maps, 4 * l + 3)
                    act.activation(ED[:, :, tb * P:(tb + 1) * P], ps[4 + tb][:].rearrange("p (h c) -> p h c", h=H),
                                   ACT.Exp).then_inc(exps_s, 1)
                for tb in range(TB):
                    act.wait_ge(maps, 4 * l + 4)
                    act.activation(X[:, tb * H:(tb + 1) * H, :].rearrange("p h c -> p (h c)"), ps[6 + tb][:],
                                   ACT.Exp).then_inc(exps_s, 1)

                def gate(j):
                    product(("gate", l, j))
                    act.activation(gate_sb[:, 2 * j:2 * j + 2, :].rearrange("p a b -> p (a b)"),
                                   ps[j % 2][:], ACT.Sigmoid).then_inc(gate_s, 1)

                for n in range(4):
                    act.wait_ge(tok_ps, 4 * l + n + 1)
                    dst = (v_tok, k_tok)[n // 2][:, n % 2]
                    act.copy(dst.rearrange("p h d -> p (h d)"), ps[2 + n][:]).then_inc(tok_s, 1)
                for j in range(5):
                    gate(j)
                for n in range(NCH):
                    rows = slice((n % 2) * CHUNK, (n % 2 + 1) * CHUNK)
                    if n < 3:
                        ahead(("gate", l, 5 + n), 0)
                    act.wait_ge(vn_ps, NCH * l + n + 1)
                    act.copy(v_new[rows].rearrange("p h d -> p (h d)"), ps[5][rows, :]).then_inc(vn_s, 1)
                    act.wait_ge(o_ps, NCH * l + n + 1)
                    act.copy(OT[:, :, n * CHUNK:(n + 1) * CHUNK],
                             ps[7][:, 0:H * CHUNK].rearrange("p (h c) -> p h c", h=H)).then_inc(o_s, 1)
                    if n < 3:
                        gate(5 + n)
                ahead(("wa", l, 1), 0)
                act.wait_ge(o_s, NCH * (l + 1))
                act.activation(o_sq, OT, ACT.Square).then_inc(osq_s, 1)
                act.wait_ge(on_ps, l + 1)
                for n in range(2):
                    act.activation(o_r[:, 2 * n:2 * n + 2, :].rearrange("p a b -> p (a b)"), ps[4 + n][:],
                                   ACT.Ln, bias=eps_c[:, 0:1], scale=1.0 / DK).then_inc(ln2_s, 1)
                act.wait_ge(ln2_s, 2 * (l + 1))
                act.activation(o_r, o_r, ACT.Exp, scale=-0.5).then_inc(on_s, 1)
                act.wait_ge(oaf, l + 1)
                act.copy(oa_hi[:], OT).then_inc(oa_h, 1)
                for cc in range(2):
                    ahead(("wb", l, cc), 1)
                    act.wait_ge(yb_s, 4 * l + 3 + cc)
                    act.copy(hT_hi[:, 4 * cc:4 * cc + 4, :], y_sum[:, 4 * cc:4 * cc + 4, :]).then_inc(y_hi_s, 1)
                ahead(("mix", l, 1, 1), 1)
                act.wait_ge(mix_s, 4 * (l + 1))
                if l == 0:
                    ahead(("fg", 0), 1)
                    norm(1, f_tmp)
                    h_high(1, f_tmp)

                    def f_silu(i):
                        product(("fg", i))
                        if i >= 2:
                            act.wait_ge(fh_s, i - 1)
                        act.activation(f_g[i % 2][:].rearrange("p a b -> p (a b)"), ps[2 * (i % 2)][:],
                                       ACT.Silu).then_inc(fs_s, 1)

                    def f_high(i):
                        if i >= 2:
                            ahead(("fd", i - 2), 1)
                            act.wait_ge(split_used, s_of[("fd", i - 2)] + 1)
                        act.wait_ge(fh_s, i + 1)
                        act.copy(f_hi[i % 2][:], f_h[:]).then_inc(fhh_s, 1)

                    for i in range(2 * FC):
                        f_silu(i)
                        ahead(("fu", i), 1)
                        f_high(i)
                    ahead(("qkvz", 1, 0), 0)
            act.wait_ge(mix_s, 4 * L)
            norm(3, e_tmp)
            h_high(3, e_tmp)
            act.wait_ge(lg_s, 1)
            act.activation(lg[:, 8, :, 0:1], lg[:, 8, :, 0:1], ACT.Exp).then_inc(lge_s, 1)
            act.wait_ge(ga_s, 2)
            act.copy(xg_hi[:], e_xf[:]).then_inc(xgh_s, 1)
            act.copy(stat[:, 9:10], one_c[:]).then_inc(ms_s, 1)
            act.wait_ge(route_s, 1)
            n_items = act.value_load(meta[0:1, 0:1], min_val=E, max_val=E + 3)

            def copy_y(i):
                act.wait_ge(cb_ps, 4 * i + 1)
                act.wait_ge(split_used, S0 + MU * i)
                for n in range(2):
                    act.copy(e_y[:, n * 512:(n + 1) * 512], ps[6 + n][:]).then_inc(y_c, 1)

            with act.Fori(0, n_items) as i:
                def split(p):
                    act.wait_ge(landed[p % RING],
                                16 * (MU // RING) * i + (level[p % RING] + 16 * (p // RING + 1)))
                    act.wait_ge(split_used, MU * i + (S0 + p - NS_MOE + 1))
                    act.copy(w_hi[p % NS_MOE][:], ring[:, p % RING, :]).then_inc(hi_ready, 1)

                split(0)
                split(1)
                copy_y(i)
                for p, (kind, fc, half) in enumerate(moe_units):
                    if p + 2 < MU:
                        split(p + 2)
                    if kind == "g" and half == 1:
                        act.wait_ge(split_used, MU * i + (S0 + p + 1))
                        act.wait_ge(mh_s, FC * i + max(fc, 1))
                        act.activation(e_g[fc % 2][:], ps[2 * (fc % 2)][:], ACT.Silu).then_inc(ms_s, 1)
                    f = turned_after.get(p)
                    if f is not None:
                        act.wait_ge(mt_ps, FC * i + (f + 2))
                        act.wait_ge(split_used, MU * i + (S0 + (mp[("d", f - 2, 1)] + 1 if f >= 2 else 0)))
                        act.copy(h_hi[f % 2][:].rearrange("p a b -> p (a b)"), ps[4][:]).then_inc(mhh_s, 1)
                    if (kind, fc, half) == ("d", FC - 2, 1):
                        act.wait_ge(ga_s, 2 * i + 4)
                        act.wait_ge(split_used, MU * i + (S0 + mp[("u", FC - 1, 1)] + 1))
                        act.copy(xg_hi[:], e_xf[:]).then_inc(xgh_s, 1)
            copy_y(n_items)
            act.wait_ge(xf_s, 2)
            norm(4, e_tmp)

        @block.tensor
        def _(pe):
            def by_token(o, xh, xl, wh, wl, start, stop):
                pe.matmul(o, xh, wh, start=start, stop=False)
                pe.matmul(o, xh, wl, start=False, stop=False)
                return pe.matmul(o, xl, wh, start=False, stop=stop)

            def by_channel(o, wh, wl, xh, xl, start, stop):
                pe.matmul(o, wh, xh, start=start, stop=False)
                pe.matmul(o, wh, xl, start=False, stop=False)
                return pe.matmul(o, wl, xh, start=False, stop=stop)

            def parts(key, k):
                pe.wait_ge(taken, u_of[key] + 1)
                b = s_of[key] % NS_PRE
                return (w_hi[b][:].rearrange("p (k n) -> p k n", k=k),
                        w_lo[b][:].rearrange("p (k n) -> p k n", k=k))

            def tokens(tb):
                return slice(tb * P, (tb + 1) * P)

            def turn_x(m, xn):
                pe.wait_ge(xn_s, 2 * m + 2)
                for kp in range(4):
                    for k in range(2):
                        for tb in range(TB):
                            ins = pe.transpose(ps[4 + kp][:, k * T + tb * P:k * T + (tb + 1) * P],
                                               xn[:, tb, (2 * kp + k) * P:(2 * kp + k + 1) * P], ident[:])
                    ins.then_inc(xnT, 1)

            def two_blocks(key, bank):
                wh, wl = parts(key, KO)
                for t in range(2):
                    for ko in range(KO):
                        ins = by_channel(ps[bank][:, t * T:(t + 1) * T], wh[:, ko, t * P:(t + 1) * P],
                                         wl[:, ko, t * P:(t + 1) * P], hT_hi[:, ko, :], hT_lo[:, ko, :],
                                         ko == 0, ko == KO - 1)
                ins.then_inc(split_used, 1)

            def gate_row(n, dg, banks):
                pe.wait_ge(gtd_s, n)
                for k in range(2):
                    ins = pe.matmul(ps[banks[k]][:], ones[:],
                                    dg[:, 4 * k:4 * k + 4, :].rearrange("p a b -> p (a b)"), start=True, stop=True)
                ins.then_inc(gt_ps, 1)

            pe.wait_ge(consts, 1)
            pe.wait_ge(setup_in, SETUP_IN)
            pe.transpose(ps[0][:, 0:P], prm_a, ident[:])
            pe.transpose(ps[0][:, P:2 * P], prm_b, ident[:]).then_inc(prm_t, 1)

            for l in range(L):
                if l == 1:
                    pe.wait_ge(fh_s, 2 * FC)
                    pe.wait_ge(xf_s, 1)
                else:
                    pe.wait_ge(cols_s, 1)
                acc = m_acc if l == 0 else f_acc
                for q in range(12):
                    pe.wait_ge(taken, u_of[("ada", l, q, 1)] + 1)
                    for t in range(4):
                        ins = pe.matmul(ps[0][:, 4 * q + t:4 * q + t + 1], acc[:, q, t * P:(t + 1) * P],
                                        ones[:, 0:1], start=True, stop=True)
                ins.then_inc(ada_ps, 1)

                turn_x(2 * l, m_xn)
                pe.wait_ge(h_s, 4 * (2 * l) + 4)
                pe.wait_ge(small_lo, 2)
                for tb in range(TB):
                    for ko in range(KO):
                        ins = by_token(ps[2][:, 8 * tb:8 * tb + 8], hT_hi[:, ko, tokens(tb)], hT_lo[:, ko, tokens(tb)],
                                       ba_hi[:, l, ko, :], ba_lo[:, l, ko, :], ko == 0, ko == KO - 1)
                ins.then_inc(ba_ps, 1)

                def l2(j):
                    pe.wait_ge(sq_s, 4 * l + j + 1)
                    pe.matmul(ps[4 + j][:], ones[:], sq[j % 2], start=True, stop=True).then_inc(l2_ps, 1)

                pe.wait_ge(ada_s, l + 1)
                for j in range(8):
                    if j >= 2:
                        pe.wait_ge(raw_s, 6 * l + min(j - 1, 6))
                    two_blocks(("qkvz", l, j), j % 2)
                    if 3 <= j < 7:
                        l2(j - 3)
                pe.wait_ge(ba_s, l + 1)
                for kh in range(2):
                    wh, wl = parts(("swq", l, kh), 4)
                    for tb in range(TB):
                        for kk in range(4):
                            ko = 4 * kh + kk
                            ins = by_token(ps[2 + tb][:], hT_hi[:, ko, tokens(tb)], hT_lo[:, ko, tokens(tb)],
                                           wh[:, kk, :], wl[:, kk, :], ko == 0, ko == KO - 1)
                    ins.then_inc(split_used, 1)
                pe.wait_ge(qkv_s, 8 * (l + 1))
                wh, wl = parts(("swkv", l), KO)
                for tb in range(TB):
                    for ko in range(KO):
                        ins = by_token(ps[tb][:, 0:2 * P], hT_hi[:, ko, tokens(tb)], hT_lo[:, ko, tokens(tb)],
                                       wh[:, ko, :], wl[:, ko, :], ko == 0, ko == KO - 1)
                ins.then_inc(split_used, 1)

                def step(t):
                    if t >= 4:
                        att_freed(pe, l, t - 4)
                    return ps[t % 4]

                pe.wait_ge(rot_s, l + 1)
                pe.wait_ge(sw_s, 6 * (l + 1))
                for t in (0, 1):
                    b = step(t)
                    for jj in range(2):
                        for tb in range(TB):
                            j = 2 * t + jj
                            ins = pe.transpose(b[:, jj * T + tb * P:jj * T + (tb + 1) * P],
                                               a_qk[:, tb, 2 * j:2 * j + 2, :].rearrange("p g d -> p (g d)"), ident[:])
                    ins.then_inc(att_ps, 1)
                b = step(2)
                for tb in range(TB):
                    ins = pe.transpose(b[:, tb * P:(tb + 1) * P],
                                       a_qk[:, tb, NQH:NQH + G, :].rearrange("p g d -> p (g d)"), ident[:])
                ins.then_inc(att_ps, 1)
                pe.wait_ge(att_a, NATT_A * l + 3)

                def scores(tb):
                    keys, per = P * (tb + 1), 4 // (tb + 1)
                    for n in range(NQH // per):
                        t = T_SCORE[tb] + n
                        b = step(t)
                        for m in range(per):
                            h = n * per + m
                            g, j = divmod(h, J)
                            rows = slice(g * DH, (g + 1) * DH)
                            ins = pe.matmul(b[:, m * keys:(m + 1) * keys], a_qT[rows, j, tokens(tb)],
                                            a_kT[rows, 0:keys], start=True, stop=True)
                        ins.then_inc(att_ps, 1)

                def turn_p(tb):
                    pe.wait_ge(pn_s, TB * l + tb + 1)
                    for n in range(2 * (tb + 1)):
                        b = step(T_TURN[tb] + n)
                        for m in range(4):
                            h, kb = divmod(4 * n + m, tb + 1)
                            ins = pe.transpose(b[:, m * P:(m + 1) * P], a_s[:, h, tokens(kb)], ident[:])
                        ins.then_inc(att_ps, 1)

                def p_v(tb):
                    for g in range(G):
                        b = step(T_PV[tb] + g)
                        pe.wait_ge(att_a, NATT_A * l + 5 + 4 * tb)
                        for j in range(J):
                            for kb in range(tb + 1):
                                ins = pe.matmul(b[:, j * P:(j + 1) * P], a_v[:, kb, :],
                                                a_pt[:, (g * J + j) * (tb + 1) + kb, :],
                                                start=kb == 0, stop=kb == tb)
                        ins.then_inc(att_ps, 1)

                scores(0)
                turn_p(0)
                p_v(0)
                scores(1)
                turn_p(1)
                p_v(1)

                def spread(lhsT, rows, banks):
                    for tb in range(TB):
                        ins = pe.matmul(ps[banks + tb][:], lhsT, rows[:, tb, :], start=True, stop=True)
                    ins.then_inc(maps, 1)

                pe.wait_ge(grow_s, l + 1)
                spread(ones[:], g_rows[0], 4)
                spread(ones[:], g_rows[2], 6)
                pe.wait_ge(kb_s, 2 * (l + 1))
                spread(ones[:], g_rows[1], 4)
                pe.wait_ge(exps_s, 6 * l + 2)
                spread(after_blk[:], g_rows[2], 6)

                pe.wait_ge(exps_s, 6 * l + 4)
                for tb in range(TB):
                    for h in range(H):
                        ins = pe.matmul(ps[4 + tb][:, h * P:(h + 1) * P], kT[:, h, tokens(tb)],
                                        KB[:, h, tokens(tb)], start=True, stop=True)
                ins.then_inc(lat, 1)
                pe.wait_ge(exps_s, 6 * l + 6)
                for tb in range(TB):
                    for h in range(H):
                        ins = pe.matmul(ps[6 + tb][:, h * P:(h + 1) * P], kT[:, h, tokens(tb)],
                                        qT[:, h, tokens(tb)], start=True, stop=True)
                ins.then_inc(lat, 1)
                pe.wait_ge(lat_s, 2 * l + 2)
                for tb in range(TB):
                    for h in range(H):
                        ins = pe.transpose(ps[6 + tb][:, h * P:(h + 1) * P], LT[:, tb * H + h, :], ident[:])
                ins.then_inc(l0_ps, 1)
                pe.wait_ge(kgb_s, l + 1)
                pe.wait_ge(att_d, NATT_D * (l + 1))
                for n in range(4):
                    src = (vT, kT)[n // 2]
                    for h in range(H):
                        ins = pe.transpose(ps[2 + n][:, h * P:(h + 1) * P], src[:, h, tokens(n % 2)], ident[:])
                    ins.then_inc(tok_ps, 1)
                pe.wait_ge(tok_s, 4 * (l + 1))
                pe.wait_ge(inv0, l + 1)
                for lev in range(1, 6):
                    for tb in range(TB):
                        if lev > 1:
                            pe.wait_ge(xx_s, 10 * l + 2 * (lev - 2) + tb + 1)
                        for h in range(H):
                            n = tb * H + h
                            ins = pe.matmul(ps[4 + tb][:, h * P:(h + 1) * P], LT[:, n, :], X[:, n, :],
                                            start=True, stop=True)
                        ins.then_inc(u_ps, 1)
                    if lev > 2:
                        pe.wait_ge(gate_s, 8 * l + lev - 2)
                    two_blocks(("gate", l, lev - 1), (lev - 1) % 2)
                    for tb in range(TB):
                        pe.wait_ge(u_s, 10 * l + 2 * (lev - 1) + tb + 1)
                        for h in range(H):
                            n = tb * H + h
                            if lev < 5:
                                pe.matmul(ps[6 + tb][:, h * P:(h + 1) * P], XT[:, n, :], U[:, n, :],
                                          start=True, stop=True)
                            ins = pe.matmul(ps[2 + tb][:, h * P:(h + 1) * P], U[:, n, :], XT[:, n, :],
                                            start=True, stop=True)
                        ins.then_inc(xu_ps, 1)
                pe.wait_ge(xx_s, 10 * (l + 1))

                for n in range(NCH):
                    tb, par = divmod(n, 2)
                    rows = slice(par * CHUNK, (par + 1) * CHUNK)
                    here = slice(n * CHUNK, (n + 1) * CHUNK)
                    if n > 0:
                        pe.wait_ge(st_s, 3 * l + n)
                        for h in range(H):
                            ins = pe.matmul(ps[4][rows, h * P:(h + 1) * P], KB[:, h, here], state[:, h, :],
                                            start=True, stop=True)
                        ins.then_inc(ks_ps, 1)
                        pe.wait_ge(res_s, 3 * l + n)
                    src = resid[rows] if n else v_tok[rows, tb]
                    if n:
                        pe.wait_ge(vn_s, NCH * l + n)
                    for h in range(H):
                        ins = pe.matmul(ps[5][rows, h * P:(h + 1) * P], XT[rows, tb * H + h, rows], src[:, h, :],
                                        start=True, stop=True)
                    ins.then_inc(vn_ps, 1)
                    if n:
                        pe.wait_ge(o_s, NCH * l + n)
                    pe.wait_ge(vn_s, NCH * l + n + 1)
                    for h in range(H):
                        o = ps[7][:, h * CHUNK:(h + 1) * CHUNK]
                        if n:
                            pe.matmul(o, state[:, h, :], qT[:, h, here], start=True, stop=False)
                        ins = pe.matmul(o, v_new[rows, h, :], AT[rows, tb * H + h, rows], start=n == 0, stop=True)
                    ins.then_inc(o_ps, 1)
                    if n < NCH - 1:
                        for h in range(H):
                            ins = pe.matmul(ps[6][:, h * P:(h + 1) * P], k_tok[rows, tb, h, :], v_new[rows, h, :],
                                            start=True, stop=True)
                        ins.then_inc(su_ps, 1)
                        pe.wait_ge(gate_s, 8 * l + 4 + n)
                        two_blocks(("gate", l, 5 + n), (5 + n) % 2)
                pe.wait_ge(osq_s, l + 1)
                for n in range(2):
                    ins = pe.matmul(ps[4 + n][:], ones[:], o_sq[:, 2 * n:2 * n + 2, :].rearrange("p a b -> p (a b)"),
                                    start=True, stop=True)
                ins.then_inc(on_ps, 1)

                pe.wait_ge(gate_s, 8 * (l + 1))
                for br, (xh, xl, ready) in enumerate(((oa_hi, oa_lo, oa_s), (ob_hi, ob_lo, att_d))):
                    pe.wait_ge(ready, (l + 1) * (NATT_D if br else 1))
                    for cc in range(2):
                        wh, wl = parts((("wa", "wb")[br], l, cc), 4)
                        if br:
                            pe.wait_ge(on_s, l + 1)
                        for t in range(4):
                            bank = ps[4 * br + 2 * cc + t // 2]
                            for k in range(4):
                                ins = by_channel(bank[:, (t % 2) * T:(t % 2 + 1) * T], wh[:, k, t * P:(t + 1) * P],
                                                 wl[:, k, t * P:(t + 1) * P], xh[:, k, :], xl[:, k, :],
                                                 k == 0, k == 3)
                        ins.then_inc(split_used, 1)
                pe.wait_ge(yb_s, 4 * (l + 1))
                gate_row(2 * l + 1, m_dg, (4, 5))
                for cc in range(2):
                    for kh in range(2):
                        wh, wl = parts(("mix", l, cc, kh), 4)
                        pe.wait_ge(y_s, 2 * l + kh + 1)
                        for tb in range(TB):
                            for kk in range(4):
                                ko = 4 * kh + kk
                                ins = by_token(ps[2 * cc + tb][:], hT_hi[:, ko, tokens(tb)], hT_lo[:, ko, tokens(tb)],
                                               wh[:, kk, :], wl[:, kk, :], ko == 0, ko == KO - 1)
                        ins.then_inc(split_used, 1)

                if l == 0:
                    turn_x(1, f_xn)
                    pe.wait_ge(h_s, 8)

                    def f_down(i):
                        wh, wl = parts(("fd", i), 2)
                        pe.wait_ge(fhl_s, i + 1)
                        for tb in range(TB):
                            for hf in range(2):
                                for ft in range(2):
                                    cs = slice(hf * 512, (hf + 1) * 512)
                                    ins = by_token(ps[4 + 2 * tb + hf][:], f_hi[i % 2][:, ft, tokens(tb)],
                                                   f_lo[i % 2][:, ft, tokens(tb)], wh[:, ft, cs], wl[:, ft, cs],
                                                   i == 0 and ft == 0, i == 2 * FC - 1 and ft == 1)
                        ins.then_inc(split_used, 1)

                    for i in range(2 * FC):
                        if i >= 2:
                            pe.wait_ge(fs_s, i - 1)
                        two_blocks(("fg", i), 2 * (i % 2))
                        if i >= 2:
                            pe.wait_ge(fh_s, i - 1)
                        two_blocks(("fu", i), 2 * (i % 2) + 1)
                        if i:
                            f_down(i - 1)
                    f_down(2 * FC - 1)
                    gate_row(2, f_dg, (0, 1))

            turn_x(3, e_xn)
            pe.wait_ge(h_s, 16)
            for tb in range(TB):
                for ko in range(KO):
                    ins = by_token(ps[2][:, E * tb:E * (tb + 1)], hT_hi[:, ko, tokens(tb)], hT_lo[:, ko, tokens(tb)],
                                   rw_hi[:, ko, :], rw_lo[:, ko, :], ko == 0, ko == KO - 1)
            ins.then_inc(logit_ps, 1)
            pe.wait_ge(upper_s, 1)
            pe.matmul(ps[3][:, 0:P], ones[:], upper[:], start=True, stop=True).then_inc(logit_ps, 1)
            pe.wait_ge(sel_s, 1)
            sel = [lg[:, 6, tb, :] for tb in range(TB)]
            pe.matmul(ps[5][:, 0:E], upper[:], sel[0], start=True, stop=True).then_inc(mt_ps, 1)
            pe.matmul(ps[5][:, E:2 * E], ones[:], sel[0], start=True, stop=False).then_inc(cb_ps, 1)
            pe.matmul(ps[5][:, E:2 * E], upper[:], sel[1], start=False, stop=True)
            pe.matmul(ps[5][:, 2 * E:3 * E], ones[:], sel[0], start=True, stop=False)
            pe.matmul(ps[5][:, 2 * E:3 * E], ones[:], sel[1], start=False, stop=True).then_inc(pos_ps, 1)
            pe.wait_ge(route_s, 1)
            n_items = pe.value_load(meta[0:1, 0:1], min_val=E, max_val=E + 3)

            def gather(piece, done):
                pe.wait_ge(ga_s, done)
                for k in range(4):
                    for tb in range(TB):
                        ko = 4 * piece + k
                        ins = pe.matmul(ps[5][:, k * P:(k + 1) * P], e_xn[:, tb, ko * P:(ko + 1) * P],
                                        e_p[:, tb, :], start=tb == 0, stop=tb == TB - 1)
                ins.then_inc(ga_ps, 1)

            def combine(i, k):
                tb, hf = divmod(k, 2)
                if k == 0:
                    pe.wait_ge(y_c, 2 * i + 2)
                    pe.wait_ge(pwt_s, i + 1)
                    pe.wait_ge(ga_s, 2 * i + 2)
                pe.wait_ge(cb_s, 4 * i + (k + 1))
                pe.matmul(ps[5][:], e_pwT[:, tokens(tb)], e_y[:, hf * 512:(hf + 1) * 512],
                          start=True, stop=True).then_inc(cb_ps, 1)

            pe.wait_ge(p_s, 1)
            gather(0, 0)
            gather(1, 1)
            with pe.Fori(0, n_items) as i:
                for p, (kind, fc, half) in enumerate(moe_units):
                    b = p % NS_MOE
                    pe.wait_ge(taken, MU * i + (U0 + p + 1))
                    if kind in "gu":
                        if p == 0:
                            pe.wait_ge(xg_s, i + 1)
                        if half == 0:
                            pe.wait_ge(ms_s if kind == "g" else mh_s, FC * i + max(fc, 1))
                        wh, wl = (w[b][:].rearrange("p (k n) -> p k n", k=4) for w in (w_hi, w_lo))
                        bank = ps[2 * (fc % 2) + (kind == "u")]
                        for kk in range(4):
                            ko = 4 * half + kk
                            ins = by_token(bank[:], xg_hi[:, ko, :], xg_lo[:, ko, :], wh[:, kk, :], wl[:, kk, :],
                                           ko == 0, ko == KO - 1)
                    else:
                        if half == 0:
                            pe.wait_ge(mhl_s, FC * i + (fc + 2))
                            if fc == 0:
                                pe.wait_ge(y_c, 2 * i + 2)
                        wh, wl = (w[b][:].rearrange("p (k n) -> p k n", k=2) for w in (w_hi, w_lo))
                        for hf in range(2):
                            for ft in range(2):
                                f = 2 * half + ft
                                cs = slice(hf * 512, (hf + 1) * 512)
                                ins = by_token(ps[6 + hf][:], h_hi[fc % 2][:, f, :], h_lo[fc % 2][:, f, :],
                                               wh[:, ft, cs], wl[:, ft, cs], fc == 0 and f == 0,
                                               fc == FC - 1 and f == 3)
                    ins.then_inc(split_used, 1)
                    if p < 4:
                        combine(i, p)
                    f = turned_after.get(p)
                    if f is not None:
                        pe.wait_ge(mh_s, FC * i + (f + 2))
                        pe.wait_ge(mhl_s, FC * i + (f + 1))
                        for k in range(4):
                            ins = pe.transpose(ps[4][:, k * P:(k + 1) * P], e_h[f % 2][:, k * P:(k + 1) * P], ident[:])
                        ins.then_inc(mt_ps, 1)
                    if p == mp[("g", 2, 0)]:
                        pe.wait_ge(pw_s, i + 1)
                        pe.wait_ge(cb_s, 4 * i + 5)
                        for tb in range(TB):
                            ins = pe.transpose(ps[5][:, tb * P:(tb + 1) * P], e_pw[:, tb, :], ident[:])
                        ins.then_inc(pwt_ps, 1)
                    if p == mp[("g", 4, 0)]:
                        pe.wait_ge(p_s, i + 2)
                        pe.wait_ge(pwt_s, i + 2)
                        gather(0, 2 * i + 2)
                    if p == mp[("g", 4, 1)]:
                        gather(1, 2 * i + 3)
            for k in range(4):
                combine(n_items, k)
            gate_row(4, e_dg, (0, 1))

        @block.vector
        def _(dve):
            n_chain = [0]

            def mark(ins):
                n_chain[0] += 1
                ins.then_inc(dve_c, 1)
                return n_chain[0]

            def link(ins):
                dve.wait_ge(dve_c, mark(ins))

            def f32(t):
                return t.bitcast(F32)

            def wide(ap, shape, axis):
                return ap.unsqueeze(axis).to_broadcast(shape)

            done = [0]

            def take(u):
                key = units[u][0]
                if key[0] != "ada":
                    s = s_of[key]
                    dve.wait_ge(hi_ready, s + 1)
                    dve.tensor_tensor(w_lo[s % NS_PRE][:], ring[:, u % RING, :], f32(w_hi[s % NS_PRE][:]),
                                      ALU.subtract).then_inc(taken, 1)
                    return
                l, q, kh = key[1:]
                acc = (m_acc if l == 0 else f_acc)[:, q, :]
                dve.wait_ge(landed[u % RING], landed_at[u])
                dve.wait_ge(taken, u)
                w = ring[:, u % RING, :].rearrange("p (k n) -> p k n", k=4)
                for kk in range(4):
                    ck = c_silu[:, 4 * kh + kk:4 * kh + kk + 1]
                    if kh == 0 and kk == 0:
                        ins = dve.tensor_scalar(acc, w[:, kk, :], ck, None, ALU.mult)
                    else:
                        ins = dve.scalar_tensor_tensor(acc, w[:, kk, :], ck, acc, ALU.mult, ALU.add)
                    if kk < 3:
                        link(ins)
                    else:
                        ins.then_inc(taken, 1)

            def take_upto(u):
                while done[0] <= u:
                    take(done[0])
                    done[0] += 1

            def ahead(key, by=1):
                take_upto(u_of[split_keys[min(s_of[key] + by, S0 - 1)]])

            def product(key, by=1):
                ahead(key, by)
                dve.wait_ge(split_used, s_of[key] + 1)

            def norm(m, xn):
                l, which = divmod(m, 2)
                w_at = (COL_NF if which else COL_NM) + l * KO
                link(dve.scalar_tensor_tensor(wsc[:], adac[:, l, (1 + 3 * which) * KO:(2 + 3 * which) * KO], 1.0,
                                              cols[:, w_at:w_at + KO], ALU.add, ALU.mult))
                dve.wait_ge(rstd_s, m + 1)
                link(dve.reciprocal(stat[:, 4:6], stat[:, 2:4]))
                for tb in range(TB):
                    dve.tensor_scalar(xn[:, tb, :], xs[:, tb, :], stat[:, 4 + tb:5 + tb], None,
                                      ALU.mult).then_inc(xn_s, 1)

            def modulate(m, tmp):
                l, which = divmod(m, 2)
                for kp in range(4):
                    dve.wait_ge(xnT, 4 * m + kp + 1)
                    for k in range(2):
                        ko = 2 * kp + k
                        sh = 3 * which * KO + ko
                        ins = dve.tensor_scalar(tmp[:, ko, :], ps[4 + kp][:, k * T:(k + 1) * T], wsc[:, ko:ko + 1],
                                                adac[:, l, sh:sh + 1], ALU.mult, ALU.add)
                    ins.then_inc(hmod, 1)
                for kp in range(4):
                    dve.wait_ge(h_hi_s, 4 * m + kp + 1)
                    two = slice(2 * kp, 2 * kp + 2)
                    dve.tensor_tensor(hT_lo[:, two, :], tmp[:, two, :], f32(hT_hi[:, two, :]),
                                      ALU.subtract).then_inc(h_s, 1)

            def gate_diag(n, l, v, dg):
                dve.tensor_tensor(dg, wide(ident[:], [P, KO, P], 1),
                                  wide(adac[:, l, v * KO:(v + 1) * KO], [P, KO, P], 2), ALU.mult).then_inc(gtd_s, 1)

            def gate_copy(n, gt, banks):
                dve.wait_ge(gt_ps, n)
                for k in range(2):
                    ins = dve.tensor_copy(gt[:, k * 512:(k + 1) * 512], ps[banks[k]][:])
                link(ins)

            dve.wait_ge(prm_t, 1)
            dve.tensor_copy(cols[:], ps[0][:, 0:2 * P]).then_inc(cols_s, 1)
            dve.wait_ge(setup_b, SETUP_B)
            dve.wait_ge(consts, 2)
            link(dve.tensor_copy(ang[:, 4, 0:TB], pos_i))
            for tb in range(TB):
                ins = dve.tensor_scalar(ang[:, 0, tb * ROT:(tb + 1) * ROT], invf, ang[:, 4, tb:tb + 1], None, ALU.mult)
            link(ins)
            link(dve.tensor_scalar(ang[:, 1, :], ang[:, 0, :], 1.0 / (2 * math.pi), None, ALU.mult))
            cosines = ang[:, 1, :].rearrange("p (t k e) -> p t k e", t=TB, k=2)[:, :, 1, :]
            link(dve.tensor_scalar(cosines, cosines, 0.25, None, ALU.add))
            magic = 1.5 * 2.0 ** 23
            link(dve.tensor_scalar(ang[:, 2, :], ang[:, 1, :], magic, None, ALU.add))
            link(dve.tensor_scalar(ang[:, 2, :], ang[:, 2, :], -magic, None, ALU.add))
            c1 = 6.28125
            c2 = float(np.frombuffer((np.frombuffer(np.float32(2 * math.pi - c1).tobytes(), np.uint32)
                                      & np.uint32(0xFFFFF000)).tobytes(), np.float32)[0])
            c3 = 2 * math.pi - c1 - c2
            for cpart in (c1, c2, c3):
                link(dve.scalar_tensor_tensor(ang[:, 0, :], ang[:, 2, :], -cpart, ang[:, 0, :], ALU.mult, ALU.add))
            cosines = ang[:, 0, :].rearrange("p (t k e) -> p t k e", t=TB, k=2)[:, :, 1, :]
            link(dve.tensor_scalar(cosines, cosines, math.pi / 2, None, ALU.add))
            dve.tensor_scalar(ang[:, 5, :], ang[:, 0, :], 3.1415925, -3.1415925, ALU.min,
                              ALU.max).then_inc(rope_pre, 1)
            dve.wait_ge(small_hi, 2)
            dve.tensor_tensor(ba_lo[:].rearrange("p l k n -> p (l k n)"), ba_raw,
                              f32(ba_hi[:]).rearrange("p l k n -> p (l k n)"), ALU.subtract).then_inc(small_lo, 1)
            dve.tensor_tensor(rw_lo[:].rearrange("p k n -> p (k n)"), rw_raw,
                              f32(rw_hi[:]).rearrange("p k n -> p (k n)"), ALU.subtract).then_inc(small_lo, 1)
            dve.wait_ge(csil, 1)
            take_upto(u_of[("ada", 0, 11, 1)])

            for l in range(L):
                dve.wait_ge(ada_ps, l + 1)
                dve.tensor_tensor(adac[:, l, :], ps[0][:, 0:48], cols[:, COL_AB + 48 * l:COL_AB + 48 * (l + 1)],
                                  ALU.add).then_inc(ada_s, 1)
                dve.wait_ge(ada_s, l + 1)
                norm(2 * l, m_xn)
                modulate(2 * l, m_tmp)
                ahead(("qkvz", l, 0), 1)
                dve.wait_ge(h_s, 8 * l + 4)
                dve.memset(raw[0][:, :, 0:PAD], 0.0)
                link(dve.memset(raw[1][:, :, 0:PAD], 0.0))
                dve.wait_ge(ba_ps, l + 1)
                dve.tensor_copy(ba[:].rearrange("p t n -> p (t n)"), ps[2][:, 0:16]).then_inc(ba_s, 1)
                dve.wait_ge(ba_s, l + 1)
                link(dve.tensor_tensor(gb[:, 2], ba[:, :, H:2 * H],
                                       wide(head_rows[:, (L + l) * H:(L + l + 1) * H], [P, TB, H], 1), ALU.add))
                dve.scalar_tensor_tensor(gb[:, 3], gb[:, 2], -1.0, gb[:, 2], ALU.mult, ALU.max).then_inc(beta_a, 1)

                for j in range(6):
                    ahead(("qkvz", l, j), 1)
                    dve.wait_ge(raw_s, 6 * l + j + 1)
                    if j >= 2:
                        dve.wait_ge(qkv_s, 8 * l + j - 1)
                    at = [0, 0]
                    for tap in range(CTAPS):
                        for t in range(2):
                            cc = COL_CONV + l * CTAPS * 12 + tap * 12 + 2 * j + t
                            src = raw[j % 2][:, t, tap:tap + T]
                            if tap == 0:
                                ins = dve.tensor_scalar(cv[j % 2][:, t, :], src, cols[:, cc:cc + 1], None, ALU.mult)
                            else:
                                dve.wait_ge(dve_c, at[t])
                                ins = dve.scalar_tensor_tensor(cv[j % 2][:, t, :], src, cols[:, cc:cc + 1],
                                                               cv[j % 2][:, t, :], ALU.mult, ALU.add)
                            if tap == CTAPS - 1 and t == 1:
                                ins.then_inc(conv_s, 1)
                            else:
                                at[t] = mark(ins)
                ahead(("swkv", l), 1)

                dve.wait_ge(rinv_s, l + 1)
                dve.scalar_tensor_tensor(qT, qT, float(DK) ** -0.5, rinv[:, 0:4, :], ALU.mult, ALU.mult)
                dve.tensor_tensor(kT, kT, rinv[:, 4:8, :], ALU.mult).then_inc(qkn_s, 1)
                dve.wait_ge(beta_e, l + 1)
                link(dve.tensor_scalar(gb[:, 0], gb[:, 0], 1.0, None, ALU.add))
                dve.reciprocal(gb[:, 1], gb[:, 0])
                link(dve.scalar_tensor_tensor(gb[:, 2], gb[:, 2], 0.0, gb[:, 4], ALU.max, ALU.add))
                link(dve.scalar_tensor_tensor(gb[:, 5], gb[:, 2], -1.0,
                                              wide(head_rows[:, (2 * L + l) * H:(2 * L + l + 1) * H], [P, TB, H], 1),
                                              ALU.mult, ALU.mult))
                dve.wait_ge(rot_s, l + 1)
                dve.wait_ge(qkn_s, l + 1)
                for rows, mask, src in ((g_rows[0], ident, 1), (g_rows[1], after_blk, 5), (g_rows[2], incl_blk, 5)):
                    for tb in range(TB):
                        ins = dve.tensor_tensor(rows[:, tb, :].rearrange("p (h c) -> p h c", h=H),
                                                wide(mask[:], [P, H, P], 1),
                                                wide(gb[:, src, tb, :], [P, H, P], 2), ALU.mult)
                ins.then_inc(grow_s, 1)

                for tb in range(TB):
                    keys, per = P * (tb + 1), 4 // (tb + 1)
                    am = (am0, am1)[tb]
                    for n in range(NQH // per):
                        t = T_SCORE[tb] + n
                        dve.wait_ge(att_ps, NTASK * l + t + 1)
                        dve.scalar_tensor_tensor(a_s[:, n * per:(n + 1) * per, 0:keys],
                                                 ps[t % 4][:].rearrange("p (h k) -> p h k", h=per), float(DH) ** -0.5,
                                                 wide(am[:], [P, per, keys], 1), ALU.mult, ALU.add).then_inc(att_d, 1)
                    dve.wait_ge(att_d, NATT_D * l + (2, 8)[tb])
                    link(dve.tensor_reduce(smax[:, 0, :], a_s[:, :, 0:keys], AX.X, ALU.max))
                    link(dve.tensor_tensor(smax[:, 1, :], smax[:, 0, :], sink_rows[:, l, :], ALU.max))
                    dve.tensor_tensor(smax[:, 3, :], sink_rows[:, l, :], smax[:, 1, :], ALU.subtract)
                    dve.tensor_scalar(smax[:, 0, :], smax[:, 1, :], -1.0, None, ALU.mult).then_inc(mx_s, 1)
                    dve.wait_ge(pe_s, TB * l + tb + 1)
                    link(dve.tensor_tensor(smax[:, 1, :], smax[:, 2, :], smax[:, 3, :], ALU.add))
                    link(dve.reciprocal(smax[:, 2, :], smax[:, 1, :]))
                    dve.tensor_tensor(a_s[:, :, 0:keys], a_s[:, :, 0:keys],
                                      wide(smax[:, 2, :], [P, NQH, keys], 2), ALU.mult).then_inc(pn_s, 1)
                    for g in range(G):
                        rows = slice(g * DH, (g + 1) * DH)
                        dve.wait_ge(obh_s, 4 * l + 2 * tb + g + 1)
                        dve.tensor_tensor(ob_lo[rows, :, tb * P:(tb + 1) * P],
                                          ps[(T_PV[tb] + g) % 4][rows, :].rearrange("p (j q) -> p j q", j=J),
                                          f32(ob_hi[rows, :, tb * P:(tb + 1) * P]), ALU.subtract).then_inc(att_d, 1)

                dve.wait_ge(maps, 4 * l + 1)
                for tb in range(TB):
                    here = slice(tb * P, (tb + 1) * P)
                    beta = ps[4 + tb][:].rearrange("p (h c) -> p h c", h=H)
                    dve.tensor_tensor(KB[:, :, here], kT[:, :, here], beta, ALU.mult)
                    dve.tensor_tensor(vT[:, :, here], vT[:, :, here], beta, ALU.mult).then_inc(kb_s, 1)
                dve.wait_ge(exps_s, 6 * l + 6)
                link(dve.tensor_tensor(XT, X, wide(before_blk[:], [P, TB * H, P], 1), ALU.mult))
                link(dve.tensor_tensor(X, X, wide(incl_blk[:], [P, TB * H, P], 1), ALU.mult))
                for n, (dst, decay) in enumerate(((LT, XT), (AT, X))):
                    dve.wait_ge(lat, 2 * l + n + 1)
                    for tb in range(TB):
                        heads = slice(tb * H, (tb + 1) * H)
                        ins = dve.tensor_tensor(dst[:, heads, :], ps[4 + 2 * n + tb][:].rearrange("p (h c) -> p h c", h=H),
                                                decay[:, heads, :], ALU.mult)
                    ins.then_inc(lat_s, 1)
                dve.tensor_tensor(kT, kT, ED, ALU.mult)
                dve.tensor_tensor(KB, KB, EG, ALU.mult)
                dve.tensor_copy(egl[:], EG.rearrange("p h (n c) -> p h n c", c=CHUNK)[:, :, :, CHUNK - 1])
                dve.tensor_tensor(qT, qT, EG, ALU.mult).then_inc(kgb_s, 1)
                dve.wait_ge(l0_ps, l + 1)
                for tb in range(TB):
                    ins = dve.tensor_tensor(U[:, tb * H:(tb + 1) * H, :],
                                            ps[6 + tb][:].rearrange("p (h c) -> p h c", h=H),
                                            wide(lev_mask[:, 0, :], [P, H, P], 1), ALU.mult)
                link(ins)
                eye = wide(ident[:], [P, TB * H, P], 1)
                link(dve.tensor_tensor(X, eye, U, ALU.subtract))
                link(dve.tensor_tensor(U, LT, wide(lev_mask[:, 6, :], [P, TB * H, P], 1), ALU.mult))
                dve.tensor_tensor(XT, eye, U, ALU.subtract).then_inc(inv0, 1)
                for lev in range(1, 6):
                    ahead(("gate", l, lev - 1), 1)
                    for tb in range(TB):
                        heads = slice(tb * H, (tb + 1) * H)
                        dve.wait_ge(u_ps, 10 * l + 2 * (lev - 1) + tb + 1)
                        if lev > 1:
                            dve.wait_ge(xu_ps, 10 * l + 2 * (lev - 2) + tb + 1)
                        dve.tensor_tensor(U[:, heads, :], ps[4 + tb][:].rearrange("p (h c) -> p h c", h=H),
                                          wide(lev_mask[:, lev, :], [P, H, P], 1), ALU.mult).then_inc(u_s, 1)
                    for tb in range(TB):
                        heads = slice(tb * H, (tb + 1) * H)
                        dve.wait_ge(xu_ps, 10 * l + 2 * (lev - 1) + tb + 1)
                        if lev < 5:
                            dve.tensor_tensor(X[:, heads, :], X[:, heads, :],
                                              ps[6 + tb][:].rearrange("p (h c) -> p h c", h=H), ALU.subtract)
                        dve.tensor_tensor(XT[:, heads, :], XT[:, heads, :],
                                          ps[2 + tb][:].rearrange("p (h c) -> p h c", h=H),
                                          ALU.subtract).then_inc(xx_s, 1)

                for n in range(NCH):
                    tb, par = divmod(n, 2)
                    rows = slice(par * CHUNK, (par + 1) * CHUNK)
                    if n:
                        dve.wait_ge(ks_ps, 3 * l + n)
                        dve.tensor_tensor(resid[rows].rearrange("p h d -> p (h d)"),
                                          v_tok[rows, tb].rearrange("p h d -> p (h d)"), ps[4][rows, :],
                                          ALU.subtract).then_inc(res_s, 1)
                    if n < NCH - 1:
                        ahead(("gate", l, 5 + n), 0)
                        dve.wait_ge(su_ps, 3 * l + n + 1)
                        if n == 0:
                            dve.tensor_copy(state.rearrange("p h d -> p (h d)"), ps[6][:]).then_inc(st_s, 1)
                        else:
                            dve.wait_ge(st_s, 3 * l + n)
                            for h in range(H):
                                ins = dve.scalar_tensor_tensor(state[:, h, :], state[:, h, :], egl[:, h, n:n + 1],
                                                               ps[6][:, h * P:(h + 1) * P], ALU.mult, ALU.add)
                            ins.then_inc(st_s, 1)
                ahead(("wa", l, 1), 0)
                dve.wait_ge(on_s, l + 1)
                gn = cols[:, COL_GN + l:COL_GN + l + 1]
                link(dve.scalar_tensor_tensor(OT, OT, gn, o_r, ALU.mult, ALU.mult))
                dve.tensor_tensor(OT, OT, zT, ALU.mult).then_inc(oaf, 1)
                dve.wait_ge(oa_h, l + 1)
                dve.tensor_tensor(oa_lo[:], OT, f32(oa_hi[:]), ALU.subtract).then_inc(oa_s, 1)

                dve.wait_ge(gate_s, 8 * (l + 1))
                for br in range(2):
                    for cc in range(2):
                        product((("wa", "wb")[br], l, cc), 1)
                        for n in range(2):
                            got = ps[4 * br + 2 * cc + n][:].rearrange("p (a b) -> p a b", a=2)
                            gate = gate_sb[:, 8 * br + 4 * cc + 2 * n:8 * br + 4 * cc + 2 * n + 2, :]
                            to = (y_tmp[:, 2 * n:2 * n + 2, :] if br
                                  else y_sum[:, 4 * cc + 2 * n:4 * cc + 2 * n + 2, :])
                            ins = dve.tensor_tensor(to, got, gate, ALU.mult)
                        if br:
                            link(ins)
                            half = y_sum[:, 4 * cc:4 * cc + 4, :]
                            ins = dve.tensor_tensor(half, half, y_tmp, ALU.add)
                        ins.then_inc(yb_s, 1)
                    if br == 0:
                        dve.wait_ge(yb_s, 4 * l + 2)
                for cc in range(2):
                    dve.wait_ge(y_hi_s, 2 * l + cc + 1)
                    half = slice(4 * cc, 4 * cc + 4)
                    dve.tensor_tensor(hT_lo[:, half, :], y_sum[:, half, :], f32(hT_hi[:, half, :]),
                                      ALU.subtract).then_inc(y_s, 1)
                gate_diag(2 * l + 1, l, 2, m_dg)
                gate_copy(2 * l + 1, m_gt, (4, 5))
                for cc in range(2):
                    product(("mix", l, cc, 1), 1)
                    cs = slice(cc * 512, (cc + 1) * 512)
                    for tb in range(TB):
                        ins = dve.tensor_tensor(m_xt[:, tb, :], ps[2 * cc + tb][:], m_gt[:, cs], ALU.mult)
                    link(ins)
                    for tb in range(TB):
                        dve.tensor_tensor(xs[:, tb, cs], xs[:, tb, cs], m_xt[:, tb, :], ALU.add).then_inc(mix_s, 1)
                dve.wait_ge(mix_s, 4 * (l + 1))

                if l == 0:
                    norm(1, f_xn)
                    modulate(1, f_tmp)
                    for i in range(2 * FC):
                        ahead(("fg", i), 1)
                        dve.wait_ge(fs_s, i + 1)
                        product(("fu", i), 1)
                        if i:
                            dve.wait_ge(fhh_s, i)
                        dve.tensor_tensor(f_h[:].rearrange("p a b -> p (a b)"), f_g[i % 2][:].rearrange("p a b -> p (a b)"),
                                          ps[2 * (i % 2) + 1][:], ALU.mult).then_inc(fh_s, 1)
                        dve.wait_ge(fhh_s, i + 1)
                        dve.tensor_tensor(f_lo[i % 2][:], f_h[:], f32(f_hi[i % 2][:]), ALU.subtract).then_inc(fhl_s, 1)
                    gate_diag(2, 0, 5, f_dg[:])
                    product(("fd", 2 * FC - 1), 1)
                    gate_copy(2, f_gt, (0, 1))
                    for tb in range(TB):
                        for hf in range(2):
                            cs = slice(hf * 512, (hf + 1) * 512)
                            ins = dve.tensor_tensor(f_xn[:, tb, cs], ps[4 + 2 * tb + hf][:], f_gt[:, cs], ALU.mult)
                            if hf == 1:
                                link(ins)
                        ins = dve.tensor_tensor(xs[:, tb, :], xs[:, tb, :], f_xn[:, tb, :], ALU.add)
                        if tb == TB - 1:
                            ins.then_inc(xf_s, 1)
                    dve.wait_ge(xf_s, 1)

            norm(3, e_xn)
            modulate(3, e_tmp)
            by_tok = [P, TB, E]
            dve.wait_ge(logit_ps, 1)
            link(dve.tensor_tensor(lg[:, 0], ps[2][:, 0:TB * E].rearrange("p (t e) -> p t e", t=TB),
                                   wide(rb_row[:], by_tok, 1), ALU.add))
            dve.wait_ge(logit_ps, 2)
            link(dve.tensor_copy(slots[:], ps[3][:, 0:P]))
            link(dve.tensor_scalar(rsm[:, 0, :], slots[:, 0:E], -1.0, float(E), ALU.mult, ALU.add))

            def first_max(src, top, dst):
                link(dve.tensor_reduce(top, src, AX.X, ALU.max))
                link(dve.tensor_tensor(lg[:, 1], src, top.to_broadcast(by_tok), ALU.is_equal))
                link(dve.tensor_tensor(lg[:, 1], lg[:, 1], wide(rsm[:, 0, :], by_tok, 1), ALU.mult))
                link(dve.tensor_reduce(lg[:, 10, :, 0:1], lg[:, 1], AX.X, ALU.max))
                link(dve.tensor_tensor(dst, lg[:, 1], lg[:, 10, :, 0:1].to_broadcast(by_tok), ALU.is_equal))

            top1, top2 = lg[:, 5, :, 0:1], lg[:, 11, :, 0:1]
            first_max(lg[:, 0], top1, lg[:, 2])
            link(dve.scalar_tensor_tensor(lg[:, 3], lg[:, 2], NEG, lg[:, 0], ALU.mult, ALU.add))
            first_max(lg[:, 3], top2, lg[:, 4])
            dve.tensor_tensor(lg[:, 6], lg[:, 2], lg[:, 4], ALU.add).then_inc(sel_s, 1)
            dve.tensor_tensor(lg[:, 8, :, 0:1], top2, top1, ALU.subtract).then_inc(lg_s, 1)
            dve.wait_ge(lge_s, 1)
            link(dve.tensor_scalar(lg[:, 9, :, 0:1], lg[:, 8, :, 0:1], 1.0, None, ALU.add))
            link(dve.reciprocal(lg[:, 9, :, 1:2], lg[:, 9, :, 0:1]))
            link(dve.tensor_tensor(lg[:, 9, :, 2:3], lg[:, 9, :, 1:2], lg[:, 8, :, 0:1], ALU.mult))
            dve.tensor_tensor(lg[:, 1], lg[:, 2], lg[:, 9, :, 1:2].to_broadcast(by_tok), ALU.mult)
            link(dve.tensor_tensor(lg[:, 3], lg[:, 4], lg[:, 9, :, 2:3].to_broadcast(by_tok), ALU.mult))
            dve.wait_ge(upper_s, 1)
            link(dve.tensor_tensor(wt_of[:, :, 0:E], lg[:, 1], lg[:, 3], ALU.add))
            dve.wait_ge(sel_s, 1)
            dve.wait_ge(pos_ps, 1)
            link(dve.scalar_tensor_tensor(lg[:, 1], ps[5][:, 0:TB * E].rearrange("p (t e) -> p t e", t=TB), 1.0,
                                          lg[:, 6], ALU.add, ALU.mult))
            link(dve.tensor_scalar(slot_of[:, :, 0:E], lg[:, 1], -1.0, None, ALU.add))
            link(dve.tensor_copy(rsm[:, 1, :], ps[5][:, 2 * E:3 * E]))
            link(dve.tensor_scalar(rsm[:, 2, :], rsm[:, 1, :], float(P), None, ALU.is_gt))
            link(dve.memset(rsm[:, 3, :], 0.0))
            for e in range(E - 1):
                link(dve.tensor_tensor(rsm[:, 3, e + 1:e + 2], rsm[:, 3, e:e + 1], rsm[:, 2, e:e + 1], ALU.add))
            link(dve.scalar_tensor_tensor(metaf[:, 0:1], rsm[:, 3, E - 1:E], float(E), rsm[:, 2, E - 1:E],
                                          ALU.add, ALU.add))
            for j in range(3):
                one = rsm[:, 4 + j, :]
                link(dve.scalar_tensor_tensor(one, rsm[:, 3, :], float(j), rsm[:, 2, :], ALU.is_equal, ALU.mult))
                link(dve.tensor_tensor(rsm[:, 7 + j, :], one, slots[:, 0:E], ALU.mult))
                link(dve.tensor_reduce(metaf[:, 1 + j:2 + j], rsm[:, 7 + j, :], AX.X, ALU.add))
                link(dve.scalar_tensor_tensor(lg[:, 1], slot_of[:, :, 0:E], -float(P), wide(one, by_tok, 1),
                                              ALU.add, ALU.mult))
                link(dve.tensor_reduce(slot_of[:, :, E + j:E + j + 1], lg[:, 1], AX.X, ALU.add))
                link(dve.tensor_tensor(lg[:, 3], wt_of[:, :, 0:E], wide(one, by_tok, 1), ALU.mult))
                link(dve.tensor_reduce(wt_of[:, :, E + j:E + j + 1], lg[:, 3], AX.X, ALU.add))
            dve.tensor_copy(meta[:], metaf[:]).then_inc(route_s, 1)

            def perm(item, n):
                dve.tensor_copy(cur[:, 0, :].unsqueeze(2), slot_of[:, :, bass.ds(item, 1)]).then_inc(cur_s, 1)
                dve.wait_ge(cur_s, n)
                for tb in range(TB):
                    ins = dve.tensor_scalar(e_p[:, tb, :], slots[:], cur[:, 0, tb:tb + 1], None, ALU.is_equal)
                ins.then_inc(p_s, 1)

            def weighted_perm(item, n):
                dve.tensor_copy(cur[:, 1, :].unsqueeze(2), slot_of[:, :, bass.ds(item, 1)])
                dve.tensor_copy(cur[:, 2, :].unsqueeze(2), wt_of[:, :, bass.ds(item, 1)]).then_inc(cur_s, 1)
                dve.wait_ge(cur_s, n)
                for tb in range(TB):
                    ins = dve.tensor_scalar(e_pw[:, tb, :], slots[:], cur[:, 1, tb:tb + 1], cur[:, 2, tb:tb + 1],
                                            ALU.is_equal, ALU.mult)
                ins.then_inc(pw_s, 1)

            def gathered(piece, n):
                dve.wait_ge(ga_ps, n)
                for k in range(4):
                    ko = 4 * piece + k
                    ins = dve.tensor_scalar(e_xf[:, ko, :], ps[5][:, k * P:(k + 1) * P], wsc[:, ko:ko + 1],
                                            adac[:, 1, 3 * KO + ko:3 * KO + ko + 1], ALU.mult, ALU.add)
                ins.then_inc(ga_s, 1)

            def gathered_low(n):
                dve.wait_ge(xgh_s, n)
                dve.tensor_tensor(xg_lo[:], e_xf[:], f32(xg_hi[:]), ALU.subtract).then_inc(xg_s, 1)

            def combined(i, k):
                tb, hf = divmod(k, 2)
                cs = slice(hf * 512, (hf + 1) * 512)
                dve.wait_ge(cb_ps, 4 * i + (k + 2))
                dve.tensor_tensor(e_acc[:, tb, cs], e_acc[:, tb, cs], ps[5][:], ALU.add).then_inc(cb_s, 1)

            for n, started in enumerate((mh_s, mhl_s, cb_s)):
                dve.memset(stat[:, 10 + n:11 + n], 0.0).then_inc(started, 1)
            perm(0, 1)
            gathered(0, 1)
            gathered(1, 2)
            gathered_low(1)
            dve.wait_ge(route_s, 1)
            n_items = dve.value_load(meta[0:1, 0:1], min_val=E, max_val=E + 3)
            with dve.Fori(0, n_items) as i:
                def low(p):
                    dve.wait_ge(hi_ready, MU * i + (S0 + p + 1))
                    dve.tensor_tensor(w_lo[p % NS_MOE][:], ring[:, p % RING, :], f32(w_hi[p % NS_MOE][:]),
                                      ALU.subtract).then_inc(taken, 1)

                low(0)
                low(1)
                for p, (kind, fc, half) in enumerate(moe_units):
                    if p + 2 < MU:
                        low(p + 2)
                    if p < 4:
                        combined(i, p)
                    if p == mp[("g", 1, 0)]:
                        weighted_perm(i, 2 * i + 2)
                    if p == mp[("g", 3, 0)]:
                        dve.wait_ge(ga_ps, 2 * i + 2)
                        perm(i + 1, 2 * i + 3)
                    if kind == "u" and half == 1:
                        dve.wait_ge(ms_s, FC * i + (fc + 2))
                        dve.wait_ge(split_used, MU * i + (S0 + p + 1))
                        dve.wait_ge(mt_ps, FC * i + max(fc, 1))
                        dve.tensor_tensor(e_h[fc % 2][:], e_g[fc % 2][:], ps[2 * (fc % 2) + 1][:],
                                          ALU.mult).then_inc(mh_s, 1)
                    f = turned_after.get(p)
                    if f is not None:
                        dve.wait_ge(mhh_s, FC * i + (f + 1))
                        dve.tensor_tensor(h_lo[f % 2][:].rearrange("p a b -> p (a b)"), ps[4][:],
                                          f32(h_hi[f % 2][:]).rearrange("p a b -> p (a b)"),
                                          ALU.subtract).then_inc(mhl_s, 1)
                    if p == mp[("g", 2, 0)]:
                        dve.wait_ge(pwt_ps, i + 1)
                        dve.tensor_copy(e_pwT[:], ps[5][:, 0:T]).then_inc(pwt_s, 1)
                    if p == mp[("g", 4, 0)]:
                        gathered(0, 2 * i + 3)
                    if p == mp[("g", 4, 1)]:
                        gathered(1, 2 * i + 4)
                    if (kind, fc, half) == ("d", FC - 2, 1):
                        gathered_low(i + 2)
            for k in range(4):
                combined(n_items, k)
            gate_diag(4, 1, 5, e_dg[:])
            gate_copy(4, e_gt, (0, 1))
            dve.wait_ge(cb_s, 4 * n_items + 5)
            link(dve.tensor_tensor(e_acc[:], e_acc[:], wide(e_gt[:], [P, TB, D], 1), ALU.mult))
            dve.tensor_tensor(xs[:], xs[:], e_acc[:], ALU.add).then_inc(xf_s, 1)
            dve.wait_ge(xf_s, 2)
            dve.wait_ge(rstd_s, 5)
            link(dve.reciprocal(stat[:, 4:6], stat[:, 2:4]))
            dve.wait_ge(fin_s, 16)
            for tb in range(TB):
                ins = dve.scalar_tensor_tensor(e_acc[:, tb, :], xs[:, tb, :], stat[:, 4 + tb:5 + tb], fw_row[:],
                                               ALU.mult, ALU.mult)
            ins.then_inc(out_s, 1)


INPUTS = ["x", "c", "positions", "ada_w", "ada_b", "norm_mix_w", "norm_ffn_w", "w_in", "conv_w", "a_log",
          "dt_bias", "gdn_norm_w", "sinks", "w_a_out", "w_b_out", "w_mix_out", "ffn_w_gate", "ffn_w_up",
          "ffn_w_down", "router_w", "router_b", "moe_w_gate", "moe_w_up", "moe_w_down", "final_norm_w"]


def kernel(**inputs):
    import concourse.bacc as bacc
    from concourse.bass_utils import run_bass_kernel_spmd

    nc = bacc.Bacc("TRN2", target_bir_lowering=False, num_devices=1)
    arrays, args = {}, []
    for name in INPUTS:
        a = np.ascontiguousarray(inputs[name])
        arrays[f"in_{name}_dram"] = a
        args.append(nc.dram_tensor(f"in_{name}_dram", a.shape, mybir.dt.from_np(a.dtype),
                                   kind="ExternalInput").ap())
    shape = tuple(inputs["x"].shape)
    args.append(nc.dram_tensor("out_dram", shape, F32, kind="ExternalOutput").ap())
    build_program(nc, *args)
    result = run_bass_kernel_spmd(nc, [arrays], core_ids=[0])
    return result.results[0]["out_dram"]
```

```python
import math
from contextlib import ExitStack

import numpy as np

import concourse.bass as bass
from concourse import mybir

F32 = mybir.dt.float32
F32R = mybir.dt.float32r
BF16 = mybir.dt.bfloat16
I32 = mybir.dt.int32
ALU = mybir.AluOpType
ACT = mybir.ActivationFunctionType
AX = mybir.AxisListType

P = 128
EPS = 1e-6
NEG = -1e30
CHUNK = 64
ROPE_THETA = 500000.0


def build_program(nc, x, c, positions, ada_w, ada_b, norm_mix_w, norm_ffn_w, w_in, conv_w, a_log,
                  dt_bias, gdn_norm_w, sinks, w_a_out, w_b_out, w_mix_out, ffn_w_gate, ffn_w_up,
                  ffn_w_down, router_w, router_b, moe_w_gate, moe_w_up, moe_w_down, final_norm_w, out):
    D = x.shape[2]
    T = x.shape[1]
    L = ada_w.shape[0]
    KO = D // P
    TB = T // P
    NCH = T // CHUNK
    H = a_log.shape[1]
    DK = P
    NQH = sinks.shape[1]
    DH = CHUNK
    G = 2
    J = NQH // G
    F = ffn_w_gate.shape[2]
    E = moe_w_gate.shape[1]
    FC = F // 512
    ROT = DH // 4
    HALF = ROT // 2
    C_SWA = 4 * H * DK + 2 * H
    C_GATE = C_SWA + NQH * DH + 2 * G * DH
    C_BA = 4 * H * DK
    CTAPS = conv_w.shape[1]
    assert (D, T, L, H, NQH, E) == (1024, 256, 2, 4, 8, 8) and F % 512 == 0
    PAD = CTAPS - 1
    RAWW = T + PAD

    RING = 6
    UW = 2048
    units = []
    NQ, NQA = 12, 4
    for q in range(NQA):
        for kh in range(2):
            units.append((("ada", 0, q, kh), False))
    ada0 = [("ada", 0, q, kh) for q in range(NQA, NQ) for kh in range(2)]

    def ada_units(n):
        for _ in range(n):
            units.append((ada0.pop(0), False))

    def mixer_units(l):
        for j in range(6):
            units.append((("qkvz", l, j), True))
        for kh in range(2):
            units.append((("swq", l, kh), True))
        units.append((("swkv", l), True))
        for j in (6, 7):
            units.append((("qkvz", l, j), True))
        if l == 0:
            ada_units(3)
        for j in range(8):
            units.append((("gate", l, j), True))
            if l == 0:
                ada_units(1 if j < 3 else 2)
        for cc in range(2):
            units.append((("wb", l, cc), True))
        for cc in range(2):
            units.append((("wa", l, cc), True))
        for kh in range(2):
            for cc in range(2):
                units.append((("mix", l, cc, kh), True))

    mixer_units(0)
    ada1 = [("ada", 1, q, kh) for q in range(NQ) for kh in range(2)]
    for i in range(2 * FC):
        units.append((("fg", i), True))
        if ada1:
            units.append((ada1.pop(0), False))
        units.append((("fu", i), True))
        if ada1:
            units.append((ada1.pop(0), False))
        if i > 0:
            units.append((("fd", i - 1), True))
    units.append((("fd", 2 * FC - 1), True))
    mixer_units(1)
    u_of = {k: n for n, (k, _) in enumerate(units)}
    split_keys = [k for k, pe_ in units if pe_]
    s_of = {k: n for n, k in enumerate(split_keys)}
    U0, S0 = len(units), len(split_keys)
    MU = 6 * FC
    NS_MIX, NS_FFN, NS_MOE = 2, 3, 3
    buf_of, free_at, last_in, n_ffn = [], [], {}, 0
    for s, k in enumerate(split_keys):
        if k[0] in ("fg", "fu", "fd"):
            if n_ffn == 0:
                last_in[2] = split_keys.index(("wa", 0, 1))
            b, n_ffn = (2 - n_ffn) % NS_FFN, n_ffn + 1
        else:
            b = s % NS_MIX
        buf_of.append(b)
        free_at.append(last_in[b] + 1 if b in last_in else None)
        last_in[b] = s
    assert not ada1 and U0 % RING == 0 and MU % RING == 0 and S0 % NS_MOE == 0 and MU % NS_MOE == 0
    moe_units = []
    for fc in range(FC):
        moe_units += [("g", fc, 0), ("g", fc, 1), ("u", fc, 0), ("u", fc, 1)]
        if fc > 0:
            moe_units += [("d", fc - 1, 0), ("d", fc - 1, 1)]
    moe_units += [("d", FC - 1, 0), ("d", FC - 1, 1)]
    mp = {k: n for n, k in enumerate(moe_units)}
    assert len(moe_units) == MU
    turned_after = {(mp[("d", f - 1, 0)] if f else mp[("g", 1, 0)]): f for f in range(FC)}

    def k_rows(ap):
        return ap.rearrange("(k p) n -> p k n", p=P)

    def unit_dram(key):
        kind, l = key[0], key[1]
        if kind == "ada":
            q, kh = key[2:]
            return k_rows(ada_w[l, kh * 512:(kh + 1) * 512, q * 512:(q + 1) * 512]), 4
        if kind == "qkvz":
            return k_rows(w_in[l, :, key[2] * 256:(key[2] + 1) * 256]), 8
        if kind == "swq":
            return k_rows(w_in[l, key[2] * 512:(key[2] + 1) * 512, C_SWA:C_SWA + 512]), 4
        if kind == "swkv":
            return k_rows(w_in[l, :, C_SWA + 512:C_SWA + 768]), 8
        if kind == "gate":
            return k_rows(w_in[l, :, C_GATE + key[2] * 256:C_GATE + (key[2] + 1) * 256]), 8
        if kind == "wa":
            return k_rows(w_a_out[l, :, key[2] * 512:(key[2] + 1) * 512]), 4
        if kind == "mix":
            cc, kh = key[2:]
            return k_rows(w_mix_out[l, kh * 512:(kh + 1) * 512, cc * 512:(cc + 1) * 512]), 4
        if kind in ("fg", "fu"):
            w = ffn_w_gate if kind == "fg" else ffn_w_up
            return k_rows(w[0, :, l * 256:(l + 1) * 256]), 8
        assert kind == "fd"
        return k_rows(ffn_w_down[0, l * 256:(l + 1) * 256, :]), 2

    ctx = ExitStack()
    with ctx:
        def sb(name, shape, dt=F32, where=ctx):
            return where.enter_context(nc.sbuf_tensor(name, shape, dt))

        def sem(name):
            return ctx.enter_context(nc.semaphore(name))

        ps = [ctx.enter_context(nc.psum_tensor(f"bank{b}", [P, 512], F32)) for b in range(8)]

        ring = sb("ring", [P, RING, UW])
        w_hi = [sb(f"w_hi{i}", [P, UW], F32R) for i in range(NS_MIX)]
        w_lo = [sb(f"w_lo{i}", [P, UW], F32R) for i in range(NS_MIX)]
        xs = sb("xs", [P, TB, D])
        hT_hi = sb("hT_hi", [P, KO, T], F32R)
        hT_lo = sb("hT_lo", [P, KO, T], F32R)
        ident = sb("ident", [P, P])
        ones = sb("ones", [P, P])
        incl_blk = sb("incl_blk", [P, P])
        after_blk = sb("after_blk", [P, P])
        before_blk = sb("before_blk", [P, P])
        lev_mask = sb("lev_mask", [P, 7, P], BF16)
        am0 = sb("am0", [P, P], BF16)
        am1 = sb("am1", [P, 2 * P], BF16)
        cols = sb("cols", [P, 2 * P])
        c_silu = sb("c_silu", [P, KO])
        ada_acc = sb("ada_acc", [P, 2, 512])
        ada_rows = sb("ada_rows", [P, 512])
        pick = sb("pick", [P, 2 * NQ - 1])
        adac = sb("adac", [P, L, 48])
        wsc = sb("wsc", [P, KO])
        eps_c = sb("eps_c", [P, 1])
        one_c = sb("one_c", [P, 1])
        w_ba = sb("w_ba", [P, L, KO, 2 * H])
        w_router = sb("w_router", [P, KO, E])
        head_rows = sb("head_rows", [P, 3 * L * H])
        sink_rows = sb("sink_rows", [P, L, NQH])
        rb_row = sb("rb_row", [P, E])
        rope = sb("rope", [P, TB, 2, HALF])
        stat = sb("stat", [P, 16])
        ba = sb("ba", [P, TB, 8])
        gb = sb("gb", [P, 6, TB, H])
        egl = sb("egl", [P, H, NCH])
        smax = sb("smax", [P, TB, 4, NQH])
        lev_f = sb("lev_f", [P, P])
        meta = sb("meta", [P, 4], I32)

        gm = ExitStack()
        oa_hi = sb("oa_hi", [P, H, T], F32R, gm)
        oa_lo = sb("oa_lo", [P, H, T], F32R, gm)
        ob_hi = sb("ob_hi", [P, J, T], F32R, gm)
        ob_lo = sb("ob_lo", [P, J, T], F32R, gm)
        work = sb("work", [P, 17152], F32, gm)
        gm.close()

        def wk(at, *shape):
            n = int(np.prod(shape))
            v = work[:, at:at + n]
            if len(shape) == 2:
                return v.rearrange("p (a b) -> p a b", a=shape[0])
            if len(shape) == 3:
                return v.rearrange("p (a b c) -> p a b c", a=shape[0], b=shape[1])
            return v

        m_xn = wk(0, TB, D)
        m_tmp = wk(8192, KO, T)
        ba_rows = wk(10240, T)
        prm_a = wk(14400, P)
        prm_b = wk(14528, P)
        pos_i = wk(14848, 2 * TB)[:, 0:TB].bitcast(I32)
        ang = wk(14860, 6, TB * 2 * HALF)
        invf = wk(15060, 2 * HALF)
        qkv = wk(0, 16, T)
        qT, kT, vT, zT = (qkv[:, 4 * i:4 * i + 4, :] for i in range(4))
        raw = [wk(4096 + i * 2 * RAWW, 2, RAWW) for i in range(2)]
        cv = [wk(5200 + i * 512, 2, T) for i in range(2)]
        sq = [wk(6256 + i * 512, 512) for i in range(2)]
        gate_sb = wk(4096, 16, T)
        a_s = (wk(13056, NQH, P), wk(4096, NQH, 2 * P))
        a_pt = wk(6144, 16, P)
        a_qk = wk(8192, TB, 10, DH)
        a_v = wk(10752, TB, P)
        a_qT = wk(9728, J, T)
        a_kT = wk(9472, T)
        a_rt = wk(14080, 4, TB * 10 * HALF)
        rinv = wk(15104, 8, T)
        KB = wk(11008, H, T)
        EG = wk(12032, H, T)
        ED = wk(13056, H, T)
        g_rows = [wk(14080, TB, 512), wk(15104, TB, 512), wk(16128, TB, 512)]
        LT = wk(14080, TB * H, P)
        AT = wk(15104, TB * H, P)
        U = wk(16128, TB * H, P)
        X = wk(8192, TB * H, P)
        XT = wk(9216, TB * H, P)
        v_tok = wk(12032, TB, H, P)
        k_tok = wk(13056, TB, H, P)
        states = [wk(14080, H, P), wk(16640, H, P)]
        resid = wk(14592, H, P)
        v_new = wk(16128, H, P)
        OT = wk(8192, H, T)
        o_sq = wk(11008, H, T)
        o_r = wk(9216, H, T)
        y_sum = wk(0, KO, T)
        y_tmp = wk(11008, 4, T)
        m_gt = wk(12032, D)
        m_dg = wk(14080, KO, P)
        m_xt = wk(13056, 4, 512)

        w_hi.append(sb("w_hi2", [P, UW], F32R))
        w_lo.append(sb("w_lo2", [P, UW], F32R))
        gf = ExitStack()
        f_xn = sb("f_xn", [P, TB, D], F32, gf)
        f_tmp = sb("f_tmp", [P, KO, T], F32, gf)
        f_hi = [sb(f"f_hi{i}", [P, 2, T], F32R, gf) for i in range(2)]
        f_lo = [sb(f"f_lo{i}", [P, 2, T], F32R, gf) for i in range(2)]
        f_g = [sb(f"f_g{i}", [P, 2, T], F32, gf) for i in range(2)]
        f_h = sb("f_h", [P, 2, T], F32, gf)
        f_gt = sb("f_gt", [P, D], F32, gf)
        f_dg = sb("f_dg", [P, KO, P], F32, gf)
        gf.close()

        ge = ExitStack()
        e_xn = sb("e_xn", [P, TB, D], F32, ge)
        e_tmp = sb("e_tmp", [P, KO, T], F32, ge)
        e_acc = sb("e_acc", [P, TB, D], F32, ge)
        e_xf = sb("e_xf", [P, KO, P], F32, ge)
        xg_hi = sb("xg_hi", [P, KO, P], F32R, ge)
        xg_lo = sb("xg_lo", [P, KO, P], F32R, ge)
        e_g = [sb(f"e_g{i}", [P, 512], F32, ge) for i in range(2)]
        e_h = [sb(f"e_h{i}", [P, 512], F32, ge) for i in range(2)]
        h_hi = [sb(f"h_hi{i}", [P, 4, P], F32R, ge) for i in range(2)]
        h_lo = [sb(f"h_lo{i}", [P, 4, P], F32R, ge) for i in range(2)]
        e_y = sb("e_y", [P, D], F32, ge)
        e_p = sb("e_p", [P, TB, P], F32, ge)
        e_pw = sb("e_pw", [P, TB, P], F32, ge)
        e_pwT = sb("e_pwT", [P, T], F32, ge)
        e_gt = sb("e_gt", [P, D], F32, ge)
        fw_row = sb("fw_row", [P, D], F32, ge)
        upper = sb("upper", [P, P], F32, ge)
        slots = sb("slots", [P, P], F32, ge)
        lg = sb("lg", [P, 12, TB, E], F32, ge)
        rsm = sb("rsm", [P, 24, E], F32, ge)
        slot_of = sb("slot_of", [P, TB, E + 4], F32, ge)
        wt_of = sb("wt_of", [P, TB, E + 4], F32, ge)
        cur = sb("cur", [P, 4, TB], F32, ge)
        metaf = sb("metaf", [P, 4], F32, ge)
        ge.close()

        landed = [sem(f"landed{i}") for i in range(RING)]
        taken = sem("taken")
        hi_ready = sem("hi_ready")
        split_used = sem("split_used")
        x_in = sem("x_in")
        setup_in = sem("setup_in")
        setup_b = sem("setup_b")
        zeroed = sem("zeroed")
        consts = sem("consts")
        pool_c = sem("pool_chain")
        dve_c = sem("dve_chain")
        act_c = sem("act_chain")
        prm_t = sem("params_turned")
        cols_s = sem("cols_ready")
        csil = sem("c_silu_ready")
        rope_pre = sem("rope_angles")
        rope_s = sem("rope_ready")
        ada_used = sem("ada_acc_used")
        ada_sum = sem("ada_rows_in_psum")
        ada_row = sem("ada_rows_ready")
        ada_ps = sem("ada_cols_in_psum")
        ada_s = sem("ada_cols_ready")
        ssq = sem("square_sums")
        rstd_s = sem("rstd_ready")
        xn_s = sem("xn_ready")
        xnT = sem("xn_turned")
        hmod = sem("h_modulated")
        h_hi_s = sem("h_hi_ready")
        h_s = sem("h_ready")
        bar_ps = sem("ba_rows_in_psum")
        bar_s = sem("ba_rows_ready")
        ba_ps = sem("ba_in_psum")
        lgr_s = sem("logit_rows_ready")
        ba_s = sem("ba_copied")
        raw_s = sem("raw_ready")
        conv_s = sem("conv_done")
        qkv_s = sem("qkvz_ready")
        sq_s = sem("qk_squares")
        l2_ps = sem("l2_in_psum")
        rinv_s = sem("rinv_ready")
        qkn_s = sem("qk_normed")
        beta_e = sem("beta_exp")
        beta_a = sem("beta_args")
        grow_s = sem("g_rows_ready")
        maps = sem("maps_in_psum")
        kb_s = sem("kbeta_ready")
        exps_s = sem("exp_maps_ready")
        lat = sem("la_in_psum")
        lat_s = sem("la_ready")
        kgb_s = sem("scaled_qk_ready")
        tok_ps = sem("tok_turned")
        tok_s = sem("tok_ready")
        l0_ps = sem("l_turned")
        inv0 = sem("inverse_started")
        u_ps = sem("u_in_psum")
        u_s = sem("u_ready")
        xu_ps = sem("xu_in_psum")
        xx_s = sem("x_updated")
        ks_ps = sem("ks_in_psum")
        res_s = sem("resid_ready")
        vn_ps = sem("vnew_in_psum")
        vn_s = sem("vnew_ready")
        su_ps = sem("state_update_in_psum")
        st_s = sem("state_ready")
        o_ps = sem("o_in_psum")
        o_s = sem("o_copied")
        osq_s = sem("o_squares")
        on_ps = sem("o_norm_in_psum")
        on_s = sem("o_rinv_ready")
        oaf = sem("oa_ready_f32")
        oa_h = sem("oa_hi_ready")
        oa_s = sem("oa_ready")
        sw_s = sem("swa_copied")
        rot_s = sem("rotated")
        att_ps = sem("attention_in_psum")
        att_a = sem("attention_act_read")
        att_d = sem("attention_dve_read")
        mx_s = sem("row_max_ready")
        pe_s = sem("exp_scores_ready")
        pn_s = sem("probs_ready")
        gate_s = sem("gates_ready")
        obh_s = sem("ob_hi_ready")
        ln_s = sem("qk_logs")
        ln2_s = sem("o_logs")
        xf_s = sem("channel_mixer_added")
        out_s = sem("out_ready")
        upper_s = sem("expert_memory_cleared")
        cur_s = sem("current_slots")
        yb_s = sem("branch_read")
        y_sum_s = sem("y_summed")
        y_hi_s = sem("y_hi_ready")
        y_s = sem("y_ready")
        gtd_s = sem("gate_diag_ready")
        gt_ps = sem("gate_row_in_psum")
        gt_s = sem("gate_row_ready")
        first_ps = sem("first_tokens_in_psum")
        mix_s = sem("mix_added")
        fs_s = sem("ffn_silu")
        fh_s = sem("ffn_hidden")
        fhh_s = sem("ffn_hidden_hi")
        fhl_s = sem("ffn_hidden_lo")
        logit_ps = sem("logits_in_psum")
        lg_s = sem("logits_ready")
        lge_s = sem("logit_exp")
        sel_s = sem("selection_ready")
        pos_ps = sem("positions_in_psum")
        route_s = sem("routing_ready")
        p_s = sem("perm_ready")
        ga_ps = sem("gather_in_psum")
        ga_s = sem("gather_read")
        xgh_s = sem("xg_hi_ready")
        xg_s = sem("xg_ready")
        pw_s = sem("weighted_perm_ready")
        pwt_ps = sem("weighted_perm_turned")
        pwt_s = sem("weighted_perm_T_ready")
        ms_s = sem("expert_silu")
        mh_s = sem("expert_hidden")
        mt_ps = sem("expert_hidden_turned")
        mhh_s = sem("expert_hidden_hi")
        mhl_s = sem("expert_hidden_lo")
        y_c = sem("expert_out_copied")
        cb_ps = sem("combine_in_psum")
        cb_s = sem("combined")
        fin_s = sem("final_rows_ready")
        stored = sem("stored")

        SETUP_IN = 16 * (2 * L + 4)
        SETUP_B = 16 * (7 + TB)
        landed_at, level = [], [0] * RING
        for u, (key, _) in enumerate(units):
            level[u % RING] += 16 * (G if key[0] == "wb" else 1)
            landed_at.append(level[u % RING])
        COL_NM, COL_NF, COL_CONV = 0, L * KO, 2 * L * KO
        COL_AB, COL_C, COL_GN = P, P + L * 48, P + L * 48 + KO

        att_reader = ["a"] * 3 + ["d"] * 6 + ["a"] * 2 + ["d"] * 2 + ["a"] * 4 + ["d"] * 2
        T_SCORE, T_TURN, T_PV = (3, 5), (9, 13), (11, 17)
        NTASK = len(att_reader)
        NATT_A = att_reader.count("a")
        NATT_D = att_reader.count("d")

        def att_freed(eng, l, t):
            r = att_reader[t]
            n = att_reader[:t + 1].count(r) + l * (NATT_A if r == "a" else NATT_D)
            eng.wait_ge(att_a if r == "a" else att_d, n)

        block = ctx.enter_context(nc.Block())

        @block.sync
        def _(sp):
            for l in range(L):
                sp.dma_start(prm_a[COL_NM + l * KO:COL_NM + (l + 1) * KO, :],
                             norm_mix_w[l].rearrange("(r n) -> r n", n=P)).then_inc(setup_in, 16)
                sp.dma_start(prm_a[COL_NF + l * KO:COL_NF + (l + 1) * KO, :],
                             norm_ffn_w[l].rearrange("(r n) -> r n", n=P)).then_inc(setup_in, 16)
            sp.dma_start(prm_a[COL_CONV:P, :],
                         conv_w.rearrange("l j (t n) -> (l j t) n", n=P)).then_inc(setup_in, 16)
            sp.wait_ge(zeroed, 1)
            sp.dma_start(prm_b[0:L * 48, :],
                         ada_b.rearrange("l (t n) -> (l t) n", n=P)).then_inc(setup_in, 16)
            sp.dma_start(prm_b[L * 48:L * 48 + KO, :],
                         c[0].rearrange("(r n) -> r n", n=P)).then_inc(setup_in, 16)
            sp.dma_start(prm_b[L * 48 + KO:L * 48 + KO + L, :], gdn_norm_w).then_inc(setup_in, 16)

            def load(u):
                key = units[u][0]
                if u >= RING:
                    sp.wait_ge(taken, u - RING + 1)
                if key[0] == "wb":
                    dst = ring[:, u % RING, :].rearrange("p (k n) -> p k n", k=4)
                    for g in range(G):
                        src = w_b_out[key[1], g * J * DH:(g + 1) * J * DH,
                                      key[2] * 512:(key[2] + 1) * 512]
                        ins = sp.dma_start(dst[g * DH:(g + 1) * DH],
                                           src.rearrange("(j d) n -> d j n", d=DH))
                        ins.then_inc(landed[u % RING], 16)
                else:
                    src, k = unit_dram(key)
                    dst = ring[:, u % RING, :].rearrange("p (k n) -> p k n", k=k)
                    sp.dma_start(dst, src).then_inc(landed[u % RING], 16)

            for u in range(RING):
                load(u)
                if u == 2:
                    sp.dma_start(xs[:], x[0].rearrange("(b p) d -> p b d", p=P)).then_inc(x_in, 16)
            for tb in range(TB):
                sp.dma_start(pos_i[:, tb:tb + 1],
                             positions[0, tb * P:(tb + 1) * P].unsqueeze(1)).then_inc(setup_b, 16)
            sp.dma_start(head_rows[:, 0:L * H],
                         a_log.rearrange("l h -> (l h)").partition_broadcast(P)).then_inc(setup_b, 16)
            sp.dma_start(head_rows[:, L * H:2 * L * H],
                         dt_bias.rearrange("l h -> (l h)").partition_broadcast(P)).then_inc(setup_b, 16)
            sp.dma_start(sink_rows[:].rearrange("p l h -> p (l h)"),
                         sinks.rearrange("l h -> (l h)").partition_broadcast(P)).then_inc(setup_b, 16)
            sp.dma_start(w_ba[:, 0],
                         k_rows(w_in[0, :, C_BA:C_BA + 8])).then_inc(setup_b, 16)
            sp.dma_start(w_ba[:, 1],
                         k_rows(w_in[1, :, C_BA:C_BA + 8])).then_inc(setup_b, 16)
            sp.dma_start(w_router[:],
                         k_rows(router_w[0])).then_inc(setup_b, 16)
            sp.dma_start(rb_row[:], router_b[0].partition_broadcast(P)).then_inc(setup_b, 16)
            for u in range(RING, U0):
                load(u)

            def expert_loads(item, e):
                for n, (kind, fc, half) in enumerate(moe_units):
                    sp.wait_ge(taken, U0 + n - RING + 1 + item * MU)
                    slot = n % RING
                    if kind == "d":
                        src = moe_w_down[0, e, fc * 512 + half * 256:fc * 512 + (half + 1) * 256, :]
                        k = 2
                    else:
                        w = moe_w_gate if kind == "g" else moe_w_up
                        src = w[0, e, half * 512:(half + 1) * 512, fc * 512:(fc + 1) * 512]
                        k = 4
                    sp.dma_start(ring[:, slot, :].rearrange("p (k n) -> p k n", k=k),
                                 k_rows(src)).then_inc(landed[slot], 16)

            with sp.Fori(0, E) as e:
                expert_loads(e, e)
            sp.wait_ge(route_s, 1)
            n_items = sp.value_load(meta[0:1, 0:1], min_val=E, max_val=E + 3)
            with sp.If(n_items > E):
                with sp.Fori(E, n_items) as item:
                    e = sp.value_load(meta[0:1, bass.ds(item - (E - 1), 1)], min_val=0, max_val=E - 1)
                    expert_loads(item, e)
            sp.dma_start(fw_row[:], final_norm_w.partition_broadcast(P)).then_inc(fin_s, 16)
            for tb in range(TB):
                sp.wait_ge(out_s, tb + 1)
                sp.dma_start(out[0, tb * P:(tb + 1) * P, :], e_acc[:, tb, :]).then_inc(stored, 16)
            sp.wait_ge(stored, 16 * TB)

        @block.gpsimd
        def _(pool):
            n_chain = [0]

            def link(ins):
                n_chain[0] += 1
                ins.then_inc(pool_c, 1)
                pool.wait_ge(pool_c, n_chain[0])

            def keep(view, pattern, base, mult, op=ALU.is_ge, fill=0.0):
                link(pool.affine_select(out=view, in_=view, compare_op=op, fill=fill, base=base,
                                        pattern=pattern, channel_multiplier=mult))

            pool.memset(prm_b, 0.0).then_inc(zeroed, 1)
            pool.memset(eps_c[:], EPS)
            pool.memset(one_c[:], 1.0)
            link(pool.memset(pick[:], 0.0))
            pool.memset(pick[:, NQ - 1:NQ], 1.0)
            link(pool.memset(ones[:], 1.0))
            link(pool.memset(ident[:], 0.0))
            pool.affine_select(out=ident[:], in_=ident[:], compare_op=ALU.not_equal, fill=1.0, base=0,
                               pattern=[[-1, P]], channel_multiplier=1).then_inc(consts, 1)
            for k in range(2):
                for i in range(HALF):
                    ins = pool.memset(invf[:, k * HALF + i:k * HALF + i + 1],
                                      float(np.float32(ROPE_THETA) ** np.float32(-2.0 * i / ROT)))
                    if k < 1 or i < HALF - 1:
                        link(ins)
            ins.then_inc(consts, 1)
            for m, base, cm, step in ((incl_blk, 0, -1, 1), (after_blk, -1, 1, -1), (before_blk, -1, -1, 1)):
                link(pool.memset(m[:], 1.0))
                keep(m[:], [[step, P]], base, cm)
                v = m[:].rearrange("p (b n) -> p b n", n=CHUNK)
                keep(v, [[-CHUNK, P // CHUNK], [0, CHUNK]], 0, 1)
                keep(v, [[CHUNK, P // CHUNK], [0, CHUNK]], CHUNK - 1, -1)
            for lev in range(7):
                w = 1 << (lev % 6)
                link(pool.memset(lev_f[:], 0.0))
                v = lev_f[:].rearrange("p (b n) -> p b n", n=2 * w)
                lo_half = v[:, :, 0:w] if lev < 6 else v[:, :, w:2 * w]
                link(pool.memset(lo_half, 1.0))
                nb = P // (2 * w)
                first = w if lev < 6 else 0
                keep(lo_half, [[-2 * w, nb], [0, w]], -first, 1)
                keep(lo_half, [[2 * w, nb], [0, w]], first + w - 1, -1)
                link(pool.tensor_copy(lev_mask[:, lev, :], lev_f[:]))
            link(pool.memset(am0[:], 0.0))
            link(pool.memset(am0[0:CHUNK, CHUNK:2 * CHUNK], NEG))
            link(pool.memset(am1[:], 0.0))
            link(pool.memset(am1[0:CHUNK, 0:CHUNK], NEG))
            link(pool.memset(am1[0:CHUNK, 3 * CHUNK:4 * CHUNK], NEG))
            pool.memset(am1[CHUNK:P, 0:2 * CHUNK], NEG).then_inc(consts, 1)

            pool.wait_ge(consts, 3)
            pool.wait_ge(rope_s, 1)
            for l in range(L):
                pool.wait_ge(sw_s, 6 * (l + 1))
                cs = [rope[:, :, i, :].unsqueeze(2).to_broadcast([P, TB, 10, HALF]) for i in range(2)]
                x1, x2 = a_qk[:, :, :, 0:HALF], a_qk[:, :, :, HALF:ROT]
                pr = [a_rt[:, i, :].rearrange("p (t h e) -> p t h e", t=TB, h=10) for i in range(4)]
                pool.tensor_tensor(pr[0], x1, cs[1], ALU.mult)
                pool.tensor_tensor(pr[1], x2, cs[0], ALU.mult)
                pool.tensor_tensor(pr[2], x2, cs[1], ALU.mult)
                link(pool.tensor_tensor(pr[3], x1, cs[0], ALU.mult))
                pool.tensor_tensor(x1, pr[0], pr[1], ALU.subtract)
                pool.tensor_tensor(x2, pr[2], pr[3], ALU.add).then_inc(rot_s, 1)

            pool.wait_ge(mix_s, 4 * L)
            for t in (e_acc, e_y, slot_of, wt_of):
                pool.memset(t[:], 0.0)
            pool.memset(e_pwT[:], 0.0).then_inc(pwt_s, 1)
            link(pool.memset(upper[:], 1.0))
            pool.affine_select(out=upper[:], in_=upper[:], compare_op=ALU.is_ge, fill=0.0, base=-1,
                               pattern=[[1, P]], channel_multiplier=-1).then_inc(upper_s, 1)

        @block.scalar
        def _(act):
            n_chain = [0]

            def link(ins):
                n_chain[0] += 1
                ins.then_inc(act_c, 1)
                act.wait_ge(act_c, n_chain[0])

            done = [0]

            def hi(u_wait, ring_slot, buf, free):
                act.wait_ge(landed[ring_slot], u_wait)
                if free is not None:
                    act.wait_ge(split_used, free)
                act.copy(w_hi[buf][:], ring[:, ring_slot, :]).then_inc(hi_ready, 1)

            def ahead(key, by=1):
                upto = min(s_of[key] + by, S0 - 1)
                while done[0] <= upto:
                    s = done[0]
                    u = u_of[split_keys[s]]
                    hi(landed_at[u], u % RING, buf_of[s], free_at[s])
                    done[0] += 1

            def product(key, by=1):
                ahead(key, by)
                act.wait_ge(split_used, s_of[key] + 1)

            def ada_copy(n, bank):
                act.wait_ge(ada_sum, n)
                act.copy(ada_rows[0:NQ, :], ps[bank][0:NQ, :]).then_inc(ada_row, 1)

            def norm(m, tmp, ready):
                act.activation(stat[:, 15:16], one_c[:], ACT.Sqrt)
                for tb in range(TB):
                    act.wait_ge(*ready[tb])
                    act.activation(tmp[:, tb * 4:(tb + 1) * 4, :].rearrange("p a b -> p (a b)"), xs[:, tb, :],
                                   ACT.Square, accum_out=stat[:, tb:tb + 1]).then_inc(ssq, 1)
                act.wait_ge(ssq, 2 * m + 2)
                act.activation(stat[:, 2:4], stat[:, 0:2], ACT.Sqrt, bias=eps_c[:, 0:1],
                               scale=1.0 / D).then_inc(rstd_s, 1)

            def h_high(m, tmp):
                for kp in range(4):
                    act.wait_ge(hmod, 4 * m + kp + 1)
                    act.copy(hT_hi[:, 2 * kp:2 * kp + 2, :], tmp[:, 2 * kp:2 * kp + 2, :]).then_inc(h_hi_s, 1)

            act.wait_ge(cols_s, 1)
            act.activation(c_silu[:], cols[:, COL_C:COL_C + KO], ACT.Silu).then_inc(csil, 1)

            for l in range(L):
                norm(2 * l, f_tmp if l else m_tmp, [(xf_s, tb + 1) if l else (x_in, 16) for tb in range(TB)])
                if l == 0:
                    ahead(("qkvz", 0, 0), 0)
                    ada_copy(1, 0)
                h_high(2 * l, m_tmp)

                def silu_of(j):
                    act.wait_ge(conv_s, 6 * l + j + 1)
                    act.activation(qkv[:, 2 * j:2 * j + 2, :], cv[j % 2], ACT.Silu).then_inc(qkv_s, 1)
                    if j < 4:
                        act.wait_ge(qkv_s, 8 * l + j + 1)
                        if j >= 2:
                            act.wait_ge(l2_ps, 4 * l + j - 1)
                        act.activation(sq[j % 2], qkv[:, 2 * j:2 * j + 2, :].rearrange("p a b -> p (a b)"),
                                       ACT.Square).then_inc(sq_s, 1)

                for j in range(6):
                    product(("qkvz", l, j))
                    if j >= 2:
                        act.wait_ge(conv_s, 6 * l + j - 1)
                    act.copy(raw[j % 2][:, :, PAD:], ps[j % 2][:].rearrange("p (a b) -> p a b", a=2)).then_inc(raw_s, 1)
                    if j:
                        silu_of(j - 1)
                    if l == 0 and j == 3:
                        act.wait_ge(rope_pre, 1)
                        act.activation(rope[:].rearrange("p t k e -> p (t k e)"), ang[:, 5, :],
                                       ACT.Sin).then_inc(rope_s, 1)
                silu_of(5)
                product(("swq", l, 1))
                for tb in range(TB):
                    act.copy(a_qk[:, tb, 0:NQH, :].rearrange("p (j g) d -> p g j d", g=G),
                             ps[2 + tb][:].rearrange("p (g j d) -> p g j d", g=G, j=J)).then_inc(sw_s, 1)
                product(("swkv", l), 1)
                for tb in range(TB):
                    act.copy(a_qk[:, tb, NQH:NQH + G, :],
                             ps[tb][:, 0:P].rearrange("p (g d) -> p g d", g=G)).then_inc(sw_s, 1)
                    act.copy(a_v[:, tb, :], ps[tb][:, P:2 * P]).then_inc(sw_s, 1)
                ahead(("qkvz", l, 7), 0)
                for j in range(4):
                    act.wait_ge(l2_ps, 4 * l + j + 1)
                    act.activation(rinv[:, 2 * j:2 * j + 2, :].rearrange("p a b -> p (a b)"), ps[4 + j][:],
                                   ACT.Ln, bias=eps_c[:, 0:1]).then_inc(ln_s, 1)
                act.wait_ge(ln_s, 4 * (l + 1))
                act.activation(rinv, rinv, ACT.Exp, scale=-0.5).then_inc(rinv_s, 1)
                act.wait_ge(beta_a, l + 1)
                act.activation(gb[:, 0], ba[:, :, 0:H], ACT.Exp, scale=-1.0)
                link(act.activation(gb[:, 4], gb[:, 3], ACT.Exp, scale=-1.0))
                if l == 0:
                    act.activation(head_rows[:, 2 * L * H:3 * L * H], head_rows[:, 0:L * H], ACT.Exp)
                act.activation(gb[:, 4], gb[:, 4], ACT.Ln, bias=one_c[:, 0:1]).then_inc(beta_e, 1)

                for j in (6, 7):
                    product(("qkvz", l, j), 0)
                    act.activation(qkv[:, 2 * j:2 * j + 2, :].rearrange("p a b -> p (a b)"), ps[j - 4][:],
                                   ACT.Silu).then_inc(qkv_s, 1)

                def att(t):
                    act.wait_ge(att_ps, NTASK * l + t + 1)

                for t in (0, 1):
                    att(t)
                    act.copy(a_qT[:, 2 * t:2 * t + 2, :].rearrange("p a b -> p (a b)"),
                             ps[t % 4][:]).then_inc(att_a, 1)
                att(2)
                act.copy(a_kT, ps[2][:, 0:T]).then_inc(att_a, 1)
                for tb in range(TB):
                    act.wait_ge(mx_s, TB * l + tb + 1)
                    act.activation(smax[:, tb, 3, :], smax[:, tb, 3, :], ACT.Exp)
                    for h in range(NQH):
                        ins = act.activation(a_s[tb][:, h, :], a_s[tb][:, h, :], ACT.Exp,
                                             bias=smax[:, tb, 0, h:h + 1], accum_out=smax[:, tb, 2, h:h + 1])
                    ins.then_inc(pe_s, 1)

                def turned_p(tb):
                    for n in range(2 * (tb + 1)):
                        t = T_TURN[tb] + n
                        att(t)
                        act.copy(a_pt[:, 4 * n:4 * n + 4, :].rearrange("p a b -> p (a b)"),
                                 ps[t % 4][:]).then_inc(att_a, 1)

                def out_high(tb):
                    for g in range(G):
                        t = T_PV[tb] + g
                        att(t)
                        rows = slice(g * DH, (g + 1) * DH)
                        act.copy(ob_hi[rows, :, tb * P:(tb + 1) * P],
                                 ps[t % 4][rows, :].rearrange("p (j q) -> p j q", j=J)).then_inc(obh_s, 1)

                def exp_map(n, dst, banks):
                    for tb in range(TB):
                        act.wait_ge(maps, 4 * l + n)
                        act.activation(dst[tb], ps[banks + tb][:].rearrange("p (h c) -> p h c", h=H),
                                       ACT.Exp).then_inc(exps_s, 1)

                exp_map(2, [EG[:, :, tb * P:(tb + 1) * P] for tb in range(TB)], 6)
                turned_p(0)
                out_high(0)
                exp_map(3, [ED[:, :, tb * P:(tb + 1) * P] for tb in range(TB)], 4)
                turned_p(1)
                ahead(("gate", l, 0), 0)
                exp_map(4, [X[:, tb * H:(tb + 1) * H, :] for tb in range(TB)], 6)
                out_high(1)

                def gate(j):
                    product(("gate", l, j))
                    act.activation(gate_sb[:, 2 * j:2 * j + 2, :].rearrange("p a b -> p (a b)"),
                                   ps[0][:], ACT.Sigmoid).then_inc(gate_s, 1)

                for j in range(6):
                    gate(j)
                for n in range(4):
                    act.wait_ge(tok_ps, 4 * l + n + 1)
                    dst = (v_tok, k_tok)[n // 2][:, n % 2]
                    act.copy(dst.rearrange("p h d -> p (h d)"), ps[(6, 7, 4, 5)[n]][:]).then_inc(tok_s, 1)
                for n in range(NCH):
                    rows = slice((n % 2) * CHUNK, (n % 2 + 1) * CHUNK)
                    act.wait_ge(vn_ps, NCH * l + n + 1)
                    act.copy(v_new[rows].rearrange("p h d -> p (h d)"), ps[5][rows, :]).then_inc(vn_s, 1)
                    if n == 0:
                        ahead(("gate", l, 7), 0)
                    if n in (1, 2):
                        gate(5 + n)
                        ahead(("wb", l, 0), 0)
                    act.wait_ge(o_ps, NCH * l + n + 1)
                    act.copy(OT[:, :, n * CHUNK:(n + 1) * CHUNK],
                             ps[7][:, 0:H * CHUNK].rearrange("p (h c) -> p h c", h=H)).then_inc(o_s, 1)
                act.wait_ge(o_s, NCH * (l + 1))
                act.activation(o_sq, OT, ACT.Square).then_inc(osq_s, 1)
                if l == 0:
                    ada_copy(2, 1)
                ahead(("wb", l, 1), 0)
                act.wait_ge(on_ps, l + 1)
                for n in range(2):
                    act.activation(o_r[:, 2 * n:2 * n + 2, :].rearrange("p a b -> p (a b)"), ps[4 + n][:],
                                   ACT.Ln, bias=eps_c[:, 0:1], scale=1.0 / DK).then_inc(ln2_s, 1)
                act.wait_ge(ln2_s, 2 * (l + 1))
                act.activation(o_r, o_r, ACT.Exp, scale=-0.5).then_inc(on_s, 1)
                ahead(("wa", l, 0), 0)
                act.wait_ge(oaf, l + 1)
                act.copy(oa_hi[:], OT).then_inc(oa_h, 1)
                ahead(("wa", l, 1), 0)
                for cc in range(2):
                    ahead(("mix", l, cc, 0), 0)
                    act.wait_ge(y_sum_s, 2 * l + cc + 1)
                    act.copy(hT_hi[:, 4 * cc:4 * cc + 4, :], y_sum[:, 4 * cc:4 * cc + 4, :]).then_inc(y_hi_s, 1)
                ahead(("mix", l, 1, 1), 1)
                if l == 0:
                    norm(1, f_tmp, [(mix_s, 3 + tb) for tb in range(TB)])
                    h_high(1, f_tmp)

                    def f_silu(i):
                        product(("fg", i), 2)
                        if i >= 2:
                            act.wait_ge(fh_s, i - 1)
                        act.activation(f_g[i % 2][:].rearrange("p a b -> p (a b)"), ps[0][:],
                                       ACT.Silu).then_inc(fs_s, 1)

                    def f_high(i):
                        if i >= 2:
                            act.wait_ge(split_used, s_of[("fd", i - 2)] + 1)
                        act.wait_ge(fh_s, i + 1)
                        act.copy(f_hi[i % 2][:], f_h[:]).then_inc(fhh_s, 1)

                    for i in range(2 * FC):
                        f_silu(i)
                        ahead(("fu", i), 2)
                        f_high(i)
                        if i == NQ:
                            ada_copy(3, 3)
                    ahead(("qkvz", 1, 0), 0)
            norm(3, e_tmp, [(mix_s, 4 * L - 1 + tb) for tb in range(TB)])
            act.wait_ge(lg_s, 1)
            act.activation(lg[:, 8, :, 0:1], lg[:, 8, :, 0:1], ACT.Exp).then_inc(lge_s, 1)
            act.wait_ge(gt_ps, 4)
            act.copy(e_gt[:, 0:512], ps[0][:])
            act.copy(e_gt[:, 512:1024], ps[1][:]).then_inc(gt_s, 1)
            act.wait_ge(ga_s, 2)
            act.copy(xg_hi[:], e_xf[:]).then_inc(xgh_s, 1)
            act.copy(stat[:, 9:10], one_c[:]).then_inc(ms_s, 1)
            act.wait_ge(route_s, 1)
            n_items = act.value_load(meta[0:1, 0:1], min_val=E, max_val=E + 3)

            def copy_y(i):
                act.wait_ge(cb_ps, 4 * i + 1)
                act.wait_ge(split_used, S0 + MU * i)
                for n in range(2):
                    act.copy(e_y[:, n * 512:(n + 1) * 512], ps[6 + n][:]).then_inc(y_c, 1)

            with act.Fori(0, n_items) as i:
                def split(p):
                    act.wait_ge(landed[p % RING],
                                16 * (MU // RING) * i + (level[p % RING] + 16 * (p // RING + 1)))
                    act.wait_ge(split_used, MU * i + (S0 + p - NS_MOE + 1))
                    act.copy(w_hi[p % NS_MOE][:], ring[:, p % RING, :]).then_inc(hi_ready, 1)

                split(0)
                split(1)
                copy_y(i)
                for p, (kind, fc, half) in enumerate(moe_units):
                    if p + 2 < MU:
                        split(p + 2)
                    if kind == "g" and half == 1:
                        act.wait_ge(split_used, MU * i + (S0 + p + 1))
                        act.wait_ge(mh_s, FC * i + max(fc, 1))
                        act.activation(e_g[fc % 2][:], ps[2 * (fc % 2)][:], ACT.Silu).then_inc(ms_s, 1)
                    f = turned_after.get(p)
                    if f is not None:
                        act.wait_ge(mt_ps, FC * i + (f + 2))
                        act.wait_ge(split_used, MU * i + (S0 + (mp[("d", f - 2, 1)] + 1 if f >= 2 else 0)))
                        act.copy(h_hi[f % 2][:].rearrange("p a b -> p (a b)"), ps[4][:]).then_inc(mhh_s, 1)
                    if (kind, fc, half) == ("d", FC - 2, 1):
                        act.wait_ge(ga_s, 2 * i + 4)
                        act.wait_ge(split_used, MU * i + (S0 + mp[("u", FC - 1, 1)] + 1))
                        act.copy(xg_hi[:], e_xf[:]).then_inc(xgh_s, 1)
            copy_y(n_items)
            norm(4, e_tmp, [(xf_s, TB + tb + 1) for tb in range(TB)])

        @block.tensor
        def _(pe):
            def by_token(o, xh, xl, wh, wl, start, stop):
                pe.matmul(o, xh, wh, start=start, stop=False)
                pe.matmul(o, xh, wl, start=False, stop=False)
                return pe.matmul(o, xl, wh, start=False, stop=stop)

            def by_channel(o, wh, wl, xh, xl, start, stop):
                pe.matmul(o, wh, xh, start=start, stop=False)
                pe.matmul(o, wh, xl, start=False, stop=False)
                return pe.matmul(o, wl, xh, start=False, stop=stop)

            def parts(key, k):
                pe.wait_ge(taken, u_of[key] + 1)
                b = buf_of[s_of[key]]
                return (w_hi[b][:].rearrange("p (k n) -> p k n", k=k),
                        w_lo[b][:].rearrange("p (k n) -> p k n", k=k))

            def ada_piece(l, q, bank, first, last):
                pe.wait_ge(taken, u_of[("ada", l, q, 1)] + 1)
                pe.matmul(ps[bank][0:NQ, :], pick[:, NQ - 1 - q:2 * NQ - 1 - q], ada_acc[:, (NQ * l + q) % 2, :],
                          start=first, stop=last).then_inc(ada_sum if last else ada_used, 1)

            def ada_turn(n, bank):
                pe.wait_ge(ada_row, n)
                for t in range(4):
                    ins = pe.transpose(ps[bank][:, NQ * t:NQ * (t + 1)], ada_rows[0:NQ, t * P:(t + 1) * P],
                                       ident[0:NQ, 0:NQ])
                ins.then_inc(ada_ps, 1)

            def tokens(tb):
                return slice(tb * P, (tb + 1) * P)

            def turn_x(m, xn):
                pe.wait_ge(xn_s, 2 * m + 2)
                for kp in range(4):
                    for k in range(2):
                        for tb in range(TB):
                            ins = pe.transpose(ps[4 + kp][:, k * T + tb * P:k * T + (tb + 1) * P],
                                               xn[:, tb, (2 * kp + k) * P:(2 * kp + k + 1) * P], ident[:])
                    ins.then_inc(xnT, 1)

            def one_block(key, bank, t, m=None):
                wh, wl = parts(key, KO)
                for ko in range(KO):
                    if m is not None and t == 0 and ko % 2 == 0:
                        pe.wait_ge(h_s, 4 * m + ko // 2 + 1)
                    ins = by_channel(ps[bank][:, t * T:(t + 1) * T], wh[:, ko, t * P:(t + 1) * P],
                                     wl[:, ko, t * P:(t + 1) * P], hT_hi[:, ko, :], hT_lo[:, ko, :],
                                     ko == 0, ko == KO - 1)
                if t == 1:
                    ins.then_inc(split_used, 1)

            def two_blocks(key, bank, m=None):
                for t in range(2):
                    one_block(key, bank, t, m)

            def gate_row(n, dg, banks):
                pe.wait_ge(gtd_s, n)
                for k in range(2):
                    ins = pe.matmul(ps[banks[k]][:], ones[:],
                                    dg[:, 4 * k:4 * k + 4, :].rearrange("p a b -> p (a b)"), start=True, stop=True)
                ins.then_inc(gt_ps, 1)

            pe.wait_ge(consts, 1)
            pe.wait_ge(setup_in, SETUP_IN)
            pe.transpose(ps[0][:, 0:P], prm_a, ident[:])
            pe.transpose(ps[0][:, P:2 * P], prm_b, ident[:]).then_inc(prm_t, 1)

            for l in range(L):
                if l == 0:
                    pe.wait_ge(cols_s, 1)
                    for q in range(NQA):
                        ada_piece(0, q, 0, q == 0, q == NQA - 1)
                    ada_turn(1, 0)

                turn_x(2 * l, m_xn)
                def narrow(w, bank):
                    for ko in range(KO):
                        ins = pe.matmul(ps[bank][0:2 * H, 0:T], w[:, ko, :], m_tmp[:, ko, :],
                                        start=ko == 0, stop=ko == KO - 1)
                    ins.then_inc(bar_ps, 1)

                def l2(j):
                    pe.wait_ge(sq_s, 4 * l + j + 1)
                    pe.matmul(ps[4 + j][:], ones[:], sq[j % 2], start=True, stop=True).then_inc(l2_ps, 1)

                if l == 0:
                    pe.wait_ge(ada_s, 1)
                for j in range(6):
                    if j >= 2:
                        pe.wait_ge(raw_s, 6 * l + j - 1)
                    two_blocks(("qkvz", l, j), j % 2, None if j else 2 * l)
                    if j == 0:
                        narrow(w_ba[:, l], 2)
                    if j == 1:
                        pe.wait_ge(bar_s, l + 1)
                        for tb in range(TB):
                            ins = pe.transpose(ps[2][:, 8 * tb:8 * tb + 8], ba_rows[0:2 * H, tokens(tb)],
                                               ident[0:2 * H, 0:2 * H])
                        ins.then_inc(ba_ps, 1)
                    if j >= 3:
                        l2(j - 3)
                pe.wait_ge(ba_s, l + 1)
                for kh in range(2):
                    wh, wl = parts(("swq", l, kh), 4)
                    for tb in range(TB):
                        for kk in range(4):
                            ko = 4 * kh + kk
                            ins = by_token(ps[2 + tb][:], hT_hi[:, ko, tokens(tb)], hT_lo[:, ko, tokens(tb)],
                                           wh[:, kk, :], wl[:, kk, :], ko == 0, ko == KO - 1)
                    ins.then_inc(split_used, 1)
                l2(3)
                pe.wait_ge(raw_s, 6 * (l + 1))
                wh, wl = parts(("swkv", l), KO)
                for tb in range(TB):
                    for ko in range(KO):
                        ins = by_token(ps[tb][:, 0:2 * P], hT_hi[:, ko, tokens(tb)], hT_lo[:, ko, tokens(tb)],
                                       wh[:, ko, :], wl[:, ko, :], ko == 0, ko == KO - 1)
                ins.then_inc(split_used, 1)

                pe.wait_ge(sw_s, 6 * l + 2)
                for j in (6, 7):
                    two_blocks(("qkvz", l, j), j - 4)

                def step(t):
                    if t >= 4:
                        att_freed(pe, l, t - 4)
                    return ps[t % 4]

                pe.wait_ge(rot_s, l + 1)
                pe.wait_ge(sw_s, 6 * (l + 1))
                for t in (0, 1):
                    b = step(t)
                    for jj in range(2):
                        for tb in range(TB):
                            j = 2 * t + jj
                            ins = pe.transpose(b[:, jj * T + tb * P:jj * T + (tb + 1) * P],
                                               a_qk[:, tb, 2 * j:2 * j + 2, :].rearrange("p g d -> p (g d)"), ident[:])
                    ins.then_inc(att_ps, 1)
                pe.wait_ge(qkv_s, 8 * (l + 1))
                b = step(2)
                for tb in range(TB):
                    ins = pe.transpose(b[:, tb * P:(tb + 1) * P],
                                       a_qk[:, tb, NQH:NQH + G, :].rearrange("p g d -> p (g d)"), ident[:])
                ins.then_inc(att_ps, 1)
                pe.wait_ge(att_a, NATT_A * l + 3)

                def scores(tb):
                    keys, per = P * (tb + 1), 4 // (tb + 1)
                    for n in range(NQH // per):
                        t = T_SCORE[tb] + n
                        b = step(t)
                        for m in range(per):
                            h = n * per + m
                            g, j = divmod(h, J)
                            rows = slice(g * DH, (g + 1) * DH)
                            ins = pe.matmul(b[:, m * keys:(m + 1) * keys], a_qT[rows, j, tokens(tb)],
                                            a_kT[rows, 0:keys], start=True, stop=True)
                        ins.then_inc(att_ps, 1)

                def turn_p(tb):
                    pe.wait_ge(pn_s, TB * l + tb + 1)
                    for n in range(2 * (tb + 1)):
                        b = step(T_TURN[tb] + n)
                        for m in range(4):
                            h, kb = divmod(4 * n + m, tb + 1)
                            ins = pe.transpose(b[:, m * P:(m + 1) * P], a_s[tb][:, h, tokens(kb)], ident[:])
                        ins.then_inc(att_ps, 1)

                def p_v(tb):
                    for g in range(G):
                        b = step(T_PV[tb] + g)
                        pe.wait_ge(att_a, NATT_A * l + 5 + 4 * tb)
                        for j in range(J):
                            for kb in range(tb + 1):
                                ins = pe.matmul(b[:, j * P:(j + 1) * P], a_v[:, kb, :],
                                                a_pt[:, (g * J + j) * (tb + 1) + kb, :],
                                                start=kb == 0, stop=kb == tb)
                        ins.then_inc(att_ps, 1)

                def spread(lhsT, rows, banks):
                    for tb in range(TB):
                        ins = pe.matmul(ps[banks + tb][:], lhsT, rows[:, tb, :], start=True, stop=True)
                    ins.then_inc(maps, 1)

                scores(0)
                scores(1)
                pe.wait_ge(grow_s, l + 1)
                spread(ones[:], g_rows[0], 4)
                spread(ones[:], g_rows[2], 6)
                turn_p(0)
                pe.wait_ge(kb_s, 2 * (l + 1))
                spread(ones[:], g_rows[1], 4)
                p_v(0)
                turn_p(1)
                pe.wait_ge(exps_s, 6 * l + 2)
                spread(after_blk[:], g_rows[2], 6)
                p_v(1)

                pe.wait_ge(exps_s, 6 * l + 4)
                for tb in range(TB):
                    for h in range(H):
                        ins = pe.matmul(ps[4 + tb][:, h * P:(h + 1) * P], kT[:, h, tokens(tb)],
                                        KB[:, h, tokens(tb)], start=True, stop=True)
                ins.then_inc(lat, 1)
                pe.wait_ge(exps_s, 6 * l + 6)
                for tb in range(TB):
                    for h in range(H):
                        ins = pe.matmul(ps[6 + tb][:, h * P:(h + 1) * P], kT[:, h, tokens(tb)],
                                        qT[:, h, tokens(tb)], start=True, stop=True)
                ins.then_inc(lat, 1)
                pe.wait_ge(att_d, NATT_D * (l + 1))
                one_block(("gate", l, 0), 0, 0)
                pe.wait_ge(lat_s, 2 * l + 1)
                for tb in range(TB):
                    for h in range(H):
                        ins = pe.transpose(ps[2 + tb][:, h * P:(h + 1) * P], LT[:, tb * H + h, :], ident[:])
                ins.then_inc(l0_ps, 1)
                one_block(("gate", l, 0), 0, 1)
                if l == 0:
                    ada_piece(0, 4, 1, True, False)
                pe.wait_ge(inv0, l + 1)
                for lev in range(1, 6):
                    for tb in range(TB):
                        if lev > 1:
                            pe.wait_ge(xx_s, 10 * l + 2 * (lev - 2) + tb + 1)
                        for h in range(H):
                            n = tb * H + h
                            ins = pe.matmul(ps[4 + tb][:, h * P:(h + 1) * P], LT[:, n, :], X[:, n, :],
                                            start=True, stop=True)
                        ins.then_inc(u_ps, 1)
                    pe.wait_ge(gate_s, 8 * l + lev)
                    two_blocks(("gate", l, lev), 0)
                    if l == 0 and lev != 2:
                        ada_piece(0, {1: 5, 3: 6, 4: 7, 5: 8}[lev], 1, False, False)
                    if lev == 5:
                        pe.wait_ge(kgb_s, l + 1)
                        pe.wait_ge(xx_s, 10 * l + 8)
                        for n in range(4):
                            if n == 2:
                                pe.wait_ge(u_s, 10 * (l + 1))
                            src = (vT, kT)[n // 2]
                            for h in range(H):
                                ins = pe.transpose(ps[(6, 7, 4, 5)[n]][:, h * P:(h + 1) * P],
                                                   src[:, h, tokens(n % 2)], ident[:])
                            ins.then_inc(tok_ps, 1)
                    for tb in range(TB):
                        pe.wait_ge(u_s, 10 * l + 2 * (lev - 1) + tb + 1)
                        for h in range(H):
                            n = tb * H + h
                            if lev < 5:
                                pe.matmul(ps[6 + tb][:, h * P:(h + 1) * P], XT[:, n, :], U[:, n, :],
                                          start=True, stop=True)
                            ins = pe.matmul(ps[2 + tb][:, h * P:(h + 1) * P], U[:, n, :], XT[:, n, :],
                                            start=True, stop=True)
                        ins.then_inc(xu_ps, 1)
                pe.wait_ge(xx_s, 10 * (l + 1))
                pe.wait_ge(tok_s, 4 * (l + 1))

                def half_branch(name, cc, banks, xh, xl, half):
                    wh, wl = parts((name, l, cc), 4)
                    for t in (2 * half, 2 * half + 1):
                        for k in range(4):
                            ins = by_channel(ps[banks[half]][:, (t % 2) * T:(t % 2 + 1) * T],
                                             wh[:, k, t * P:(t + 1) * P], wl[:, k, t * P:(t + 1) * P],
                                             xh[:, k, :], xl[:, k, :], k == 0, k == 3)
                    if half == 1:
                        ins.then_inc(split_used, 1)

                def branch(*args):
                    half_branch(*args, 0)
                    half_branch(*args, 1)

                for n in range(NCH):
                    tb, par = divmod(n, 2)
                    rows = slice(par * CHUNK, (par + 1) * CHUNK)
                    here = slice(n * CHUNK, (n + 1) * CHUNK)
                    state = states[n % 2]

                    def meanwhile(t):
                        if n in (1, 2):
                            if t == 0:
                                pe.wait_ge(gate_s, 8 * l + 5 + n)
                            one_block(("gate", l, 5 + n), 0, t)
                        if n == 3:
                            half_branch("wb", 0, (2, 3), ob_hi, ob_lo, t)

                    if n > 0:
                        pe.wait_ge(st_s, 3 * l + n)
                        for h in range(H):
                            ins = pe.matmul(ps[4][rows, h * P:(h + 1) * P], KB[:, h, here], state[:, h, :],
                                            start=True, stop=True)
                        ins.then_inc(ks_ps, 1)
                        meanwhile(0)
                        pe.wait_ge(res_s, 3 * l + n)
                    src = resid[rows] if n else v_tok[rows, tb]
                    if n:
                        pe.wait_ge(vn_s, NCH * l + n)
                    for h in range(H):
                        ins = pe.matmul(ps[5][rows, h * P:(h + 1) * P], XT[rows, tb * H + h, rows], src[:, h, :],
                                        start=True, stop=True)
                    ins.then_inc(vn_ps, 1)
                    meanwhile(1)
                    pe.wait_ge(vn_s, NCH * l + n + 1)
                    if n < NCH - 1:
                        for h in range(H):
                            ins = pe.matmul(ps[6][:, h * P:(h + 1) * P], k_tok[rows, tb, h, :], v_new[rows, h, :],
                                            start=True, stop=True)
                        ins.then_inc(su_ps, 1)
                    if n:
                        pe.wait_ge(o_s, NCH * l + n)
                    for h in range(H):
                        o = ps[7][:, h * CHUNK:(h + 1) * CHUNK]
                        if n:
                            pe.matmul(o, state[:, h, :], qT[:, h, here], start=True, stop=False)
                        ins = pe.matmul(o, v_new[rows, h, :], AT[rows, tb * H + h, rows], start=n == 0, stop=True)
                    ins.then_inc(o_ps, 1)
                    if l == 0 and n in (0, 2):
                        ada_piece(0, 9 + n // 2, 1, False, False)
                if l == 0:
                    ada_piece(0, 11, 1, False, True)
                if l == 0:
                    ada_turn(2, 1)
                pe.wait_ge(osq_s, l + 1)
                for n in range(2):
                    ins = pe.matmul(ps[4 + n][:], ones[:], o_sq[:, 2 * n:2 * n + 2, :].rearrange("p a b -> p (a b)"),
                                    start=True, stop=True)
                ins.then_inc(on_ps, 1)
                pe.wait_ge(gate_s, 8 * (l + 1))
                if l == 0:
                    pe.wait_ge(ada_s, 2)
                branch("wb", 1, (0, 1), ob_hi, ob_lo)
                pe.wait_ge(yb_s, 4 * l + 1)
                gate_row(2 * l + 1, m_dg, (2, 3))
                pe.wait_ge(oa_s, l + 1)
                branch("wa", 0, (6, 7), oa_hi, oa_lo)
                branch("wa", 1, (4, 5), oa_hi, oa_lo)
                pe.wait_ge(yb_s, 4 * l + 2)
                pe.wait_ge(gt_s, 2 * l + 1)
                for kh in range(2):
                    pe.wait_ge(y_s, 2 * l + kh + 1)
                    for cc in range(2):
                        wh, wl = parts(("mix", l, cc, kh), 4)
                        for tb in range(TB):
                            for kk in range(4):
                                ko = 4 * kh + kk
                                ins = by_token(ps[2 * cc + tb][:], hT_hi[:, ko, tokens(tb)], hT_lo[:, ko, tokens(tb)],
                                               wh[:, kk, :], wl[:, kk, :], ko == 0, ko == KO - 1)
                            if kh == 1 and cc == 1 and tb == 0:
                                ins.then_inc(first_ps, 1)
                        ins.then_inc(split_used, 1)

                if l == 0:
                    turn_x(1, f_xn)

                    def f_down(i):
                        wh, wl = parts(("fd", i), 2)
                        pe.wait_ge(fhl_s, i + 1)
                        for tb in range(TB):
                            for hf in range(2):
                                for ft in range(2):
                                    cs = slice(hf * 512, (hf + 1) * 512)
                                    ins = by_token(ps[4 + 2 * tb + hf][:], f_hi[i % 2][:, ft, tokens(tb)],
                                                   f_lo[i % 2][:, ft, tokens(tb)], wh[:, ft, cs], wl[:, ft, cs],
                                                   i == 0 and ft == 0, i == 2 * FC - 1 and ft == 1)
                            if i == 2 * FC - 1 and tb == 0:
                                ins.then_inc(first_ps, 1)
                        ins.then_inc(split_used, 1)

                    for i in range(2 * FC):
                        if i:
                            pe.wait_ge(fs_s, i)
                        two_blocks(("fg", i), 0, None if i else 1)
                        if i:
                            pe.wait_ge(fh_s, i)
                        two_blocks(("fu", i), 1)
                        if i:
                            f_down(i - 1)
                        if i < NQ:
                            ada_piece(1, i, 3, i == 0, i == NQ - 1)
                        if i == NQ:
                            ada_turn(3, 3)
                    gate_row(2, f_dg, (2, 3))
                    f_down(2 * FC - 1)

            turn_x(3, e_xn)
            for ko in range(KO):
                if ko % 2 == 0:
                    pe.wait_ge(hmod, 4 * 3 + ko // 2 + 1)
                ins = pe.matmul(ps[2][0:E, 0:T], w_router[:, ko, :], e_tmp[:, ko, :], start=ko == 0, stop=ko == KO - 1)
            ins.then_inc(logit_ps, 1)
            pe.wait_ge(upper_s, 1)
            pe.matmul(ps[3][:, 0:P], ones[:], upper[:], start=True, stop=True).then_inc(logit_ps, 1)
            pe.wait_ge(lgr_s, 1)
            for tb in range(TB):
                ins = pe.transpose(ps[2][:, E * tb:E * (tb + 1)], e_y[0:E, tokens(tb)], ident[0:E, 0:E])
            ins.then_inc(logit_ps, 1)
            gate_row(4, e_xf, (0, 1))
            pe.wait_ge(sel_s, 1)
            sel = [lg[:, 6, tb, :] for tb in range(TB)]
            pe.matmul(ps[5][:, 0:E], upper[:], sel[0], start=True, stop=True).then_inc(mt_ps, 1)
            pe.matmul(ps[5][:, E:2 * E], ones[:], sel[0], start=True, stop=False).then_inc(cb_ps, 1)
            pe.matmul(ps[5][:, E:2 * E], upper[:], sel[1], start=False, stop=True)
            pe.matmul(ps[5][:, 2 * E:3 * E], ones[:], sel[0], start=True, stop=False)
            pe.matmul(ps[5][:, 2 * E:3 * E], ones[:], sel[1], start=False, stop=True).then_inc(pos_ps, 1)

            def gather(piece, done, bank=5):
                if done is not None:
                    pe.wait_ge(ga_s, done)
                for k in range(4):
                    for tb in range(TB):
                        ko = 4 * piece + k
                        ins = pe.matmul(ps[bank][:, k * P:(k + 1) * P], e_xn[:, tb, ko * P:(ko + 1) * P],
                                        e_p[:, tb, :], start=tb == 0, stop=tb == TB - 1)
                ins.then_inc(ga_ps, 1)

            def combine(i, k):
                tb, hf = divmod(k, 2)
                if k == 0:
                    pe.wait_ge(y_c, 2 * i + 2)
                    pe.wait_ge(pwt_s, i + 1)
                    pe.wait_ge(ga_s, 2 * i + 2)
                pe.wait_ge(cb_s, 4 * i + (k + 1))
                pe.matmul(ps[5][:], e_pwT[:, tokens(tb)], e_y[:, hf * 512:(hf + 1) * 512],
                          start=True, stop=True).then_inc(cb_ps, 1)

            pe.wait_ge(p_s, 1)
            gather(0, None)
            gather(1, None, 4)
            pe.wait_ge(route_s, 1)
            n_items = pe.value_load(meta[0:1, 0:1], min_val=E, max_val=E + 3)
            with pe.Fori(0, n_items) as i:
                for p, (kind, fc, half) in enumerate(moe_units):
                    b = p % NS_MOE
                    pe.wait_ge(taken, MU * i + (U0 + p + 1))
                    if kind in "gu":
                        if p == 0:
                            pe.wait_ge(xg_s, i + 1)
                        if half == 0:
                            pe.wait_ge(ms_s if kind == "g" else mh_s, FC * i + max(fc, 1))
                        wh, wl = (w[b][:].rearrange("p (k n) -> p k n", k=4) for w in (w_hi, w_lo))
                        bank = ps[2 * (fc % 2) + (kind == "u")]
                        for kk in range(4):
                            ko = 4 * half + kk
                            ins = by_token(bank[:], xg_hi[:, ko, :], xg_lo[:, ko, :], wh[:, kk, :], wl[:, kk, :],
                                           ko == 0, ko == KO - 1)
                    else:
                        if half == 0:
                            pe.wait_ge(mhl_s, FC * i + (fc + 2))
                            if fc == 0:
                                pe.wait_ge(y_c, 2 * i + 2)
                        wh, wl = (w[b][:].rearrange("p (k n) -> p k n", k=2) for w in (w_hi, w_lo))
                        for hf in range(2):
                            for ft in range(2):
                                f = 2 * half + ft
                                cs = slice(hf * 512, (hf + 1) * 512)
                                ins = by_token(ps[6 + hf][:], h_hi[fc % 2][:, f, :], h_lo[fc % 2][:, f, :],
                                               wh[:, ft, cs], wl[:, ft, cs], fc == 0 and f == 0,
                                               fc == FC - 1 and f == 3)
                    ins.then_inc(split_used, 1)
                    if p < 4:
                        combine(i, p)
                    f = turned_after.get(p)
                    if f is not None:
                        pe.wait_ge(mh_s, FC * i + (f + 2))
                        pe.wait_ge(mhl_s, FC * i + (f + 1))
                        for k in range(4):
                            ins = pe.transpose(ps[4][:, k * P:(k + 1) * P], e_h[f % 2][:, k * P:(k + 1) * P], ident[:])
                        ins.then_inc(mt_ps, 1)
                    if p == mp[("g", 2, 0)]:
                        pe.wait_ge(pw_s, i + 1)
                        pe.wait_ge(cb_s, 4 * i + 5)
                        for tb in range(TB):
                            ins = pe.transpose(ps[5][:, tb * P:(tb + 1) * P], e_pw[:, tb, :], ident[:])
                        ins.then_inc(pwt_ps, 1)
                    if p == mp[("g", 4, 0)]:
                        pe.wait_ge(p_s, i + 2)
                        pe.wait_ge(pwt_s, i + 2)
                        gather(0, 2 * i + 2)
                    if p == mp[("g", 4, 1)]:
                        gather(1, 2 * i + 3)
            pe.wait_ge(y_c, 2 * n_items + 2)
            for k in range(4):
                tb, hf = divmod(k, 2)
                pe.matmul(ps[k][:], e_pwT[:, tokens(tb)], e_y[:, hf * 512:(hf + 1) * 512],
                          start=True, stop=True).then_inc(cb_ps, 1)

        @block.vector
        def _(dve):
            n_chain = [0]

            def mark(ins):
                n_chain[0] += 1
                ins.then_inc(dve_c, 1)
                return n_chain[0]

            def link(ins):
                dve.wait_ge(dve_c, mark(ins))

            def f32(t):
                return t.bitcast(F32)

            def wide(ap, shape, axis):
                return ap.unsqueeze(axis).to_broadcast(shape)

            done = [0]

            def take(u):
                key = units[u][0]
                if key[0] != "ada":
                    s = s_of[key]
                    dve.wait_ge(hi_ready, s + 1)
                    dve.tensor_tensor(w_lo[buf_of[s]][:], ring[:, u % RING, :], f32(w_hi[buf_of[s]][:]),
                                      ALU.subtract).then_inc(taken, 1)
                    return
                l, q, kh = key[1:]
                n = NQ * l + q
                acc = ada_acc[:, n % 2, :]
                dve.wait_ge(landed[u % RING], landed_at[u])
                if kh == 0 and n >= 2:
                    dve.wait_ge(ada_used, n - 1 - (n - 2 >= NQA - 1) - (n - 2 >= NQ - 1))
                    if n - 2 == NQA - 1:
                        dve.wait_ge(ada_sum, 1)
                    if n - 2 == NQ - 1:
                        dve.wait_ge(ada_sum, 2)
                if kh == 1:
                    dve.wait_ge(taken, u_of[("ada", l, q, 0)] + 1)
                w = ring[:, u % RING, :].rearrange("p (k n) -> p k n", k=4)
                for kk in range(4):
                    ck = c_silu[:, 4 * kh + kk:4 * kh + kk + 1]
                    if kh == 0 and kk == 0:
                        ins = dve.tensor_scalar(acc, w[:, kk, :], ck, None, ALU.mult)
                    else:
                        ins = dve.scalar_tensor_tensor(acc, w[:, kk, :], ck, acc, ALU.mult, ALU.add)
                    if kk < 3:
                        link(ins)
                    else:
                        ins.then_inc(taken, 1)

            def take_upto(u):
                while done[0] <= u:
                    take(done[0])
                    done[0] += 1

            def ahead(key, by=1):
                take_upto(u_of[split_keys[min(s_of[key] + by, S0 - 1)]])

            def product(key, by=1):
                ahead(key, by)
                dve.wait_ge(split_used, s_of[key] + 1)

            def norm(m, xn):
                dve.wait_ge(rstd_s, m + 1)
                link(dve.reciprocal(stat[:, 4:6], stat[:, 2:4]))
                for tb in range(TB):
                    dve.tensor_scalar(xn[:, tb, :], xs[:, tb, :], stat[:, 4 + tb:5 + tb], None,
                                      ALU.mult).then_inc(xn_s, 1)

            def modulate(m, tmp, parts=True):
                l, which = divmod(m, 2)
                w_at = (COL_NF if which else COL_NM) + l * KO
                link(dve.scalar_tensor_tensor(wsc[:], adac[:, l, (1 + 3 * which) * KO:(2 + 3 * which) * KO], 1.0,
                                              cols[:, w_at:w_at + KO], ALU.add, ALU.mult))

                def low(kp):
                    dve.wait_ge(h_hi_s, 4 * m + kp + 1)
                    two = slice(2 * kp, 2 * kp + 2)
                    dve.tensor_tensor(hT_lo[:, two, :], tmp[:, two, :], f32(hT_hi[:, two, :]),
                                      ALU.subtract).then_inc(h_s, 1)

                for kp in range(4):
                    dve.wait_ge(xnT, 4 * m + kp + 1)
                    for k in range(2):
                        ko = 2 * kp + k
                        sh = 3 * which * KO + ko
                        ins = dve.tensor_scalar(tmp[:, ko, :], ps[4 + kp][:, k * T:(k + 1) * T], wsc[:, ko:ko + 1],
                                                adac[:, l, sh:sh + 1], ALU.mult, ALU.add)
                    ins.then_inc(hmod, 1)
                    if kp and parts:
                        low(kp - 1)
                if parts:
                    low(3)

            def gate_diag(n, l, v, dg):
                dve.tensor_tensor(dg, wide(ident[:], [P, KO, P], 1),
                                  wide(adac[:, l, v * KO:(v + 1) * KO], [P, KO, P], 2), ALU.mult).then_inc(gtd_s, 1)

            def gate_copy(n, gt, banks):
                dve.wait_ge(gt_ps, n)
                for k in range(2):
                    ins = dve.tensor_copy(gt[:, k * 512:(k + 1) * 512], ps[banks[k]][:])
                ins.then_inc(gt_s, 1)
                dve.wait_ge(gt_s, n)

            dve.wait_ge(prm_t, 1)
            dve.tensor_copy(cols[:], ps[0][:, 0:2 * P]).then_inc(cols_s, 1)
            dve.wait_ge(csil, 1)
            def rotary_angles():
                dve.wait_ge(setup_b, SETUP_B)
                dve.wait_ge(consts, 2)
                link(dve.tensor_copy(ang[:, 4, 0:TB], pos_i))
                for tb in range(TB):
                    ins = dve.tensor_scalar(ang[:, 0, tb * ROT:(tb + 1) * ROT], invf, ang[:, 4, tb:tb + 1], None, ALU.mult)
                link(ins)
                link(dve.tensor_scalar(ang[:, 1, :], ang[:, 0, :], 1.0 / (2 * math.pi), None, ALU.mult))
                cosines = ang[:, 1, :].rearrange("p (t k e) -> p t k e", t=TB, k=2)[:, :, 1, :]
                link(dve.tensor_scalar(cosines, cosines, 0.25, None, ALU.add))
                magic = 1.5 * 2.0 ** 23
                link(dve.tensor_scalar(ang[:, 2, :], ang[:, 1, :], magic, None, ALU.add))
                link(dve.tensor_scalar(ang[:, 2, :], ang[:, 2, :], -magic, None, ALU.add))
                c1 = 6.28125
                c2 = float(np.frombuffer((np.frombuffer(np.float32(2 * math.pi - c1).tobytes(), np.uint32)
                                          & np.uint32(0xFFFFF000)).tobytes(), np.float32)[0])
                c3 = 2 * math.pi - c1 - c2
                for cpart in (c1, c2, c3):
                    link(dve.scalar_tensor_tensor(ang[:, 0, :], ang[:, 2, :], -cpart, ang[:, 0, :], ALU.mult, ALU.add))
                cosines = ang[:, 0, :].rearrange("p (t k e) -> p t k e", t=TB, k=2)[:, :, 1, :]
                link(dve.tensor_scalar(cosines, cosines, math.pi / 2, None, ALU.add))
                dve.tensor_scalar(ang[:, 5, :], ang[:, 0, :], 3.1415925, -3.1415925, ALU.min,
                                  ALU.max).then_inc(rope_pre, 1)

            def ada_columns(n, l, bank, q0, q1):
                dve.wait_ge(ada_ps, n)
                dve.tensor_tensor(adac[:, l, 4 * q0:4 * q1].rearrange("p (q t) -> p q t", t=4),
                                  ps[bank][:, 0:48].rearrange("p (t q) -> p q t", t=4)[:, q0:q1],
                                  cols[:, COL_AB + 48 * l + 4 * q0:COL_AB + 48 * l + 4 * q1]
                                  .rearrange("p (q t) -> p q t", t=4), ALU.add).then_inc(ada_s, 1)

            take_upto(u_of[("ada", 0, 1, 1)])
            norm(0, m_xn)
            take_upto(u_of[("ada", 0, NQA - 1, 1)])

            for l in range(L):
                if l == 0:
                    ahead(("qkvz", 0, 0), 0)
                    ada_columns(1, 0, 0, 0, NQA)
                    dve.wait_ge(ada_s, 1)
                if l:
                    norm(2 * l, m_xn)
                modulate(2 * l, m_tmp)
                ahead(("qkvz", l, 0), 1)
                dve.memset(raw[0][:, :, 0:PAD], 0.0)
                link(dve.memset(raw[1][:, :, 0:PAD], 0.0))
                for j in range(6):
                    ahead(("qkvz", l, j), 1)
                    if j == 0:
                        dve.wait_ge(bar_ps, l + 1)
                        dve.tensor_copy(ba_rows[0:2 * H, :], ps[2][0:2 * H, 0:T]).then_inc(bar_s, 1)
                    if l == 0 and j == 1:
                        rotary_angles()
                    if j == 2:
                        dve.wait_ge(ba_ps, l + 1)
                        dve.tensor_copy(ba[:].rearrange("p t n -> p (t n)"), ps[2][:, 0:16]).then_inc(ba_s, 1)
                        dve.wait_ge(ba_s, l + 1)
                        link(dve.tensor_tensor(gb[:, 2], ba[:, :, H:2 * H],
                                               wide(head_rows[:, (L + l) * H:(L + l + 1) * H], [P, TB, H], 1), ALU.add))
                        dve.scalar_tensor_tensor(gb[:, 3], gb[:, 2], -1.0, gb[:, 2], ALU.mult,
                                                 ALU.max).then_inc(beta_a, 1)
                    dve.wait_ge(raw_s, 6 * l + j + 1)
                    if j >= 2:
                        dve.wait_ge(qkv_s, 8 * l + j - 1)
                    at = [0, 0]
                    for tap in range(CTAPS):
                        for t in range(2):
                            cc = COL_CONV + l * CTAPS * 12 + tap * 12 + 2 * j + t
                            src = raw[j % 2][:, t, tap:tap + T]
                            if tap == 0:
                                ins = dve.tensor_scalar(cv[j % 2][:, t, :], src, cols[:, cc:cc + 1], None, ALU.mult)
                            else:
                                dve.wait_ge(dve_c, at[t])
                                ins = dve.scalar_tensor_tensor(cv[j % 2][:, t, :], src, cols[:, cc:cc + 1],
                                                               cv[j % 2][:, t, :], ALU.mult, ALU.add)
                            if tap == CTAPS - 1 and t == 1:
                                ins.then_inc(conv_s, 1)
                            else:
                                at[t] = mark(ins)
                ahead(("qkvz", l, 7), 0)

                dve.wait_ge(rinv_s, l + 1)
                dve.scalar_tensor_tensor(qT, qT, float(DK) ** -0.5, rinv[:, 0:4, :], ALU.mult, ALU.mult)
                dve.tensor_tensor(kT, kT, rinv[:, 4:8, :], ALU.mult).then_inc(qkn_s, 1)
                dve.wait_ge(beta_e, l + 1)
                link(dve.tensor_scalar(gb[:, 0], gb[:, 0], 1.0, None, ALU.add))
                dve.reciprocal(gb[:, 1], gb[:, 0])
                link(dve.scalar_tensor_tensor(gb[:, 2], gb[:, 2], 0.0, gb[:, 4], ALU.max, ALU.add))
                link(dve.scalar_tensor_tensor(gb[:, 5], gb[:, 2], -1.0,
                                              wide(head_rows[:, (2 * L + l) * H:(2 * L + l + 1) * H], [P, TB, H], 1),
                                              ALU.mult, ALU.mult))
                dve.wait_ge(rot_s, l + 1)
                dve.wait_ge(qkn_s, l + 1)
                for rows, mask, src in ((g_rows[0], ident, 1), (g_rows[1], after_blk, 5), (g_rows[2], incl_blk, 5)):
                    for tb in range(TB):
                        ins = dve.tensor_tensor(rows[:, tb, :].rearrange("p (h c) -> p h c", h=H),
                                                wide(mask[:], [P, H, P], 1),
                                                wide(gb[:, src, tb, :], [P, H, P], 2), ALU.mult)
                ins.then_inc(grow_s, 1)

                def evacuate(tb):
                    keys, per = P * (tb + 1), 4 // (tb + 1)
                    am, sm = (am0, am1)[tb], smax[:, tb]
                    for n in range(NQH // per):
                        t = T_SCORE[tb] + n
                        dve.wait_ge(att_ps, NTASK * l + t + 1)
                        dve.scalar_tensor_tensor(a_s[tb][:, n * per:(n + 1) * per, :],
                                                 ps[t % 4][:].rearrange("p (h k) -> p h k", h=per), float(DH) ** -0.5,
                                                 wide(am[:], [P, per, keys], 1), ALU.mult, ALU.add).then_inc(att_d, 1)
                    dve.wait_ge(att_d, NATT_D * l + (2, 6)[tb])
                    link(dve.tensor_reduce(sm[:, 0, :], a_s[tb], AX.X, ALU.max))
                    link(dve.tensor_tensor(sm[:, 1, :], sm[:, 0, :], sink_rows[:, l, :], ALU.max))
                    dve.tensor_tensor(sm[:, 3, :], sink_rows[:, l, :], sm[:, 1, :], ALU.subtract)
                    dve.tensor_scalar(sm[:, 0, :], sm[:, 1, :], -1.0, None, ALU.mult).then_inc(mx_s, 1)

                def divide(tb):
                    sm = smax[:, tb]
                    dve.wait_ge(pe_s, TB * l + tb + 1)
                    link(dve.tensor_tensor(sm[:, 1, :], sm[:, 2, :], sm[:, 3, :], ALU.add))
                    link(dve.reciprocal(sm[:, 2, :], sm[:, 1, :]))
                    dve.tensor_tensor(a_s[tb], a_s[tb], wide(sm[:, 2, :], [P, NQH, P * (tb + 1)], 2),
                                      ALU.mult).then_inc(pn_s, 1)

                def out_low(tb):
                    for g in range(G):
                        rows = slice(g * DH, (g + 1) * DH)
                        dve.wait_ge(obh_s, 4 * l + 2 * tb + g + 1)
                        dve.tensor_tensor(ob_lo[rows, :, tb * P:(tb + 1) * P],
                                          ps[(T_PV[tb] + g) % 4][rows, :].rearrange("p (j q) -> p j q", j=J),
                                          f32(ob_hi[rows, :, tb * P:(tb + 1) * P]), ALU.subtract).then_inc(att_d, 1)

                evacuate(0)
                evacuate(1)
                divide(0)
                dve.wait_ge(maps, 4 * l + 1)
                for tb in range(TB):
                    here = slice(tb * P, (tb + 1) * P)
                    beta = ps[4 + tb][:].rearrange("p (h c) -> p h c", h=H)
                    dve.tensor_tensor(KB[:, :, here], kT[:, :, here], beta, ALU.mult)
                    dve.tensor_tensor(vT[:, :, here], vT[:, :, here], beta, ALU.mult).then_inc(kb_s, 1)
                divide(1)
                if l == 0:
                    take_upto(u_of[("ada", 0, 4, 0)])
                out_low(0)
                if l == 0:
                    take_upto(u_of[("ada", 0, 5, 0)])
                dve.wait_ge(exps_s, 6 * l + 6)
                link(dve.tensor_tensor(XT, X, wide(before_blk[:], [P, TB * H, P], 1), ALU.mult))
                link(dve.tensor_tensor(X, X, wide(incl_blk[:], [P, TB * H, P], 1), ALU.mult))
                ahead(("gate", l, 0), 0)
                out_low(1)
                for n, (dst, decay) in enumerate(((LT, XT), (AT, X))):
                    dve.wait_ge(lat, 2 * l + n + 1)
                    for tb in range(TB):
                        heads = slice(tb * H, (tb + 1) * H)
                        ins = dve.tensor_tensor(dst[:, heads, :], ps[4 + 2 * n + tb][:].rearrange("p (h c) -> p h c", h=H),
                                                decay[:, heads, :], ALU.mult)
                    ins.then_inc(lat_s, 1)
                eye = wide(ident[:], [P, TB * H, P], 1)
                dve.wait_ge(lat_s, 2 * l + 2)
                link(dve.tensor_tensor(U, LT, wide(lev_mask[:, 6, :], [P, TB * H, P], 1), ALU.mult))
                link(dve.tensor_tensor(XT, eye, U, ALU.subtract))
                dve.wait_ge(l0_ps, l + 1)
                for tb in range(TB):
                    ins = dve.tensor_tensor(U[:, tb * H:(tb + 1) * H, :],
                                            ps[2 + tb][:].rearrange("p (h c) -> p h c", h=H),
                                            wide(lev_mask[:, 0, :], [P, H, P], 1), ALU.mult)
                link(ins)
                dve.tensor_tensor(X, eye, U, ALU.subtract).then_inc(inv0, 1)
                ahead(("gate", l, 1), 0)
                for lev in range(1, 6):
                    for tb in range(TB):
                        heads = slice(tb * H, (tb + 1) * H)
                        dve.wait_ge(u_ps, 10 * l + 2 * (lev - 1) + tb + 1)
                        if lev > 1:
                            dve.wait_ge(xu_ps, 10 * l + 2 * (lev - 2) + tb + 1)
                        dve.tensor_tensor(U[:, heads, :], ps[4 + tb][:].rearrange("p (h c) -> p h c", h=H),
                                          wide(lev_mask[:, lev, :], [P, H, P], 1), ALU.mult).then_inc(u_s, 1)
                    ahead(("gate", l, lev + 1), 0)
                    if lev == 2:
                        dve.tensor_tensor(kT, kT, ED, ALU.mult)
                        dve.tensor_copy(egl[:], EG.rearrange("p h (n c) -> p h n c", c=CHUNK)[:, :, :, CHUNK - 1])
                    if lev == 3:
                        dve.tensor_tensor(KB, KB, EG, ALU.mult)
                    if lev == 4:
                        dve.tensor_tensor(qT, qT, EG, ALU.mult).then_inc(kgb_s, 1)
                    for tb in range(TB):
                        heads = slice(tb * H, (tb + 1) * H)
                        dve.wait_ge(xu_ps, 10 * l + 2 * (lev - 1) + tb + 1)
                        if lev < 5:
                            dve.tensor_tensor(X[:, heads, :], X[:, heads, :],
                                              ps[6 + tb][:].rearrange("p (h c) -> p h c", h=H), ALU.subtract)
                        dve.tensor_tensor(XT[:, heads, :], XT[:, heads, :],
                                          ps[2 + tb][:].rearrange("p (h c) -> p h c", h=H),
                                          ALU.subtract).then_inc(xx_s, 1)

                for n in range(NCH):
                    tb, par = divmod(n, 2)
                    rows = slice(par * CHUNK, (par + 1) * CHUNK)
                    if n:
                        dve.wait_ge(ks_ps, 3 * l + n)
                        dve.tensor_tensor(resid[rows].rearrange("p h d -> p (h d)"),
                                          v_tok[rows, tb].rearrange("p h d -> p (h d)"), ps[4][rows, :],
                                          ALU.subtract).then_inc(res_s, 1)
                    if n == 0:
                        ahead(("gate", l, 7), 0)
                    if n < NCH - 1:
                        state, after = states[n % 2], states[(n + 1) % 2]
                        dve.wait_ge(su_ps, 3 * l + n + 1)
                        if n == 0:
                            dve.tensor_copy(after.rearrange("p h d -> p (h d)"), ps[6][:]).then_inc(st_s, 1)
                        else:
                            dve.wait_ge(st_s, 3 * l + n)
                            for h in range(H):
                                ins = dve.scalar_tensor_tensor(after[:, h, :], state[:, h, :], egl[:, h, n:n + 1],
                                                               ps[6][:, h * P:(h + 1) * P], ALU.mult, ALU.add)
                            ins.then_inc(st_s, 1)
                        if n == 1:
                            ahead(("wb", l, 0), 0)
                def gated(br, cc, banks, to):
                    product((("wa", "wb")[br], l, cc), 0)
                    for n in range(2):
                        got = ps[banks[n]][:].rearrange("p (a b) -> p a b", a=2)
                        gate = gate_sb[:, 8 * br + 4 * cc + 2 * n:8 * br + 4 * cc + 2 * n + 2, :]
                        ins = dve.tensor_tensor(to[:, 2 * n:2 * n + 2, :], got, gate, ALU.mult)
                    ins.then_inc(yb_s, 1)

                ahead(("wb", l, 0), 0)
                if l == 0:
                    ada_columns(2, 0, 1, NQA, NQ)
                    dve.wait_ge(ada_s, 2)
                dve.wait_ge(gate_s, 8 * (l + 1))
                dve.wait_ge(o_ps, NCH * (l + 1))
                gate_diag(2 * l + 1, l, 2, m_dg)
                gated(1, 0, (2, 3), y_sum[:, 0:4, :])
                ahead(("wb", l, 1), 0)
                dve.wait_ge(on_s, l + 1)
                gn = cols[:, COL_GN + l:COL_GN + l + 1]
                link(dve.scalar_tensor_tensor(OT, OT, gn, o_r, ALU.mult, ALU.mult))
                dve.tensor_tensor(OT, OT, zT, ALU.mult).then_inc(oaf, 1)
                ahead(("wa", l, 0), 0)
                dve.wait_ge(oa_h, l + 1)
                dve.tensor_tensor(oa_lo[:], OT, f32(oa_hi[:]), ALU.subtract).then_inc(oa_s, 1)
                gated(1, 1, (0, 1), y_sum[:, 4:8, :])
                ahead(("wa", l, 1), 0)
                gate_copy(2 * l + 1, m_gt, (2, 3))
                for cc in range(2):
                    half = slice(4 * cc, 4 * cc + 4)
                    if cc:
                        dve.wait_ge(y_sum_s, 2 * l + 1)
                    gated(0, cc, ((6, 7), (4, 5))[cc], y_tmp)
                    dve.wait_ge(yb_s, 4 * l + 3 + cc)
                    dve.tensor_tensor(y_sum[:, half, :], y_sum[:, half, :], y_tmp, ALU.add).then_inc(y_sum_s, 1)
                    ahead(("mix", l, cc, 0), 0)
                    dve.wait_ge(y_hi_s, 2 * l + cc + 1)
                    dve.tensor_tensor(hT_lo[:, half, :], y_sum[:, half, :], f32(hT_hi[:, half, :]),
                                      ALU.subtract).then_inc(y_s, 1)
                for cc in range(2):
                    cs = slice(cc * 512, (cc + 1) * 512)
                    for tb in range(TB):
                        if cc == 1 and tb == 0:
                            ahead(("mix", l, 1, 1), 0)
                            dve.wait_ge(first_ps, 2 * l + 1)
                        else:
                            product(("mix", l, cc, 1), 1 - cc)
                        link(dve.tensor_tensor(m_xt[:, 2 * cc + tb, :], ps[2 * cc + tb][:], m_gt[:, cs], ALU.mult))
                        dve.tensor_tensor(xs[:, tb, cs], xs[:, tb, cs], m_xt[:, 2 * cc + tb, :],
                                          ALU.add).then_inc(mix_s, 1)
                if l == 0:
                    ahead(("fg", 0), 0)
                dve.wait_ge(mix_s, 4 * (l + 1))

                if l == 0:
                    norm(1, f_xn)
                    modulate(1, f_tmp)
                    for i in range(2 * FC):
                        ahead(("fg", i), 2)
                        dve.wait_ge(fs_s, i + 1)
                        product(("fu", i), 2)
                        if i:
                            dve.wait_ge(fhh_s, i)
                        dve.tensor_tensor(f_h[:].rearrange("p a b -> p (a b)"), f_g[i % 2][:].rearrange("p a b -> p (a b)"),
                                          ps[1][:], ALU.mult).then_inc(fh_s, 1)
                        dve.wait_ge(fhh_s, i + 1)
                        dve.tensor_tensor(f_lo[i % 2][:], f_h[:], f32(f_hi[i % 2][:]), ALU.subtract).then_inc(fhl_s, 1)
                        if i == NQ:
                            ada_columns(3, 1, 3, 0, NQ)
                            dve.wait_ge(ada_s, 3)
                            gate_diag(2, 0, 5, f_dg[:])
                    ahead(("fd", 2 * FC - 1), 0)
                    gate_copy(2, f_gt, (2, 3))
                    for tb in range(TB):
                        if tb == 0:
                            dve.wait_ge(first_ps, 2)
                        else:
                            product(("fd", 2 * FC - 1), 0)
                        for hf in range(2):
                            cs = slice(hf * 512, (hf + 1) * 512)
                            ins = dve.tensor_tensor(f_xn[:, tb, cs], ps[4 + 2 * tb + hf][:], f_gt[:, cs], ALU.mult)
                        link(ins)
                        dve.tensor_tensor(xs[:, tb, :], xs[:, tb, :], f_xn[:, tb, :], ALU.add).then_inc(xf_s, 1)
                    ahead(("qkvz", 1, 0), 0)
                    dve.wait_ge(xf_s, TB)

            norm(3, e_xn)
            gate_diag(4, 1, 5, e_xf[:])
            modulate(3, e_tmp, False)
            by_tok = [P, TB, E]
            dve.wait_ge(logit_ps, 1)
            dve.wait_ge(upper_s, 1)
            dve.tensor_copy(e_y[0:E, 0:T], ps[2][0:E, 0:T]).then_inc(lgr_s, 1)
            dve.wait_ge(logit_ps, 2)
            dve.tensor_copy(slots[:], ps[3][:, 0:P])
            link(dve.tensor_scalar(rsm[:, 0, :], ps[3][:, 0:E], -1.0, float(E), ALU.mult, ALU.add))
            dve.wait_ge(logit_ps, 3)
            link(dve.tensor_tensor(lg[:, 0], ps[2][:, 0:TB * E].rearrange("p (t e) -> p t e", t=TB),
                                   wide(rb_row[:], by_tok, 1), ALU.add))

            def first_max(src, top, dst):
                link(dve.tensor_reduce(top, src, AX.X, ALU.max))
                link(dve.tensor_tensor(lg[:, 1], src, top.to_broadcast(by_tok), ALU.is_equal))
                link(dve.tensor_tensor(lg[:, 1], lg[:, 1], wide(rsm[:, 0, :], by_tok, 1), ALU.mult))
                link(dve.tensor_reduce(lg[:, 10, :, 0:1], lg[:, 1], AX.X, ALU.max))
                link(dve.tensor_tensor(dst, lg[:, 1], lg[:, 10, :, 0:1].to_broadcast(by_tok), ALU.is_equal))

            top1, top2 = lg[:, 5, :, 0:1], lg[:, 11, :, 0:1]
            first_max(lg[:, 0], top1, lg[:, 2])
            link(dve.scalar_tensor_tensor(lg[:, 3], lg[:, 2], NEG, lg[:, 0], ALU.mult, ALU.add))
            first_max(lg[:, 3], top2, lg[:, 4])
            dve.tensor_tensor(lg[:, 6], lg[:, 2], lg[:, 4], ALU.add).then_inc(sel_s, 1)
            dve.tensor_tensor(lg[:, 8, :, 0:1], top2, top1, ALU.subtract).then_inc(lg_s, 1)
            dve.wait_ge(lge_s, 1)
            link(dve.tensor_scalar(lg[:, 9, :, 0:1], lg[:, 8, :, 0:1], 1.0, None, ALU.add))
            link(dve.reciprocal(lg[:, 9, :, 1:2], lg[:, 9, :, 0:1]))
            link(dve.tensor_tensor(lg[:, 9, :, 2:3], lg[:, 9, :, 1:2], lg[:, 8, :, 0:1], ALU.mult))
            dve.tensor_tensor(lg[:, 1], lg[:, 2], lg[:, 9, :, 1:2].to_broadcast(by_tok), ALU.mult)
            link(dve.tensor_tensor(lg[:, 3], lg[:, 4], lg[:, 9, :, 2:3].to_broadcast(by_tok), ALU.mult))
            link(dve.tensor_tensor(wt_of[:, :, 0:E], lg[:, 1], lg[:, 3], ALU.add))
            dve.wait_ge(sel_s, 1)
            dve.wait_ge(pos_ps, 1)
            link(dve.scalar_tensor_tensor(lg[:, 1], ps[5][:, 0:TB * E].rearrange("p (t e) -> p t e", t=TB), 1.0,
                                          lg[:, 6], ALU.add, ALU.mult))
            link(dve.tensor_scalar(slot_of[:, :, 0:E], lg[:, 1], -1.0, None, ALU.add))
            def perm(item, n):
                dve.tensor_copy(cur[:, 0, :].unsqueeze(2), slot_of[:, :, bass.ds(item, 1)]).then_inc(cur_s, 1)
                dve.wait_ge(cur_s, n)
                for tb in range(TB):
                    ins = dve.tensor_scalar(e_p[:, tb, :], slots[:], cur[:, 0, tb:tb + 1], None, ALU.is_equal)
                ins.then_inc(p_s, 1)

            def weighted_perm(item, n):
                dve.tensor_copy(cur[:, 1, :].unsqueeze(2), slot_of[:, :, bass.ds(item, 1)])
                dve.tensor_copy(cur[:, 2, :].unsqueeze(2), wt_of[:, :, bass.ds(item, 1)]).then_inc(cur_s, 1)
                dve.wait_ge(cur_s, n)
                for tb in range(TB):
                    ins = dve.tensor_scalar(e_pw[:, tb, :], slots[:], cur[:, 1, tb:tb + 1], cur[:, 2, tb:tb + 1],
                                            ALU.is_equal, ALU.mult)
                ins.then_inc(pw_s, 1)

            def gathered(piece, n, bank=5):
                dve.wait_ge(ga_ps, n)
                for k in range(4):
                    ko = 4 * piece + k
                    ins = dve.tensor_scalar(e_xf[:, ko, :], ps[bank][:, k * P:(k + 1) * P], wsc[:, ko:ko + 1],
                                            adac[:, 1, 3 * KO + ko:3 * KO + ko + 1], ALU.mult, ALU.add)
                ins.then_inc(ga_s, 1)

            def gathered_low(n):
                dve.wait_ge(xgh_s, n)
                dve.tensor_tensor(xg_lo[:], e_xf[:], f32(xg_hi[:]), ALU.subtract).then_inc(xg_s, 1)

            def combined(i, k):
                tb, hf = divmod(k, 2)
                cs = slice(hf * 512, (hf + 1) * 512)
                dve.wait_ge(cb_ps, 4 * i + (k + 2))
                dve.tensor_tensor(e_acc[:, tb, cs], e_acc[:, tb, cs], ps[5][:], ALU.add).then_inc(cb_s, 1)

            for n, started in enumerate((mh_s, mhl_s, cb_s)):
                dve.memset(stat[:, 10 + n:11 + n], 0.0).then_inc(started, 1)
            dve.tensor_copy(rsm[:, 1, :], ps[5][:, 2 * E:3 * E])
            perm(0, 1)
            link(dve.tensor_scalar(rsm[:, 2, :], rsm[:, 1, :], float(P), None, ALU.is_gt))
            link(dve.memset(rsm[:, 3, :], 0.0))
            for e in range(E - 1):
                link(dve.tensor_tensor(rsm[:, 3, e + 1:e + 2], rsm[:, 3, e:e + 1], rsm[:, 2, e:e + 1], ALU.add))
            link(dve.scalar_tensor_tensor(metaf[:, 0:1], rsm[:, 3, E - 1:E], float(E), rsm[:, 2, E - 1:E],
                                          ALU.add, ALU.add))
            gathered(0, 1)
            for j in range(3):
                one = rsm[:, 4 + j, :]
                link(dve.scalar_tensor_tensor(one, rsm[:, 3, :], float(j), rsm[:, 2, :], ALU.is_equal, ALU.mult))
                link(dve.tensor_tensor(rsm[:, 7 + j, :], one, slots[:, 0:E], ALU.mult))
                link(dve.tensor_reduce(metaf[:, 1 + j:2 + j], rsm[:, 7 + j, :], AX.X, ALU.add))
            dve.tensor_copy(meta[:], metaf[:]).then_inc(route_s, 1)
            gathered(1, 2, 4)
            gathered_low(1)
            for j in range(3):
                one = rsm[:, 4 + j, :]
                link(dve.scalar_tensor_tensor(lg[:, 1], slot_of[:, :, 0:E], -float(P), wide(one, by_tok, 1),
                                              ALU.add, ALU.mult))
                link(dve.tensor_reduce(slot_of[:, :, E + j:E + j + 1], lg[:, 1], AX.X, ALU.add))
                link(dve.tensor_tensor(lg[:, 3], wt_of[:, :, 0:E], wide(one, by_tok, 1), ALU.mult))
                link(dve.tensor_reduce(wt_of[:, :, E + j:E + j + 1], lg[:, 3], AX.X, ALU.add))
            dve.wait_ge(route_s, 1)
            n_items = dve.value_load(meta[0:1, 0:1], min_val=E, max_val=E + 3)
            with dve.Fori(0, n_items) as i:
                def low(p):
                    dve.wait_ge(hi_ready, MU * i + (S0 + p + 1))
                    dve.tensor_tensor(w_lo[p % NS_MOE][:], ring[:, p % RING, :], f32(w_hi[p % NS_MOE][:]),
                                      ALU.subtract).then_inc(taken, 1)

                low(0)
                low(1)
                for p, (kind, fc, half) in enumerate(moe_units):
                    if p + 2 < MU:
                        low(p + 2)
                    if p < 4:
                        combined(i, p)
                    if p == mp[("g", 1, 0)]:
                        weighted_perm(i, 2 * i + 2)
                    if p == mp[("g", 3, 0)]:
                        dve.wait_ge(ga_ps, 2 * i + 2)
                        perm(i + 1, 2 * i + 3)
                    if kind == "u" and half == 1:
                        dve.wait_ge(ms_s, FC * i + (fc + 2))
                        dve.wait_ge(split_used, MU * i + (S0 + p + 1))
                        dve.wait_ge(mt_ps, FC * i + max(fc, 1))
                        dve.tensor_tensor(e_h[fc % 2][:], e_g[fc % 2][:], ps[2 * (fc % 2) + 1][:],
                                          ALU.mult).then_inc(mh_s, 1)
                    f = turned_after.get(p)
                    if f is not None:
                        dve.wait_ge(mhh_s, FC * i + (f + 1))
                        dve.tensor_tensor(h_lo[f % 2][:].rearrange("p a b -> p (a b)"), ps[4][:],
                                          f32(h_hi[f % 2][:]).rearrange("p a b -> p (a b)"),
                                          ALU.subtract).then_inc(mhl_s, 1)
                    if p == mp[("g", 2, 0)]:
                        dve.wait_ge(pwt_ps, i + 1)
                        dve.tensor_copy(e_pwT[:], ps[5][:, 0:T]).then_inc(pwt_s, 1)
                    if p == mp[("g", 4, 0)]:
                        gathered(0, 2 * i + 3)
                    if p == mp[("g", 4, 1)]:
                        gathered(1, 2 * i + 4)
                    if (kind, fc, half) == ("d", FC - 2, 1):
                        gathered_low(i + 2)
            dve.wait_ge(gt_s, 4)
            dve.wait_ge(cb_s, 4 * n_items + 1)
            for tb in range(TB):
                at = [0, 0]
                for hf in range(2):
                    cs = slice(hf * 512, (hf + 1) * 512)
                    dve.wait_ge(cb_ps, 4 * n_items + (2 * tb + hf + 2))
                    at[hf] = mark(dve.tensor_tensor(e_acc[:, tb, cs], e_acc[:, tb, cs], ps[2 * tb + hf][:], ALU.add))
                for hf in range(2):
                    cs = slice(hf * 512, (hf + 1) * 512)
                    dve.wait_ge(dve_c, at[hf])
                    at[hf] = mark(dve.tensor_tensor(e_acc[:, tb, cs], e_acc[:, tb, cs], e_gt[:, cs], ALU.mult))
                for hf in range(2):
                    cs = slice(hf * 512, (hf + 1) * 512)
                    dve.wait_ge(dve_c, at[hf])
                    ins = dve.tensor_tensor(xs[:, tb, cs], xs[:, tb, cs], e_acc[:, tb, cs], ALU.add)
                ins.then_inc(xf_s, 1)
            dve.wait_ge(xf_s, 2 * TB)
            dve.wait_ge(rstd_s, 5)
            link(dve.reciprocal(stat[:, 4:6], stat[:, 2:4]))
            dve.wait_ge(fin_s, 16)
            for tb in range(TB):
                dve.scalar_tensor_tensor(e_acc[:, tb, :], xs[:, tb, :], stat[:, 4 + tb:5 + tb], fw_row[:],
                                         ALU.mult, ALU.mult).then_inc(out_s, 1)


INPUTS = ["x", "c", "positions", "ada_w", "ada_b", "norm_mix_w", "norm_ffn_w", "w_in", "conv_w", "a_log",
          "dt_bias", "gdn_norm_w", "sinks", "w_a_out", "w_b_out", "w_mix_out", "ffn_w_gate", "ffn_w_up",
          "ffn_w_down", "router_w", "router_b", "moe_w_gate", "moe_w_up", "moe_w_down", "final_norm_w"]


def kernel(**inputs):
    import concourse.bacc as bacc
    from concourse.bass_utils import run_bass_kernel_spmd

    nc = bacc.Bacc("TRN2", target_bir_lowering=False, num_devices=1)
    arrays, args = {}, []
    for name in INPUTS:
        a = np.ascontiguousarray(inputs[name])
        arrays[f"in_{name}_dram"] = a
        args.append(nc.dram_tensor(f"in_{name}_dram", a.shape, mybir.dt.from_np(a.dtype),
                                   kind="ExternalInput").ap())
    shape = tuple(inputs["x"].shape)
    args.append(nc.dram_tensor("out_dram", shape, F32, kind="ExternalOutput").ap())
    build_program(nc, *args)
    result = run_bass_kernel_spmd(nc, [arrays], core_ids=[0])
    return result.results[0]["out_dram"]
```
